# Optimizing a Trainium2 kernel written in Bass

```python
import math
import jax, jax.numpy as jnp
from jax import lax
import numpy as np

D_MODEL = 1024
BATCH = 1
SEQ = 256
DEPTH = 4
DEC_BATCH = 8
DEC_SEQ = 8
PAST_LEN = 2048
PAGE_SIZE = 128

N_MIXERS = 3
LAYER_MIXER = tuple(i % N_MIXERS for i in range(DEPTH))
N_RWKV = LAYER_MIXER.count(0)
N_MLA = LAYER_MIXER.count(1)
N_GDN = LAYER_MIXER.count(2)
N_VRES = max(N_RWKV - 1, 0)
NORM_EPS = 1e-6

RW_N = 64
RW_H = D_MODEL // RW_N
RW_DECAY_LORA = 64
RW_A_LORA = 64
RW_V_LORA = 32
RW_G_LORA = 160
RW_LNX_EPS = 64e-5

MLA_H = 16
MLA_NOPE = 64
MLA_ROPE = 32
MLA_V = 64
MLA_Q_LORA = 512
MLA_KV_LORA = 256
MLA_SCALE = (MLA_NOPE + MLA_ROPE) ** -0.5
ROPE_THETA = 10000.0
Q_BLOCK = 128

GDN_QK_H = 8
GDN_V_H = 16
GDN_DK = 128
GDN_DV = 128
GDN_QK_DIM = GDN_QK_H * GDN_DK
GDN_V_DIM = GDN_V_H * GDN_DV
GDN_CONV_DIM = 2 * GDN_QK_DIM + GDN_V_DIM
GDN_IN = GDN_CONV_DIM + GDN_V_DIM + 2 * GDN_V_H
GDN_CONV = 4
GDN_CHUNK = 64

D_FF = 2816
FFN_CONV = 3

kernel_name = 'hybrid_rwkv7_mla_gdn_convffn_step'

def rmsnorm(x, w, eps=NORM_EPS):
    xf = x.astype(jnp.float32)
    y = xf * lax.rsqrt(jnp.mean(xf * xf, axis=-1, keepdims=True) + eps)
    return (y * w.astype(jnp.float32)).astype(x.dtype)

def l2norm(x, eps=1e-6):
    xf = x.astype(jnp.float32)
    return xf * lax.rsqrt(jnp.sum(xf * xf, axis=-1, keepdims=True) + eps)

def causal_conv(x, buf, w):
    K = w.shape[0]
    T = x.shape[1]
    xp = jnp.concatenate([buf.astype(x.dtype), x], axis=1)
    y = xp[:, 0:T] * w[0]
    for j in range(1, K):
        y = y + xp[:, j:j + T] * w[j]
    return y, xp[:, T:]

def rope(x, pos):
    half = x.shape[-1] // 2
    inv = ROPE_THETA ** (-jnp.arange(half, dtype=jnp.float32) / half)
    ang = pos.astype(jnp.float32)[:, None] * inv[None, :]
    ang = ang.reshape(ang.shape[:1] + (1,) * (x.ndim - 3) + (half,))
    cos, sin = jnp.cos(ang), jnp.sin(ang)
    xf = x.astype(jnp.float32)
    x1, x2 = xf[..., :half], xf[..., half:]
    return jnp.concatenate([x1 * cos - x2 * sin, x1 * sin + x2 * cos], axis=-1).astype(x.dtype)

def rwkv7_time_mix(x, shift_prev, S0, v_first, p, ri):
    B, T, D = x.shape
    f32 = jnp.float32
    x_prev = jnp.concatenate([shift_prev[:, None, :].astype(x.dtype), x[:, :-1]], axis=1)
    xm = x[None] + (x_prev - x)[None] * p['rw_mu'][ri][:, None, None, :]
    r, k, v = jnp.einsum('nbtd,nde->nbte', xm[:3], p['rw_wrkv'][ri])
    xw, xa, xg = xm[3], xm[4], xm[5]
    w = -jax.nn.softplus(-(p['rw_w0'][ri] + jnp.tanh(xw @ p['rw_w1'][ri]) @ p['rw_w2'][ri])) - 0.5
    if v_first is None:
        v_first = v
    else:
        vi = ri - 1
        v = v + (v_first - v) * jax.nn.sigmoid(p['rw_v0'][vi] + (xm[2] @ p['rw_v1'][vi]) @ p['rw_v2'][vi])
    a = jax.nn.sigmoid(p['rw_a0'][ri] + (xa @ p['rw_a1'][ri]) @ p['rw_a2'][ri])
    g = jax.nn.sigmoid(xg @ p['rw_g1'][ri]) @ p['rw_g2'][ri]
    hs = (B, T, RW_H, RW_N)
    kk = l2norm((k * p['rw_kk'][ri]).reshape(hs))
    k = k * (1 + (a - 1) * p['rw_ka'][ri])
    rh, kh, vh, ah = (t.reshape(hs).astype(f32) for t in (r, k, v, a))
    decay = jnp.exp(-jnp.exp(w.reshape(hs).astype(f32)))

    def tm(t):
        return jnp.moveaxis(t, 1, 0)

    def step(S, inp):
        r_t, w_t, k_t, v_t, a_t, b_t = inp
        sa = jnp.einsum('bhvk,bhk->bhv', S, a_t)
        S = S * w_t[:, :, None, :] + sa[..., None] * b_t[:, :, None, :] + v_t[..., None] * k_t[:, :, None, :]
        return S, jnp.einsum('bhvk,bhk->bhv', S, r_t)

    S, y = lax.scan(step, S0.astype(f32), (tm(rh), tm(decay), tm(kh), tm(vh), tm(-kk), tm(kk * ah)))
    y = tm(y)
    mu = jnp.mean(y, axis=-1, keepdims=True)
    var = jnp.mean(jnp.square(y - mu), axis=-1, keepdims=True)
    y = ((y - mu) * lax.rsqrt(var + RW_LNX_EPS)).reshape(B, T, D) * p['rw_lnx_w'][ri] + p['rw_lnx_b'][ri]
    bonus = jnp.sum(rh * kh * p['rw_rk'][ri], axis=-1, keepdims=True) * vh
    y = (y + bonus.reshape(B, T, D)).astype(x.dtype) * g
    return y @ p['rw_wo'][ri], x[:, -1], S, v_first

def mla_project(x, pos, p, mi):
    B, T, _ = x.shape
    h = x @ p['mla_w_in'][mi]
    cq = rmsnorm(h[..., :MLA_Q_LORA], p['mla_q_norm'][mi])
    c = rmsnorm(h[..., MLA_Q_LORA:MLA_Q_LORA + MLA_KV_LORA], p['mla_kv_norm'][mi])
    kr = rope(h[..., MLA_Q_LORA + MLA_KV_LORA:], pos)
    q = (cq @ p['mla_w_qb'][mi]).reshape(B, T, MLA_H, MLA_NOPE + MLA_ROPE)
    q_lat = jnp.einsum('bthn,chn->bthc', q[..., :MLA_NOPE], p['mla_w_uk'][mi])
    q_rope = rope(q[..., MLA_NOPE:], pos)
    return q_lat, q_rope, c, kr

def mla_attend_prompt(q_lat, q_rope, c, kr):
    B, T, H, C = q_lat.shape
    nb = T // Q_BLOCK

    def blk(t):
        return jnp.moveaxis(t.reshape((B, nb, Q_BLOCK) + t.shape[2:]), 1, 0)

    kpos = jnp.arange(T)

    def one_block(args):
        ql, qr, i = args
        s = (jnp.einsum('bqhc,bkc->bhqk', ql, c) + jnp.einsum('bqhr,bkr->bhqk', qr, kr)).astype(jnp.float32) * MLA_SCALE
        qpos = i * Q_BLOCK + jnp.arange(Q_BLOCK)
        s = jnp.where(kpos[None, :] <= qpos[:, None], s, -jnp.inf)
        pr = jax.nn.softmax(s, axis=-1).astype(c.dtype)
        return jnp.einsum('bhqk,bkc->bqhc', pr, c)

    o = lax.map(one_block, (blk(q_lat), blk(q_rope), jnp.arange(nb)))
    return jnp.moveaxis(o, 0, 1).reshape(B, T, H, C)

def mla_attend_sample(q_lat, q_rope, c, kr, pages_c, pages_kr, page_table):
    B, T, H, C = q_lat.shape
    c_past = pages_c[page_table].reshape(B, -1, C).astype(c.dtype)
    kr_past = pages_kr[page_table].reshape(B, -1, MLA_ROPE).astype(kr.dtype)
    P = c_past.shape[1]
    s_past = jnp.einsum('bqhc,bkc->bhqk', q_lat, c_past) + jnp.einsum('bqhr,bkr->bhqk', q_rope, kr_past)
    s_new = jnp.einsum('bqhc,bkc->bhqk', q_lat, c) + jnp.einsum('bqhr,bkr->bhqk', q_rope, kr)
    causal = jnp.tril(jnp.ones((T, T), dtype=bool))
    s_new = jnp.where(causal, s_new.astype(jnp.float32), -jnp.inf)
    s = jnp.concatenate([s_past.astype(jnp.float32), s_new], axis=-1) * MLA_SCALE
    pr = jax.nn.softmax(s, axis=-1).astype(c.dtype)
    return jnp.einsum('bhqk,bkc->bqhc', pr[..., :P], c_past) + jnp.einsum('bhqk,bkc->bqhc', pr[..., P:], c)

def mla_out(o_lat, p, mi):
    B, T = o_lat.shape[:2]
    v = jnp.einsum('bthc,chv->bthv', o_lat, p['mla_w_uv'][mi])
    return v.reshape(B, T, MLA_H * MLA_V) @ p['mla_wo'][mi]

def chunk_gated_delta(q, k, v, beta, g, S0):
    B, T, H, DK = q.shape
    DV = v.shape[-1]
    C = GDN_CHUNK if T % GDN_CHUNK == 0 else T
    n = T // C

    def cs(t):
        t = t.reshape((B, n, C) + t.shape[2:])
        return jnp.moveaxis(jnp.moveaxis(t, 1, 0), 2, 3)

    q, k, v, beta, g = (cs(t) for t in (q, k, v, beta, g))
    gc = jnp.cumsum(g, axis=-1)
    idx = jnp.arange(C)
    lower = idx[:, None] >= idx[None, :]
    strict = idx[:, None] > idx[None, :]
    L = jnp.exp(jnp.where(lower, gc[..., :, None] - gc[..., None, :], -jnp.inf))
    kb = k * beta[..., None]
    A = jnp.where(strict, jnp.einsum('...ik,...jk->...ij', kb, k) * L, 0.0)
    Tm = A + jnp.eye(C, dtype=A.dtype)
    rhs = jnp.concatenate([v * beta[..., None], kb * jnp.exp(gc)[..., None]], axis=-1)
    sol = lax.linalg.triangular_solve(Tm, rhs, left_side=True, lower=True, unit_diagonal=True)
    u, w = sol[..., :DV], sol[..., DV:]
    Aqk = jnp.einsum('...ik,...jk->...ij', q, k) * L
    qg = q * jnp.exp(gc)[..., None]
    kg = k * jnp.exp(gc[..., -1:] - gc)[..., None]
    gl = jnp.exp(gc[..., -1])

    def step(S, inp):
        u_i, w_i, aqk_i, qg_i, kg_i, gl_i = inp
        v_new = u_i - jnp.einsum('bhck,bhkv->bhcv', w_i, S)
        o = jnp.einsum('bhck,bhkv->bhcv', qg_i, S) + jnp.einsum('bhij,bhjv->bhiv', aqk_i, v_new)
        S = S * gl_i[..., None, None] + jnp.einsum('bhck,bhcv->bhkv', kg_i, v_new)
        return S, o

    S, o = lax.scan(step, S0, (u, w, Aqk, qg, kg, gl))
    o = jnp.moveaxis(jnp.moveaxis(o, 2, 3), 0, 1).reshape(B, T, H, DV)
    return o, S

def gdn_mix(x, conv_buf, S0, p, gi):
    B, T, _ = x.shape
    f32 = jnp.float32
    h = x @ p['gdn_w_in'][gi]
    o1 = GDN_CONV_DIM
    o2 = o1 + GDN_V_DIM
    o3 = o2 + GDN_V_H
    qkv, conv_new = causal_conv(h[..., :o1], conv_buf, p['gdn_conv_w'][gi])
    qkv = jax.nn.silu(qkv)
    z = h[..., o1:o2]
    beta = jax.nn.sigmoid(h[..., o2:o3].astype(f32))
    gdec = -jnp.exp(p['gdn_a_log'][gi].astype(f32)) * jax.nn.softplus(h[..., o3:].astype(f32) + p['gdn_dt_bias'][gi].astype(f32))
    rep = GDN_V_H // GDN_QK_H
    q = l2norm(qkv[..., :GDN_QK_DIM].reshape(B, T, GDN_QK_H, GDN_DK)) * (GDN_DK ** -0.5)
    k = l2norm(qkv[..., GDN_QK_DIM:2 * GDN_QK_DIM].reshape(B, T, GDN_QK_H, GDN_DK))
    q = jnp.repeat(q, rep, axis=2)
    k = jnp.repeat(k, rep, axis=2)
    v = qkv[..., 2 * GDN_QK_DIM:].reshape(B, T, GDN_V_H, GDN_DV).astype(f32)
    o, S = chunk_gated_delta(q, k, v, beta, gdec, S0.astype(f32))
    o = rmsnorm(o, p['gdn_norm_w'][gi]) * jax.nn.silu(z.reshape(B, T, GDN_V_H, GDN_DV).astype(f32))
    return o.reshape(B, T, GDN_V_DIM).astype(x.dtype) @ p['gdn_wo'][gi], conv_new, S

def conv_ffn(x, buf, p, l):
    u, buf_new = causal_conv(x @ p['ffn_w_up'][l], buf, p['ffn_conv_w'][l])
    u = u + p['ffn_conv_b'][l]
    return (jax.nn.silu(u[..., :D_FF]) * u[..., D_FF:]) @ p['ffn_w_down'][l], buf_new

def trunk(x, pos, rw_S, rw_shift, gdn_S, gdn_conv, ffn_conv, p, paged):
    new = {'rw_S': [], 'rw_shift': [], 'mla_c': [], 'mla_kr': [], 'gdn_S': [], 'gdn_conv': [], 'ffn_conv': []}
    v_first = None
    ri = 0
    mi = 0
    gi = 0
    for l in range(DEPTH):
        nw = p['norm_w'][l]
        h = rmsnorm(x, nw[0])
        kind = LAYER_MIXER[l]
        if kind == 0:
            out, sh, S, v_first = rwkv7_time_mix(h, rw_shift[ri], rw_S[ri], v_first, p, ri)
            new['rw_S'].append(S)
            new['rw_shift'].append(sh)
            ri += 1
        elif kind == 1:
            q_lat, q_rope, c, kr = mla_project(h, pos, p, mi)
            if paged is None:
                o = mla_attend_prompt(q_lat, q_rope, c, kr)
            else:
                o = mla_attend_sample(q_lat, q_rope, c, kr, paged[0][mi], paged[1][mi], paged[2])
            out = mla_out(o, p, mi)
            new['mla_c'].append(c)
            new['mla_kr'].append(kr)
            mi += 1
        else:
            out, cb, S = gdn_mix(h, gdn_conv[gi], gdn_S[gi], p, gi)
            new['gdn_S'].append(S)
            new['gdn_conv'].append(cb)
            gi += 1
        x = x + rmsnorm(out.astype(x.dtype), nw[1])
        f, fb = conv_ffn(rmsnorm(x, nw[2]), ffn_conv[l], p, l)
        new['ffn_conv'].append(fb)
        x = x + rmsnorm(f, nw[3])
    stacked = {name: jnp.stack(vals).astype(x.dtype) for name, vals in new.items()}
    return x, stacked

def setup_inputs(seed: int = 0) -> dict:
    key = jax.random.key(seed)
    keys = jax.random.split(key, 64)
    counter = iter(range(64))
    f32 = jnp.float32

    def nrm(shape, scale=1.0):
        return jax.random.normal(keys[next(counter)], shape, f32) * scale

    def unif(shape, lo, hi):
        return jax.random.uniform(keys[next(counter)], shape, f32, lo, hi)

    d = D_MODEL
    n_pages = PAST_LEN // PAGE_SIZE
    n_pool = (DEC_BATCH * n_pages * 5) // 4
    page_table = jax.random.permutation(keys[next(counter)], n_pool)[:DEC_BATCH * n_pages].reshape(DEC_BATCH, n_pages).astype(jnp.int32)
    dt = jnp.exp(unif((N_GDN, GDN_V_H), math.log(1e-3), math.log(1e-1)))
    return {
        'x_prompt': nrm((BATCH, SEQ, d)),
        'x_sample': nrm((DEC_BATCH, DEC_SEQ, d)),
        'state_rwkv_wkv': nrm((N_RWKV, DEC_BATCH, RW_H, RW_N, RW_N), 0.1),
        'state_rwkv_shift': nrm((N_RWKV, DEC_BATCH, d)),
        'cache_mla_latent': nrm((N_MLA, n_pool, PAGE_SIZE, MLA_KV_LORA)),
        'cache_mla_krope': nrm((N_MLA, n_pool, PAGE_SIZE, MLA_ROPE)),
        'state_gdn_S': nrm((N_GDN, DEC_BATCH, GDN_V_H, GDN_DK, GDN_DV), 0.1),
        'state_gdn_conv': nrm((N_GDN, DEC_BATCH, GDN_CONV - 1, GDN_CONV_DIM)),
        'state_ffn_conv': nrm((DEPTH, DEC_BATCH, FFN_CONV - 1, 2 * D_FF), 0.5),
        'page_table': page_table,
        'norm_w': 1.0 + nrm((DEPTH, 4, d), 0.05),
        'rw_mu': unif((N_RWKV, 6, d), 0.0, 1.0),
        'rw_wrkv': nrm((N_RWKV, 3, d, d), d ** -0.5),
        'rw_w0': unif((N_RWKV, d), -5.0, 0.5),
        'rw_w1': nrm((N_RWKV, d, RW_DECAY_LORA), d ** -0.5),
        'rw_w2': nrm((N_RWKV, RW_DECAY_LORA, d), 0.5 * RW_DECAY_LORA ** -0.5),
        'rw_a0': nrm((N_RWKV, d), 0.1),
        'rw_a1': nrm((N_RWKV, d, RW_A_LORA), d ** -0.5),
        'rw_a2': nrm((N_RWKV, RW_A_LORA, d), RW_A_LORA ** -0.5),
        'rw_v0': nrm((N_VRES, d), 0.1),
        'rw_v1': nrm((N_VRES, d, RW_V_LORA), d ** -0.5),
        'rw_v2': nrm((N_VRES, RW_V_LORA, d), RW_V_LORA ** -0.5),
        'rw_g1': nrm((N_RWKV, d, RW_G_LORA), d ** -0.5),
        'rw_g2': nrm((N_RWKV, RW_G_LORA, d), RW_G_LORA ** -0.5),
        'rw_kk': 0.85 + nrm((N_RWKV, d), 0.05),
        'rw_ka': 1.0 + nrm((N_RWKV, d), 0.05),
        'rw_rk': nrm((N_RWKV, RW_H, RW_N), 0.1),
        'rw_lnx_w': 1.0 + nrm((N_RWKV, d), 0.05),
        'rw_lnx_b': nrm((N_RWKV, d), 0.01),
        'rw_wo': nrm((N_RWKV, d, d), d ** -0.5),
        'mla_w_in': nrm((N_MLA, d, MLA_Q_LORA + MLA_KV_LORA + MLA_ROPE), d ** -0.5),
        'mla_q_norm': 1.0 + nrm((N_MLA, MLA_Q_LORA), 0.05),
        'mla_kv_norm': 1.0 + nrm((N_MLA, MLA_KV_LORA), 0.05),
        'mla_w_qb': nrm((N_MLA, MLA_Q_LORA, MLA_H * (MLA_NOPE + MLA_ROPE)), MLA_Q_LORA ** -0.5),
        'mla_w_uk': nrm((N_MLA, MLA_KV_LORA, MLA_H, MLA_NOPE), MLA_KV_LORA ** -0.5),
        'mla_w_uv': nrm((N_MLA, MLA_KV_LORA, MLA_H, MLA_V), MLA_KV_LORA ** -0.5),
        'mla_wo': nrm((N_MLA, MLA_H * MLA_V, d), (MLA_H * MLA_V) ** -0.5),
        'gdn_w_in': nrm((N_GDN, d, GDN_IN), d ** -0.5),
        'gdn_conv_w': nrm((N_GDN, GDN_CONV, GDN_CONV_DIM), GDN_CONV ** -0.5),
        'gdn_a_log': jnp.log(unif((N_GDN, GDN_V_H), 1.0, 16.0)),
        'gdn_dt_bias': jnp.log(jnp.expm1(dt)),
        'gdn_norm_w': 1.0 + nrm((N_GDN, GDN_DV), 0.05),
        'gdn_wo': nrm((N_GDN, GDN_V_DIM, d), GDN_V_DIM ** -0.5),
        'ffn_w_up': nrm((DEPTH, d, 2 * D_FF), d ** -0.5),
        'ffn_conv_w': nrm((DEPTH, FFN_CONV, 2 * D_FF), FFN_CONV ** -0.5),
        'ffn_conv_b': nrm((DEPTH, 2 * D_FF), 0.01),
        'ffn_w_down': nrm((DEPTH, D_FF, d), D_FF ** -0.5),
    }

def reference(x_prompt, x_sample, state_rwkv_wkv, state_rwkv_shift, cache_mla_latent, cache_mla_krope,
              state_gdn_S, state_gdn_conv, state_ffn_conv, page_table, norm_w,
              rw_mu, rw_wrkv, rw_w0, rw_w1, rw_w2, rw_a0, rw_a1, rw_a2, rw_v0, rw_v1, rw_v2,
              rw_g1, rw_g2, rw_kk, rw_ka, rw_rk, rw_lnx_w, rw_lnx_b, rw_wo,
              mla_w_in, mla_q_norm, mla_kv_norm, mla_w_qb, mla_w_uk, mla_w_uv, mla_wo,
              gdn_w_in, gdn_conv_w, gdn_a_log, gdn_dt_bias, gdn_norm_w, gdn_wo,
              ffn_w_up, ffn_conv_w, ffn_conv_b, ffn_w_down):
    p = {
        'norm_w': norm_w,
        'rw_mu': rw_mu, 'rw_wrkv': rw_wrkv, 'rw_w0': rw_w0, 'rw_w1': rw_w1, 'rw_w2': rw_w2,
        'rw_a0': rw_a0, 'rw_a1': rw_a1, 'rw_a2': rw_a2, 'rw_v0': rw_v0, 'rw_v1': rw_v1, 'rw_v2': rw_v2,
        'rw_g1': rw_g1, 'rw_g2': rw_g2, 'rw_kk': rw_kk, 'rw_ka': rw_ka, 'rw_rk': rw_rk,
        'rw_lnx_w': rw_lnx_w, 'rw_lnx_b': rw_lnx_b, 'rw_wo': rw_wo,
        'mla_w_in': mla_w_in, 'mla_q_norm': mla_q_norm, 'mla_kv_norm': mla_kv_norm, 'mla_w_qb': mla_w_qb,
        'mla_w_uk': mla_w_uk, 'mla_w_uv': mla_w_uv, 'mla_wo': mla_wo,
        'gdn_w_in': gdn_w_in, 'gdn_conv_w': gdn_conv_w, 'gdn_a_log': gdn_a_log, 'gdn_dt_bias': gdn_dt_bias,
        'gdn_norm_w': gdn_norm_w, 'gdn_wo': gdn_wo,
        'ffn_w_up': ffn_w_up, 'ffn_conv_w': ffn_conv_w, 'ffn_conv_b': ffn_conv_b, 'ffn_w_down': ffn_w_down,
    }
    B, T = x_prompt.shape[0], x_prompt.shape[1]
    dt = x_prompt.dtype
    y_prompt, sp = trunk(
        x_prompt, jnp.arange(T),
        jnp.zeros((N_RWKV, B, RW_H, RW_N, RW_N), dt),
        jnp.zeros((N_RWKV, B, D_MODEL), dt),
        jnp.zeros((N_GDN, B, GDN_V_H, GDN_DK, GDN_DV), dt),
        jnp.zeros((N_GDN, B, GDN_CONV - 1, GDN_CONV_DIM), dt),
        jnp.zeros((DEPTH, B, FFN_CONV - 1, 2 * D_FF), dt),
        p, None)
    past_len = page_table.shape[1] * cache_mla_latent.shape[2]
    pos_s = past_len + jnp.arange(x_sample.shape[1])
    y_sample, ss = trunk(
        x_sample, pos_s, state_rwkv_wkv, state_rwkv_shift, state_gdn_S, state_gdn_conv, state_ffn_conv,
        p, (cache_mla_latent, cache_mla_krope, page_table))
    return (y_prompt, y_sample,
            sp['rw_S'], sp['rw_shift'], sp['mla_c'], sp['mla_kr'], sp['gdn_S'], sp['gdn_conv'], sp['ffn_conv'],
            ss['rw_S'], ss['rw_shift'], ss['mla_c'], ss['mla_kr'], ss['gdn_S'], ss['gdn_conv'], ss['ffn_conv'])


_drawn_inputs = setup_inputs


def setup_inputs(seed=0):
    import zlib

    import numpy as np

    out = dict(_drawn_inputs(seed))
    spreads = {}
    factors = {}
    for name, (base, spread) in spreads.items():
        noise = np.random.default_rng([zlib.crc32(name.encode()), seed]).standard_normal(out[name].shape)
        drawn = base * np.exp(spread * noise) if base else spread * noise
        out[name] = __import__('jax').numpy.asarray(drawn.astype(out[name].dtype))
    for name, factor in factors.items():
        out[name] = (out[name] * factor).astype(out[name].dtype)
    return out
```

```python
from contextlib import ExitStack

import numpy as np
import concourse.bass as bass
from concourse import mybir

F32 = mybir.dt.float32
I32 = mybir.dt.int32
ALU = mybir.AluOpType
ACT = mybir.ActivationFunctionType
AX = mybir.AxisListType

P = 128
D, SEQ, DEC, STEPS = 1024, 256, 8, 8
DEPTH, DFF = 4, 2816
NT = SEQ + DEC * STEPS
MT = D // P
FT = DFF // P
BLK = MT * NT
NS = 4
SLOT = 2048
EPS = 1e-6
LNX_EPS = 64e-5
C64 = 64
PAGE, PAGES, LAT, ROPE = 128, 16, 256, 32
POOL = 160
MH, NOPE = 16, 64
SCALE = (NOPE + ROPE) ** -0.5
GH, GQK = 16, 8
NEG = -1e30


def constants():
    i = np.arange(P)
    cols = {}
    cols["ident"] = np.eye(P)
    cols["ones"] = np.ones((P, P))
    cols["onesB"] = np.kron(np.eye(2), np.ones((64, 64)))
    cols["mean64"] = cols["onesB"] / 64.0
    sw = np.zeros((P, P))
    for b in range(0, P, ROPE):
        for r in range(ROPE // 2):
            sw[b + 16 + r, b + r] = -1.0
            sw[b + r, b + 16 + r] = 1.0
    cols["swap"] = sw
    cols["spread"] = np.concatenate([np.tile(np.eye(P)[:, 32 * j:32 * j + 32], (1, 4)) for j in range(4)], 1)
    cols["group4"] = (i[:, None] // 32) == np.arange(4)[None, :]
    for lev in range(7):
        w = 2 ** lev
        same = (i[:, None] // (2 * w)) == (i[None, :] // (2 * w))
        cols[f"lev{lev}"] = same & ((i[:, None] // w) % 2 == 0) & ((i[None, :] // w) % 2 == 1)
    j, t = i[:, None], i[None, :]
    t64 = np.arange(64)[None, :]
    for name, w in (("p", 64), ("s", 8)):
        strict = (j < t) & (j // w == t // w) & (j // 64 == t // 64)
        incl = ((j % 64) <= t64) & ((j % 64) // w == t64 // w)
        cols["amask_" + name] = np.concatenate([strict, incl, strict, incl], 1)
    cols["gincl"] = j <= t
    cols["gincl_s"] = np.where(j < 64, (j <= t64) & (j // 8 == t64 // 8), 0)
    cols["causal"] = np.where(t <= j, 0.0, NEG)
    c8 = np.full((P, 120), NEG)
    c8[:, 56:64] = np.where(np.arange(8)[None, :] <= (j % 8), 0.0, NEG)
    cols["causal8"] = c8
    seg = np.ones(NT)
    seg[0:SEQ:C64] = 0
    seg[SEQ::8] = 0
    cols["seg64"] = np.tile(seg, (P, 1))
    seg = np.ones(NT)
    seg[0:SEQ:P] = 0
    seg[SEQ::8] = 0
    cols["seg128"] = np.tile(seg, (P, 1))
    pos = np.concatenate([np.arange(SEQ), np.tile(PAGE * PAGES + np.arange(8), 8)]).astype(np.float32)
    inv = (np.float32(10000.0) ** (-np.arange(16, dtype=np.float32) / np.float32(16))).astype(np.float32)
    ang = (pos[None, :] * inv[(i % 16)][:, None]).astype(np.float32)
    cols["cos"] = np.cos(ang)
    cols["sin"] = np.sin(ang)
    cols["batch8"] = (i[:, None] % 64) // 8 == np.arange(8)[None, :]
    cols["half"] = (i[:, None] // 64) == np.arange(2)[None, :]
    tables = []
    for mla in (False, True):
        at, out, off = {}, [], 0
        for k, v in cols.items():
            if (k in ("swap", "spread", "group4", "causal", "causal8", "cos", "sin")) == mla:
                v = np.asarray(v, np.float32)
                at[k] = (off, v.shape[1])
                off += v.shape[1]
                out.append(v)
        tables += [at, np.ascontiguousarray(np.concatenate(out, 1))]
    return tables


CONST_AT, CONST, MLA_CONST_AT, MLA_CONST = constants()
NCONST = CONST.shape[1]

PARAM_ROWS = [("norm_w", 128), ("rw_mu", 96), ("rw_w0", 16), ("rw_a0", 16), ("rw_kk", 16), ("rw_ka", 16),
              ("rw_rk", 16), ("rw_lnx_w", 16), ("rw_lnx_b", 16), ("rw_v0", 8), ("mla_q_norm", 4),
              ("mla_kv_norm", 2), ("gdn_norm_w", 1), ("gdn_conv_w", 128), ("ffn_conv_w", 528), ("ffn_conv_b", 176)]
PARAM_AT, _n = {}, 0
for _name, _rows in PARAM_ROWS:
    PARAM_AT[_name] = _n
    _n += _rows
NPARAM = _n



SHARED = {
    "products": "out_done half_done rkv_done lora1_done lora2_done up_done min_done q_done kn_done v_done ql_done qrs_done "
                "swapped gin_done vs_done",
    "turned": "pro_turned tail_turned shift_turned y_turned gtail_turned tok_turned ukt_done ctok_done",
    "sums": "kk_summed bonus_summed ymean yvar mla_summed l2_summed go_summed sq_summed",
    "rwkv_inverse_products": "amm pmm imm",
    "rwkv_chunk_products": "tv_done rhs_done sa_done y_done ymm pstate_turned",
    "rwkv_sample_products": "sin_turned z_done smm sout_turned",
    "gdn_inverse_products": "gpmm gimm kq_done gc_done bb_done",
    "gdn_turned": "vt_done kt_done",
    "gdn_chunk_products": "ks_done vn_done go_done g_mu",
    "gdn_sample_products": "gz_done gks_done gvn_done gso_done gs_mm",
    "prompt_attention_products": "ps_done pt_done po_done",
    "sample_attention_products": "turn_done score_done sp_done s_values ol_done",
    "norm_rstd": "rstd_ln rstd",
    "squares": "sq kk_sq y_sq mla_sq l2_sq go_sq",
    "rows_copied": "tail_rows shift_rows gtail_rows y_rows",
    "products_copied": "rkv lora_copied lora2_out q_raw min_raw kn ukt ctok vtok ql qrs z_out vs",
    "head_rstd": "kk_ln kk_rstd y_ln y_rstd l2_ln l2_rstd gn_ln gn_rstd mla_ln mla_rstd",
    "decays": "decay_prev decay decay_inv",
    "rwkv_chunk_copies": "tv p rhs sa mg pstate",
    "rwkv_sample_copies": "z_zero m0 z sout",
    "gdn_gates": "exp_alog g_e1 g_sp g_e",
    "gdn_copies": "tok gc bb vt kt g_decay gp",
    "gdn_chunk_copies": "vn go gz gs_vn gs_o",
    "prompt_attention_copies": "p_exp pt po",
    "sample_attention_copies": "c_turned_a s_exp sp_turned ol_turned",
    "prologue": "pro_copied eps params2",
    "rwkv_mix": "shift_kept dx_run dx",
    "lora": "mid_sum mid_recip lora_mid",
    "log_decays": "sig_sum log_decay log_sum log_prev",
    "rwkv_values": "v_diff v_part v_mixed",
    "rwkv_keys": "kkr k_gain k_mod rk kk b a_scaled prepared",
    "group_norm": "bonus_v y_centered y1 y2 y3 y_gated",
    "rwkv_chunk_sums": "am inv y state m_sum m_new",
    "ffn_taps": "tap1 tap2 conv",
    "ffn_gate": "gate_d gate_gu gate_r hff",
    "residual": "x post",
    "gdn_taps": "gtap1 gtap2 gtap3 gconv",
    "gdn_silu": "g_1e g_sig g_silu z_add z_rec z_1e",
    "gdn_rows": "g_abs g_r g_t g_rows g_nbe",
    "gdn_inverse": "g_diff kq_read g_aq g_am qg ginv",
    "gdn_states": "g_rhs g_state gs_rhs gs_scaled gs_new",
    "gdn_scaled": "g_n1 g_gated qk_normed",
    "mla_scaled": "cq c rot rot_c rot_s",
    "prompt_softmax": "p_masked p_max p_maxr p_rec p_norm",
    "sample_softmax": "c_turned s_gmax s_masked s_maxr s_max sp_turned_d s_sum s_rec s_out",
}
SEMAPHORE_OF = {step: name for name, steps in SHARED.items() for step in steps.split()}


class Signals:

    def __init__(self, nc, ctx, values):
        self.nc, self.ctx, self.values = nc, ctx, values
        self.sems, self.count, self.found = {}, {}, {}

    def sem(self, name):
        if name not in self.sems:
            self.sems[name] = self.ctx.enter_context(self.nc.semaphore(name))
        return self.sems[name]

    def to(self, name, step, n=1):
        sem = SEMAPHORE_OF.get(name, name)
        self.count[sem] = self.count.get(sem, 0) + n
        self.found[name, step] = self.count[sem]
        return self.sem(sem), n

    def at(self, name, step):
        return self.sem(SEMAPHORE_OF.get(name, name)), (self.values[name, step] if self.values else 1)


def build(nc, io, values, layers=DEPTH):
    ctx = ExitStack()
    with ctx:
        sig = Signals(nc, ctx, values)
        to, at = sig.to, sig.at

        def sb(name, shape, dt=F32):
            return ctx.enter_context(nc.sbuf_tensor(name, shape, dt))

        psum = [ctx.enter_context(nc.psum_tensor(f"bank{b}", [P, 512], F32)) for b in range(8)]

        C = sb("consts", [P, NCONST])
        PT = sb("params", [P, NPARAM])
        PX = sb("params2", [P, 64])
        AH = sb("head_rows", [16, 4])
        EB = sb("eps_cols", [P, 8])
        ffn_state = sb("ffn_state", [P, 16 * 44])
        gdn_state = sb("gdn_state", [P, 24 * 32])
        shift_state = sb("shift_state", [P, P])
        X = sb("x", [P, MT, NT])
        H = sb("h", [P, MT, NT])
        W = sb("weights", [P, NS, SLOT])
        SQ = sb("squares", [P, 4, NT])
        RS = sb("rstd", [P, 2, NT])
        PS = sb("post_scaled", [P, 2, NT])
        SMALL = sb("small", [P, 1936])
        PG = sb("pages", [1, DEC * PAGES], I32)
        AR = (nc.sbuf_usable_end - nc.sbuf_base) // 4 - 32
        A = sb("arena", [P, AR])

        def const(name, a=0, b=None):
            off, n = CONST_AT[name]
            return C[:, off + a:off + (n if b is None else b)]

        def par(name, i):
            return PT[:, PARAM_AT[name] + i:PARAM_AT[name] + i + 1]

        def block(i):
            return A[:, i * BLK:(i + 1) * BLK].rearrange("p (m t) -> p m t", m=MT)

        def flat(i):
            return A[:, i * BLK:(i + 1) * BLK]

        def arena(off, *dims):
            n = int(np.prod(dims))
            assert off + n <= AR, (off, n, AR)
            ap = A[:, off:off + n]
            if len(dims) == 2:
                ap = ap.rearrange("p (a b) -> p a b", a=dims[0])
            if len(dims) == 3:
                ap = ap.rearrange("p (a b c) -> p a b c", a=dims[0], b=dims[1])
            if len(dims) == 4:
                ap = ap.rearrange("p (a b c d) -> p a b c d", a=dims[0], b=dims[1], c=dims[2])
            return ap

        ident, ones, onesB, mean64 = const("ident"), const("ones"), const("onesB"), const("mean64")

        NW0, NA0, NV0, OMKA = 0, 16, 32, 40
        rw_of = {0: 0, 3: 1}

        plan = []

        def slot_view(i, k, n):
            return W[:, i % NS, 0:k * n].rearrange("p (k n) -> p k n", k=k)

        def add_weight(key, w, k, n0, n1, k0=0):
            i = len(plan)
            src = w[k0 * P:(k0 + k) * P, n0:n1].rearrange("(k p) n -> p k n", p=P)
            plan.append((key, [(slot_view(i, k, n1 - n0), src)]))

        def add_rows(key, parts):
            i = len(plan)
            loads, off = [], 0
            for src in parts:
                r, n = src.shape
                loads.append((W[0:r, i % NS, off:off + n], src))
                off += n
            plan.append((key, loads))

        for l in range(layers):
            if l in rw_of:
                ri = rw_of[l]
                for i in range(3):
                    for c in range(4):
                        add_weight(("rkv", l, i, c), io["rw_wrkv"][ri, i], 8, c * 256, c * 256 + 256)
                if ri:
                    add_weight(("v1", l), io["rw_v1"][0], 8, 0, 32)
                add_weight(("w1", l), io["rw_w1"][ri], 8, 0, 64)
                add_weight(("a1", l), io["rw_a1"][ri], 8, 0, 64)
                add_weight(("g1", l), io["rw_g1"][ri], 8, 0, 160)
                add_rows(("w2", l), [io["rw_w2"][ri]])
                add_rows(("a2", l), [io["rw_a2"][ri]])
                if ri:
                    add_rows(("v2", l), [io["rw_v2"][0]])
                add_rows(("g2", l), [io["rw_g2"][ri, 0:P], io["rw_g2"][ri, P:160]])
                for c in range(4):
                    add_weight(("wo", l, c), io["rw_wo"][ri], 8, c * 256, c * 256 + 256)
            elif l == 1:
                for c in range(3):
                    add_weight(("min", c), io["mla_w_in"][0], 8, c * 256, c * 256 + 256)
                src = io["mla_w_in"][0][:, 768:800].rearrange("(k p) n -> p k n", p=P)
                plan.append((("min", 3), [(slot_view(len(plan), 8, P)[:, :, 32 * j:32 * j + 32], src) for j in range(4)]))
                for c in range(4):
                    dst, loads = slot_view(len(plan), 4, 384), []
                    for k in range(4):
                        src = io["mla_w_qb"][0][k * P:(k + 1) * P, c * 384:c * 384 + 384].rearrange("p (h n) -> p h n", h=4)
                        loads.append((dst[:, k, 0:256].rearrange("p (h n) -> p h n", h=4), src[:, :, 0:NOPE]))
                        loads.append((dst[:, k, 256:384].rearrange("p (h n) -> p h n", h=4), src[:, :, NOPE:NOPE + ROPE]))
                    plan.append((("qb", c), loads))
                add_weight(("uk",), io["mla_w_uk"][0].rearrange("c h n -> c (h n)"), 2, 0, 1024)
                add_weight(("uv",), io["mla_w_uv"][0].rearrange("c h n -> c (h n)"), 2, 0, 1024)
                for c in range(4):
                    add_weight(("wo", l, c), io["mla_wo"][0], 8, c * 256, c * 256 + 256)
            else:
                for c in range(24):
                    add_weight(("gin", c), io["gdn_w_in"][0], 8, c * 256, c * 256 + 256)
                add_weight(("gin", 24), io["gdn_w_in"][0], 8, 6144, 6176)
                for c in range(8):
                    add_weight(("gwo", c), io["gdn_wo"][0], 16, c * P, c * P + P)
            for c in range(11):
                for half in range(2):
                    add_weight(("up", l, half, c), io["ffn_w_up"][l], 8, half * DFF + c * 256, half * DFF + c * 256 + 256)
            for m in range(MT):
                for kk in range(2):
                    add_weight(("down", l, m, kk), io["ffn_w_down"][l], 11, m * P, m * P + P, k0=kk * 11)
        where = {key: i for i, (key, _) in enumerate(plan)}
        weight_used = {}

        banks = {"n": 0, "free": [[] for _ in range(8)], "of": {}}

        def bank(pe, key, *read_by, which=None):
            b = banks["n"] % 8 if which is None else which
            banks["n"] += which is None
            for step in banks["free"][b]:
                pe.wait_ge(*at(*step))
            banks["free"][b] = read_by
            banks["of"][key] = b
            return psum[b][:, :]

        def of(key):
            return psum[banks["of"][key]][:, :]

        def mm(pe, out, lhsT, rhs, first, last):
            return pe.matmul(out, lhsT, rhs, start=first, stop=last, skip_group_check=True)

        def sample(ap3):
            return ap3.rearrange("p (b s) -> p b s", b=DEC)

        def x_step(q, m):
            return ("x", (-1, 4)) if q == 0 else ("x", (q - 1, m))

        def pe_norm(pe, q):
            ps = bank(pe, ("norm", q), ("rstd_ln", q))
            for m in range(MT):
                pe.wait_ge(*at("sq", (q, m)))
                mm(pe, ps[:, 0:NT], ones, SQ[:, m % 4, :], m == 0, m == 7).then_inc(*to("sq_summed", (q, m)))

        squares = {"last": None}

        def act_square(act, m, src, made, summed, count=MT):
            last = summed(m - 4) if m >= 4 else squares["last"]
            if last is not None:
                act.wait_ge(*at(*last))
            act.activation(SQ[:, m % 4, :], src, ACT.Square).then_inc(*to(*made))
            if m == count - 1:
                squares["last"] = summed(m)

        def act_rstd(act, q, scale):
            act.wait_ge(*at("sq_summed", (q, 7)))
            act.activation(RS[:, 0, :], of(("norm", q))[:, 0:NT], ACT.Ln, bias=EB[:, 0:1], scale=scale)\
               .then_inc(*to("rstd_ln", q))
            act.wait_ge(*at("rstd_ln", q))
            act.activation(RS[:, 1, :], RS[:, 0, :], ACT.Exp, scale=-0.5).then_inc(*to("rstd", q))

        def act_pre_norm(act, q):
            for m in range(MT):
                act.wait_ge(*at(*x_step(q, m)))
                act_square(act, m, X[:, m, :], ("sq", (q, m)), lambda n: ("sq_summed", (q, n)))
            if q == 0:
                act.wait_ge(*at("eps", 0))
            act_rstd(act, q, 1.0 / D)

        def dve_pre_norm(dve, q):
            dve.wait_ge(*at("rstd", q))
            for m in range(MT):
                dve.scalar_tensor_tensor(out=H[:, m, :], in0=X[:, m, :], scalar=par("norm_w", q * 8 + m),
                                         in1=RS[:, 1, :], op0=ALU.mult, op1=ALU.mult).then_inc(*to("h", (q, m)))

        def act_outputs(act, q, stored=None):
            for m in range(MT):
                act.wait_ge(*at("out_done", (q, m)))
                act_square(act, m, of(("out", q, m))[:, 0:NT], ("sq", (q, m)), lambda n: ("sq_summed", (q, n)))
                act.activation(H[:, m, :], of(("out", q, m))[:, 0:NT], ACT.Copy).then_inc(*to("out", (q, m)))
            if stored:
                act.wait_ge(*at(*stored))
            act_rstd(act, q, 1.0 / D)

        def dve_post_norm(dve, q):
            dve.wait_ge(*at("rstd", q))
            for m in range(MT):
                dve.wait_ge(*at("out", (q, m)))
                dve.scalar_tensor_tensor(out=PS[:, m % 2, :], in0=H[:, m, :], scalar=par("norm_w", q * 8 + m),
                                         in1=RS[:, 1, :], op0=ALU.mult, op1=ALU.mult).then_inc(*to("post", (q, m)))
                dve.wait_ge(*at("post", (q, m)))
                dve.tensor_tensor(X[:, m, :], X[:, m, :], PS[:, m % 2, :], ALU.add).then_inc(*to("x", (q, m)))

        def weight(pe, key):
            i = where[key]
            pe.wait_ge(*at(f"slot{i % NS}", key))
            return i % NS

        def pe_out(pe, q, keys, k, ready, rhs):
            for c, slot_keys in enumerate(keys):
                two = len(slot_keys) == 1 and k == 8
                for j in range(2 if two else 1):
                    m = 2 * c + j if two else c
                    ps = bank(pe, ("out", q, m), ("out", (q, m)))
                    n, total = 0, k * len(slot_keys)
                    for key in slot_keys:
                        w = W[:, weight(pe, key), :]
                        for kt in range(k):
                            if c == 0 and j == 0:
                                for step in ready(n):
                                    pe.wait_ge(*at(*step))
                            width = 256 if two else P
                            ins = mm(pe, ps[:, 0:NT], w[:, kt * width + j * P:kt * width + j * P + P], rhs(n),
                                     n == 0, n == total - 1)
                            n += 1
                            if kt == k - 1 and key != slot_keys[-1]:
                                ins.then_inc(*to("half_done", (q, m)))
                                weight_used[key] = ("half_done", (q, m))
                    ins.then_inc(*to("out_done", (q, m)))
                    weight_used[slot_keys[-1]] = ("out_done", (q, m))

        HFF = arena(0, FT, NT)
        CV0 = FT * NT
        CONV = arena(CV0, 2, 2, 336)
        CT = arena(CV0 + 4 * 336, 2, 336)
        EGATE = arena(CV0 + 6 * 336, 2, 336)
        GD = arena(CV0 + 8 * 336, 3, 336)
        XP = arena(CV0 + 11 * 336, 4, 344)
        TAIL = arena(CV0 + 11 * 336 + 4 * 344, 792)
        TOUT = arena(CV0 + 11 * 336 + 4 * 344 + 792, 7, P)
        tail_p = TAIL[:, 0:88].rearrange("p (j m) -> p j m", j=2)
        tail_s = TAIL[:, 88:792].rearrange("p (b j m) -> p b j m", b=DEC, j=2)

        def ffn_tiles():
            for c in range(11):
                for half in range(2):
                    for j in range(2):
                        yield c, half, j, 2 * c + j

        def pe_ffn(pe, l):
            q = 4 * l + 2
            pe_norm(pe, q)
            for c, half, j, m in ffn_tiles():
                key = ("up", l, half, c)
                w = W[:, weight(pe, key), :]
                ps = bank(pe, ("up", l, half, m), ("xp", (l, half, m)))
                for k in range(MT):
                    if (c, half, j) == (0, 0, 0):
                        pe.wait_ge(*at("h", (q, k)))
                    ins = mm(pe, ps[:, 0:NT], w[:, k * 256 + j * P:k * 256 + j * P + P], H[:, k, :], k == 0, k == 7)
                ins.then_inc(*to("up_done", (l, half, m)))
                weight_used[key] = ("up_done", (l, half, m))
            for g, (first, n) in enumerate([(0, 4), (4, 3)]):
                ps = bank(pe, ("tail", l, g), ("tail_rows", (l, g)))
                for i in range(first, first + n):
                    a, b = (0, 88) if i == 0 else (88 + (i - 1) * P, min(88 + i * P, 792))
                    if i == 0:
                        pe.wait_ge(*at("tail", (l, 1, FT - 1)))
                    ins = pe.transpose(ps[0:b - a, (i - first) * P:(i - first + 1) * P], TAIL[:, a:b], ident)
                ins.then_inc(*to("tail_turned", (l, g)))
            pe_out(pe, q + 1, [[("down", l, m, 0), ("down", l, m, 1)] for m in range(MT)], 11,
                   lambda n: [("hff", (l, n))], lambda n: HFF[:, n, :])
            pe_norm(pe, q + 1)

        def act_ffn(act, l):
            q = 4 * l + 2
            if l:
                act.wait_ge(*at("tail", (l - 1, 1, FT - 1)))
            else:
                act.wait_ge(*at("ffn_state_t", 0))
            act.dma_start(ffn_state[:, :], io["ffn_state_t"][:, l * 704:(l + 1) * 704])\
               .then_inc(*to("ffn_state_in", l, 16))
            act_pre_norm(act, q)
            for n, (c, half, j, m) in enumerate(ffn_tiles()):
                for step in conv_users(l, n):
                    act.wait_ge(*at(*step))
                act.wait_ge(*at("up_done", (l, half, m)))
                ps = of(("up", l, half, m))
                act.activation(XP[:, n % 4, 2:258], ps[:, 0:SEQ], ACT.Copy)
                act.activation(sample_window(n % 4)[:, :, 2:10], sample(ps[:, SEQ:NT]), ACT.Copy)\
                   .then_inc(*to("xp", (l, half, m)))
                if half == 1:
                    act.wait_ge(*at("conv", (l, 0, m)))
                    if m >= 2:
                        act.wait_ge(*at("gate_d", (l, m - 2)))
                    act.activation(EGATE[:, m % 2, :], CONV[:, 0, m % 2, :], ACT.Exp, scale=-1.0).then_inc(*to("gate_e", (l, m)))
            for g, n in ((0, 4), (1, 3)):
                act.wait_ge(*at("tail_turned", (l, g)))
                act.activation(TOUT[:, 4 * g:4 * g + n, :], of(("tail", l, g))[:, 0:n * P], ACT.Copy)\
                   .then_inc(*to("tail_rows", (l, g)))
            act.wait_ge(*at("tail_rows", (l, 1)))
            rows = io["p_ffn_conv"][l, 0].rearrange("j (m p) -> (j m) p", p=P)
            act.dma_start(rows, TOUT[0:88, 0, :]).then_inc(*to("tail_stored", l, 16))
            rows = io["s_ffn_conv"][l].rearrange("b j (m p) -> (b j m) p", p=P)
            for i in range(6):
                r = min(P, 704 - i * P)
                act.dma_start(rows[i * P:i * P + r, :], TOUT[0:r, 1 + i, :]).then_inc(*to("tail_stored", l, 16))
            act_outputs(act, q + 1, ("tail_stored", l))

        def sample_window(s):
            return XP[:, s, 258:338].rearrange("p (b w) -> p b w", b=DEC)

        order = list(ffn_tiles())

        def conv_users(l, n):
            if n >= 4:
                c, half, j, m = order[n - 4]
                return [("conv", (l, half, m)), ("tail", (l, half, m))]
            return []

        def pool_ffn(pool, l):
            pool.wait_ge(*at("rstd", 4 * l + 2))
            pool.memset(XP[:, :, 0:2], 0.0)
            for n, (c, half, j, m) in enumerate(order):
                for step in conv_users(l, n):
                    pool.wait_ge(*at(*step))
                m2 = half * FT + m
                st = ffn_state[:, :].rearrange("p (b j m) -> p b j m", b=DEC, j=2)[:, :, :, m2]
                if n == 0:
                    pool.wait_ge(*at("ffn_state_in", l))
                pool.tensor_copy(sample_window(n % 4)[:, :, 0:2], st).then_inc(*to("xp_state", (l, half, m)))
                pool.wait_ge(*at("xp", (l, half, m)))
                pool.tensor_copy(tail_p[:, :, m2], XP[:, n % 4, 256:258])
                pool.tensor_copy(tail_s[:, :, :, m2], sample_window(n % 4)[:, :, 8:10]).then_inc(*to("tail", (l, half, m)))

        def dve_ffn(dve, l):
            q = 4 * l + 2
            dve_pre_norm(dve, q)

            def gate(m):
                g, u = CONV[:, 0, m % 2, :], CONV[:, 1, m % 2, :]
                dve.wait_ge(*at("gate_e", (l, m)))
                if m:
                    dve.wait_ge(*at("hff", (l, m - 1)))
                dve.tensor_scalar(GD[:, 0, :], EGATE[:, m % 2, :], 1.0, None, ALU.add).then_inc(*to("gate_d", (l, m)))
                dve.wait_ge(*at("conv", (l, 1, m)))
                dve.tensor_tensor(GD[:, 2, :], g, u, ALU.mult).then_inc(*to("gate_gu", (l, m)))
                dve.wait_ge(*at("gate_d", (l, m)))
                dve.reciprocal(GD[:, 1, :], GD[:, 0, :]).then_inc(*to("gate_r", (l, m)))
                dve.wait_ge(*at("gate_r", (l, m)))
                dve.tensor_tensor(HFF[:, m, 0:SEQ], GD[:, 2, 0:SEQ], GD[:, 1, 0:SEQ], ALU.mult)
                win = [GD[:, i, 256:336].rearrange("p (b w) -> p b w", b=DEC)[:, :, 2:10] for i in (2, 1)]
                dve.tensor_tensor(sample(HFF[:, m, SEQ:NT]), win[0], win[1], ALU.mult).then_inc(*to("hff", (l, m)))

            for n, (c, half, j, m) in enumerate(order):
                w = lambda tap: par("ffn_conv_w", (l * 3 + tap) * 44 + half * FT + m)
                dve.wait_ge(*at("xp", (l, half, m)))
                dve.wait_ge(*at("xp_state", (l, half, m)))
                if half == 0 and m >= 2:
                    dve.wait_ge(*at("gate_e", (l, m - 2)))
                dve.tensor_scalar(CT[:, 0, :], XP[:, n % 4, 2:338], w(2), par("ffn_conv_b", l * 44 + half * FT + m),
                                  ALU.mult, ALU.add).then_inc(*to("tap2", (l, half, m)))
                dve.wait_ge(*at("tap2", (l, half, m)))
                if n:
                    dve.wait_ge(*at("conv", (l, order[n - 1][1], order[n - 1][3])))
                dve.scalar_tensor_tensor(out=CT[:, 1, :], in0=XP[:, n % 4, 1:337], scalar=w(1), in1=CT[:, 0, :],
                                         op0=ALU.mult, op1=ALU.add).then_inc(*to("tap1", (l, half, m)))
                dve.wait_ge(*at("tap1", (l, half, m)))
                dve.scalar_tensor_tensor(out=CONV[:, half, m % 2, :], in0=XP[:, n % 4, 0:336], scalar=w(0),
                                         in1=CT[:, 1, :], op0=ALU.mult, op1=ALU.add).then_inc(*to("conv", (l, half, m)))
                if half == 1 and j == 1:
                    gate(m - 1)
                    gate(m)
            dve_post_norm(dve, q + 1)

        stage_x = arena(0, 20, P)
        stage_state = arena(20 * P, 29, P)
        stage_par = arena(49 * P, 10, P)
        n_state = 22 + 6 + 1
        turns = [("x", i) for i in range(20)] + [("par", i) for i in range(10)] + [("state", i) for i in range(n_state)]
        groups = [turns[i:i + 4] for i in range(0, 20, 4)] + [turns[i:min(i + 4, 30)] for i in range(20, 30, 4)] + \
                 [turns[i:i + 4] for i in range(30, len(turns), 4)]

        def param_segments():
            row = 0
            for name, n in PARAM_ROWS:
                done = 0
                while done < n:
                    r = min(n - done, P - row % P)
                    yield name, done, r, row // P, row % P
                    done += r
                    row += r

        def stored_rows(name):
            ap = io[name]
            names = " ".join("abcd"[:len(ap.shape)])
            flat_ap = ap.rearrange(f"{names} -> ({names})")
            return flat_ap.rearrange("(r p) -> r p", p=P)

        def sp_prologue(sp):
            sp.dma_start(stage_x[:, 0:16, :], io["x_prompt"].rearrange("o t (m p) -> (o t m) p", p=P)
                         .rearrange("(i r) p -> r i p", r=P)).then_inc(*to("x_in", 0, 16))
            sp.dma_start(stage_x[:, 16:20, :], io["x_sample"].rearrange("o t (m p) -> (o t m) p", p=P)
                         .rearrange("(i r) p -> r i p", r=P)).then_inc(*to("x_in", 0, 16))

        def act_loads(act):
            act.dma_start(C[:, :], io["const"]).then_inc(*to("const_in", 0, 16))
            for name, first, r, tile, p0 in param_segments():
                act.dma_start(stage_par[p0:p0 + r, tile, :], stored_rows(name)[first:first + r, :])\
                   .then_inc(*to("param_in", 0, 16))
            act.dma_start(stage_state[:, 28, :], stored_rows("state_rwkv_shift")).then_inc(*to("states_in", 0, 16))
            act.dma_start(stage_state[:, 22:28, :], stored_rows("state_gdn_conv").rearrange("(i r) p -> r i p", r=P))\
               .then_inc(*to("states_in", 0, 16))
            act.dma_start(stage_state[:, 0:22, :], stored_rows("state_ffn_conv").rearrange("(i r) p -> r i p", r=P))\
               .then_inc(*to("states_in", 0, 16))
            act.dma_start(PG[:, :], io["page_table"].rearrange("(o b) n -> o (b n)", o=1)).then_inc(*to("pages_in", 0, 16))
            act.dma_start(AH[:, 0:1], io["gdn_a_log"].rearrange("o h -> h o")).then_inc(*to("heads_in", 0, 16))
            act.dma_start(AH[:, 1:2], io["gdn_dt_bias"].rearrange("o h -> h o")).then_inc(*to("heads_in", 0, 16))

        def stage_tile(kind, i):
            return {"x": stage_x, "par": stage_par, "state": stage_state}[kind][:, i, :]

        def pe_prologue(pe):
            pe.wait_ge(*at("const_in", 0))
            pe.wait_ge(*at("x_in", 0))
            for g, group in enumerate(groups):
                if group[0] == ("par", 0):
                    pe.wait_ge(*at("param_in", 0))
                if group[0] == ("state", 0):
                    pe.wait_ge(*at("states_in", 0))
                ps = bank(pe, ("pro", g), prologue_step(g))
                for n, (kind, i) in enumerate(group):
                    r = NPARAM - 9 * P if (kind, i) == ("par", 9) else P
                    ins = pe.transpose(ps[:, n * P:n * P + r], stage_tile(kind, i)[0:r, :], ident[0:r, 0:r])
                ins.then_inc(*to("pro_turned", g))

        def prologue_step(g):
            return ("x", (-1, g)) if g < 5 else ("pro_copied", g)

        turned_state = arena(59 * P, 22 * P)
        state_dst = [turned_state[:, i * P:(i + 1) * P] for i in range(22)] + \
                    [gdn_state[:, i * P:(i + 1) * P] for i in range(6)] + [shift_state[:, :]]

        def dve_prologue(dve):
            dve.memset(EB[:, 0:1], EPS)
            dve.memset(EB[:, 1:2], LNX_EPS).then_inc(*to("eps", 0))
            for g, group in enumerate(groups):
                dve.wait_ge(*at("pro_turned", g))
                ps = of(("pro", g))
                if g < 5:
                    dve.tensor_copy(X[:, :, g * 64:(g + 1) * 64],
                                    ps[:, :].rearrange("p (t m) -> p m t", m=MT)).then_inc(*to("x", (-1, g)))
                elif group[0][0] == "par":
                    a = group[0][1] * P
                    b = min(a + 512, NPARAM)
                    dve.tensor_copy(PT[:, a:b], ps[:, 0:b - a]).then_inc(*to("pro_copied", g))
                else:
                    for n, (_, i) in enumerate(group):
                        ins = dve.tensor_copy(state_dst[i], ps[:, n * P:(n + 1) * P])
                    ins.then_inc(*to("pro_copied", g))
                if group[-1] == ("par", 9):
                    dve.wait_ge(*at("pro_copied", g))
                    for dst, name in ((NW0, "rw_w0"), (NA0, "rw_a0"), (NV0, "rw_v0")):
                        n = 8 if name == "rw_v0" else 16
                        o = PARAM_AT[name]
                        dve.tensor_scalar(PX[:, dst:dst + n], PT[:, o:o + n], -1.0, None, ALU.mult)
                    o = PARAM_AT["rw_ka"]
                    dve.tensor_scalar(PX[:, OMKA:OMKA + 16], PT[:, o:o + 16], -1.0, 1.0, ALU.mult, ALU.add)\
                       .then_inc(*to("params2", 0))

        def act_keep_states(act):
            act.wait_ge(*at("pro_copied", len(groups) - 1))
            act.dma_start(io["ffn_state_t"], turned_state).then_inc(*to("ffn_state_t", 0, 16))
            act.wait_ge(*at("ffn_state_t", 0))

        Y = arena(0, 3, D)

        def pe_final(pe):
            q = 4 * layers - 1
            for g in range(6):
                t, half = divmod(g, 2)
                n = P if t < 2 else 64
                ps = bank(pe, ("y", g), ("y_rows", g))
                for i in range(4):
                    m = half * 4 + i
                    if t == 0:
                        pe.wait_ge(*at("x", (q, m)))
                    ins = pe.transpose(ps[0:n, i * P:(i + 1) * P], X[:, m, t * P:t * P + n], ident)
                ins.then_inc(*to("y_turned", g))

        def act_final(act):
            for g in range(6):
                t, half = divmod(g, 2)
                n = P if t < 2 else 64
                act.wait_ge(*at("y_turned", g))
                act.activation(Y[0:n, t, half * 512:(half + 1) * 512], of(("y", g))[0:n, :], ACT.Copy)\
                   .then_inc(*to("y_rows", g))
                if half:
                    act.wait_ge(*at("y_rows", g))
                    dst = io["y_prompt"][0, t * P:(t + 1) * P, :] if t < 2 else io["y_sample"].rearrange("b s d -> (b s) d")
                    act.dma_start(dst, Y[0:n, t, :]).then_inc(*to("y_stored", 0, 16))
            act.wait_ge(*at("y_stored", 0))

        BA, BB, BK, BV, BR, BG, BBON, B7, B8, B9, B10 = range(11)
        GE = SMALL[:, 0:96].rearrange("p (m c) -> p m c", m=MT)
        MID = SMALL[:, 96:96 + 5 * NT].rearrange("p (a t) -> p a t", a=5)
        mids = {"w": MID[0:64, 0, :], "a": MID[0:64, 1, :], "v": MID[0:32, 2, :]}
        SHO = SMALL[:, 1696:1768]
        SHR = SMALL[0:72, 1808:1936]
        U = 4608
        u0 = 7 * BLK

        def unit(u):
            o = u0 + u * U
            return dict(ea=arena(o, 4, P), am=arena(o + 512, 4, 384), tv=arena(o + 2048, 4, 384),
                        p=arena(o + 3584, 4, P), off=arena(o + 4096, 4, P),
                        inv=H[:, :, :].rearrange("p m t -> p (m t)")[:, u * 1024:(u + 1) * 1024]
                        .rearrange("p (a b) -> p a b", a=4))

        UNIT = [unit(0), unit(1)]
        ERING = arena(u0 + 2 * U, 3, 3, P)
        halves = PS[:, :, :].rearrange("p a t -> p (a t)"), SQ[:, :, :].rearrange("p a t -> p (a t)")
        MST = halves[0][:, 0:256].rearrange("p (u n) -> p u n", u=2)
        RHS = halves[0][:, 256:512].rearrange("p (u n) -> p u n", u=2)
        SAB = halves[1][:, 0:256].rearrange("p (u n) -> p u n", u=2)
        MG = halves[1][:, 256:512].rearrange("p (u n) -> p u n", u=2)

        def heads(ap3):
            return ap3[0:64, :, 0:64], ap3[64:128, :, 64:128]

        def rw_expect(l):
            return rw_of[l], 4 * l

        projections = [("r", B10), ("k", BK), ("v", BV)]

        def pe_rwkv(pe, l):
            ri, q = rw_expect(l)
            pe_norm(pe, q)
            ps = bank(pe, ("shift", l), ("shift_rows", l))
            pe.wait_ge(*at("shift_kept", l))
            pe.transpose(ps[0:72, 0:P], SHO, ident).then_inc(*to("shift_turned", l))
            XM = [block(B8), block(B9)]
            for i, (name, _) in enumerate(projections):
                for c in range(4):
                    key = ("rkv", l, i, c)
                    w = W[:, weight(pe, key), :]
                    for j in range(2):
                        m = 2 * c + j
                        ps = bank(pe, ("rkv", l, i, m), ("rkv", (l, i, m)))
                        for k in range(MT):
                            if c == 0 and j == 0:
                                pe.wait_ge(*at("mixed", (l, i, k)))
                            ins = mm(pe, ps[:, 0:NT], w[:, k * 256 + j * P:k * 256 + j * P + P], XM[i % 2][:, k, :],
                                     k == 0, k == 7)
                        ins.then_inc(*to("rkv_done", (l, i, m)))
                    weight_used[key] = ("rkv_done", (l, i, m))
                if i == 2 and ri:
                    w = W[:, weight(pe, ("v1", l)), :]
                    ps = bank(pe, ("lora1", l, "v", 0), ("lora_copied", (l, "v")))
                    for k in range(MT):
                        ins = mm(pe, ps[0:32, 0:NT], w[:, k * 32:k * 32 + 32], XM[0][:, k, :], k == 0, k == 7)
                    ins.then_inc(*to("lora1_done", (l, "v")))
                    weight_used[("v1", l)] = ("lora1_done", (l, "v"))
            for i, (name, width) in enumerate((("w", 64), ("a", 64), ("g", 160))):
                w = W[:, weight(pe, (name + "1", l)), :]
                for part, n in enumerate((min(width, P), width - P)[:2 if width > P else 1]):
                    ps = bank(pe, ("lora1", l, name, part), ("lora_copied", (l, name)))
                    for k in range(MT):
                        if part == 0:
                            pe.wait_ge(*at("mixed", (l, 3 + i, k)))
                        ins = mm(pe, ps[0:n, 0:NT], w[:, k * width + part * P:k * width + part * P + n],
                                 XM[(3 + i) % 2][:, k, :], k == 0, k == 7)
                ins.then_inc(*to("lora1_done", (l, name)))
                weight_used[(name + "1", l)] = ("lora1_done", (l, name))
            for name in ("w", "a", "v", "g") if ri else ("w", "a", "g"):
                w = W[:, weight(pe, (name + "2", l)), :]
                pe.wait_ge(*at("lora_mid" if name in "wg" else "lora_copied", (l, name)))
                for m in range(MT):
                    ps = bank(pe, ("lora2", l, name, m), ("lora2_out", (l, name, m)))
                    if name == "g":
                        mm(pe, ps[:, 0:NT], w[:, m * P:m * P + P], MID[:, 3, :], True, False)
                        ins = mm(pe, ps[:, 0:NT], w[0:32, D + m * P:D + m * P + P], MID[0:32, 4, :], False, True)
                    else:
                        n = 32 if name == "v" else 64
                        ins = mm(pe, ps[:, 0:NT], w[0:n, m * P:m * P + P], mids[name], True, True)
                    ins.then_inc(*to("lora2_done", (l, name, m)))
                weight_used[(name + "2", l)] = ("lora2_done", (l, name, m))
            for m in range(MT):
                ps = bank(pe, ("kkss", l, m), ("kk_ln", (l, m)))
                pe.wait_ge(*at("kk_sq", (l, m)))
                mm(pe, ps[:, 0:NT], onesB, SQ[:, m % 4, :], True, True).then_inc(*to("kk_summed", (l, m)))
            for m in range(MT):
                ps = bank(pe, ("bonus", l, m), ("bonus_v", (l, m)))
                pe.wait_ge(*at("rk", (l, m)))
                mm(pe, ps[:, 0:NT], onesB, block(B8)[:, m, :], True, True).then_inc(*to("bonus_summed", (l, m)))
            pe_rwkv_chunks(pe, l)
            for m in range(MT):
                ps = bank(pe, ("ymean", l, m), ("y_centered", (l, m)))
                pe.wait_ge(*at("y", (l, "s", m)))
                mm(pe, ps[:, 0:NT], mean64, block(BR)[:, m, :], True, True).then_inc(*to("ymean", (l, m)))
            for m in range(MT):
                ps = bank(pe, ("yvar", l, m), ("y_ln", (l, m)))
                pe.wait_ge(*at("y_sq", (l, m)))
                mm(pe, ps[:, 0:NT], mean64, SQ[:, m % 4, :], True, True).then_inc(*to("yvar", (l, m)))
            pe_out(pe, q + 1, [[("wo", l, c)] for c in range(4)], 8, lambda n: [("y_gated", (l, n))],
                   lambda n: block(BA)[:, n, :])
            pe_norm(pe, q + 1)

        def act_rwkv(act, l):
            ri, q = rw_expect(l)
            act_pre_norm(act, q)
            if l == 0:
                act_keep_states(act)
            act.wait_ge(*at("shift_turned", l))
            act.activation(SHR, of(("shift", l))[0:72, 0:P], ACT.Copy).then_inc(*to("shift_rows", l))
            act.wait_ge(*at("shift_rows", l))
            act.dma_start(io["p_rwkv_shift"][ri].rearrange("o (m p) -> (o m) p", p=P), SHR[0:8, :])\
               .then_inc(*to("shift_stored", l, 16))
            act.dma_start(io["s_rwkv_shift"][ri].rearrange("b (m p) -> (b m) p", p=P), SHR[8:72, :])\
               .then_inc(*to("shift_stored", l, 16))
            for i, (name, dst) in enumerate(projections):
                for m in range(MT):
                    act.wait_ge(*at("rkv_done", (l, i, m)))
                    act.activation(block(dst)[:, m, :], of(("rkv", l, i, m))[:, 0:NT], ACT.Copy)\
                       .then_inc(*to("rkv", (l, i, m)))
            if ri == 0:
                act.wait_ge(*at("rkv", (l, 2, 7)))
                act.dma_start(io["v_first"], flat(BV)).then_inc(*to("v_first_stored", 0, 16))
            else:
                act.wait_ge(*at("v_first_stored", 0))
                act.dma_start(flat(BA), io["v_first"]).then_inc(*to("v_first_in", 0, 16))
                act.wait_ge(*at("lora1_done", (l, "v")))
                act.activation(mids["v"], of(("lora1", l, "v", 0))[0:32, 0:NT], ACT.Copy)\
                   .then_inc(*to("lora_copied", (l, "v")))
            for name, scale in (("w", -2.0), ("a", None), ("g", -1.0)):
                act.wait_ge(*at("lora1_done", (l, name)))
                if name == "a":
                    ins = act.activation(mids["a"], of(("lora1", l, "a", 0))[0:64, 0:NT], ACT.Copy)
                elif name == "w":
                    ins = act.activation(mids["w"], of(("lora1", l, "w", 0))[0:64, 0:NT], ACT.Exp, scale=scale)
                else:
                    act.activation(MID[:, 3, :], of(("lora1", l, "g", 0))[:, 0:NT], ACT.Exp, scale=scale)
                    ins = act.activation(MID[0:32, 4, :], of(("lora1", l, "g", 1))[0:32, 0:NT], ACT.Exp, scale=scale)
                ins.then_inc(*to("lora_copied", (l, name)))
            if ri == 0:
                act.wait_ge(*at("params2", 0))
            for name in ("w", "a", "v", "g") if ri else ("w", "a", "g"):
                for m in range(MT):
                    act.wait_ge(*at("lora2_done", (l, name, m)))
                    src = of(("lora2", l, name, m))[:, 0:NT]
                    if name == "g":
                        ins = act.activation(block(BG)[:, m, :], src, ACT.Copy)
                    else:
                        dst, bias = {"w": (BR, NW0 + ri * 8), "a": (BB, NA0 + ri * 8), "v": (BBON, NV0)}[name]
                        ins = act.activation(block(dst)[:, m, :], src, ACT.Exp, scale=-1.0,
                                             bias=PX[:, bias + m:bias + m + 1])
                    ins.then_inc(*to("lora2_out", (l, name, m)))
            for m in range(MT):
                act.wait_ge(*at("kkr", (l, m)))
                act_square(act, m, block(BA)[:, m, :], ("kk_sq", (l, m)), lambda n: ("kk_summed", (l, n)))
                if m >= 2:
                    kk_rstd(act, l, m - 2)
            kk_rstd(act, l, 6)
            kk_rstd(act, l, 7)
            act.wait_ge(*at("log_prev", l))
            act.activation(flat(BR), flat(BR), ACT.Exp).then_inc(*to("decay_prev", l))
            act.activation(flat(B7), flat(B9), ACT.Exp).then_inc(*to("decay", l))
            act.wait_ge(*at("decay", l))
            act.activation(flat(B9), flat(B9), ACT.Exp, scale=-1.0).then_inc(*to("decay_inv", l))
            act_rwkv_chunks(act, l)
            for m in range(MT):
                act.wait_ge(*at("y_centered", (l, m)))
                act_square(act, m, block(BR)[:, m, :], ("y_sq", (l, m)), lambda n: ("yvar", (l, n)))
                if m >= 2:
                    y_rstd(act, l, m - 2)
            y_rstd(act, l, 6)
            y_rstd(act, l, 7)
            act_outputs(act, q + 1, ("shift_stored", l))

        def kk_rstd(act, l, m):
            act.wait_ge(*at("kk_summed", (l, m)))
            if m == 0 and rw_of[l]:
                act.wait_ge(*at("v_mixed", l))
            act.activation(block(BBON)[:, m, :], of(("kkss", l, m))[:, 0:NT], ACT.Ln, bias=EB[:, 0:1])\
               .then_inc(*to("kk_ln", (l, m)))
            act.wait_ge(*at("kk_ln", (l, m)))
            act.activation(block(BBON)[:, m, :], block(BBON)[:, m, :], ACT.Exp, scale=-0.5)\
               .then_inc(*to("kk_rstd", (l, m)))

        def y_rstd(act, l, m):
            act.wait_ge(*at("yvar", (l, m)))
            act.activation(block(B7)[:, m, :], of(("yvar", l, m))[:, 0:NT], ACT.Ln, bias=EB[:, 1:2])\
               .then_inc(*to("y_ln", (l, m)))
            act.wait_ge(*at("y_ln", (l, m)))
            act.activation(block(B7)[:, m, :], block(B7)[:, m, :], ACT.Exp, scale=-0.5)\
               .then_inc(*to("y_rstd", (l, m)))

        def dve_rwkv(dve, l):
            ri, q = rw_expect(l)
            dve_pre_norm(dve, q)
            dve.wait_ge(*at("h", (q, 7)))
            sho = SHO.rearrange("p (b m) -> p m b", m=MT)
            dve.tensor_copy(sho[:, :, 0:1], H[:, :, 255:256])
            dve.tensor_copy(sho[:, :, 1:9], H[:, :, SEQ + 7::8]).then_inc(*to("shift_kept", l))
            dx = block(B7)
            dve.tensor_tensor(dx[:, :, 1:NT], H[:, :, 0:NT - 1], H[:, :, 1:NT], ALU.subtract).then_inc(*to("dx_run", l))
            dve.wait_ge(*at("dx_run", l))
            dve.tensor_scalar(dx[:, :, 0:1], H[:, :, 0:1], -1.0, None, ALU.mult)
            st = shift_state[:, ri * 64:(ri + 1) * 64].rearrange("p (b m) -> p m b", m=MT)
            if l == 0:
                dve.wait_ge(*at("pro_copied", len(groups) - 1))
            dve.tensor_tensor(dx[:, :, SEQ::8], st, H[:, :, SEQ::8], ALU.subtract).then_inc(*to("dx", l))
            dve.wait_ge(*at("dx", l))
            for i in range(6):
                if i in (2, 3, 4):
                    dve.wait_ge(*at("rkv_done", (l, i - 2, 7)))
                if i == 4 and ri:
                    dve.wait_ge(*at("lora1_done", (l, "v")))
                if i == 5:
                    dve.wait_ge(*at("lora1_done", (l, "w")))
                for k in range(MT):
                    dve.scalar_tensor_tensor(out=block(B8 + i % 2)[:, k, :], in0=dx[:, k, :],
                                             scalar=par("rw_mu", (ri * 6 + i) * 8 + k), in1=H[:, k, :],
                                             op0=ALU.mult, op1=ALU.add).then_inc(*to("mixed", (l, i, k)))
            for name, views in (("w", [mids["w"]]), ("g", [MID[:, 3, :], MID[0:32, 4, :]])):
                dve.wait_ge(*at("lora_copied", (l, name)))
                for v in views:
                    dve.tensor_scalar(v, v, 1.0, None, ALU.add).then_inc(*to("mid_sum", (l, name)))
                dve.wait_ge(*at("mid_sum", (l, name)))
                for v in views:
                    ins = dve.reciprocal(v, v)
                if name == "w":
                    ins.then_inc(*to("mid_recip", l))
                    dve.wait_ge(*at("mid_recip", l))
                    ins = dve.tensor_scalar(mids["w"], mids["w"], 2.0, -1.0, ALU.mult, ALU.add)
                ins.then_inc(*to("lora_mid", (l, name)))

            def sigmoid(b, name, step):
                dve.wait_ge(*at("lora2_out", (l, name, 7)))
                dve.tensor_scalar(flat(b), flat(b), 1.0, None, ALU.add).then_inc(*to("sig_sum", (l, name)))
                dve.wait_ge(*at("sig_sum", (l, name)))
                dve.reciprocal(flat(b), flat(b)).then_inc(*to(step, l))
                dve.wait_ge(*at(step, l))

            sigmoid(BR, "w", "w_sig")
            dve.tensor_scalar(flat(BR), flat(BR), -float(np.exp(-0.5)), None, ALU.mult).then_inc(*to("log_decay", l))
            dve.wait_ge(*at("log_decay", l))
            dve.wait_ge(*at("lora1_done", (l, "g")))
            for m in range(MT):
                ins = dve.tensor_tensor_scan(block(B9)[:, m, :], const("seg64"), block(BR)[:, m, :], 0.0, ALU.mult, ALU.add)
            ins.then_inc(*to("log_sum", l))
            dve.wait_ge(*at("log_sum", l))
            dve.tensor_tensor(flat(BR), flat(B9), flat(BR), ALU.subtract).then_inc(*to("log_prev", l))
            sigmoid(BB, "a", "a_sig")
            if ri:
                sigmoid(BBON, "v", "v_sig")
                dve.wait_ge(*at("v_first_in", 0))
                dve.tensor_tensor(flat(BA), flat(BA), flat(BV), ALU.subtract).then_inc(*to("v_diff", l))
                dve.wait_ge(*at("v_diff", l))
                dve.tensor_tensor(flat(BA), flat(BA), flat(BBON), ALU.mult).then_inc(*to("v_part", l))
                dve.wait_ge(*at("v_part", l))
                dve.tensor_tensor(flat(BV), flat(BV), flat(BA), ALU.add).then_inc(*to("v_mixed", l))
                dve.wait_ge(*at("v_mixed", l))
            for m in range(MT):
                dve.tensor_scalar(block(BA)[:, m, :], block(BK)[:, m, :], par("rw_kk", ri * 8 + m), None, ALU.mult)\
                   .then_inc(*to("kkr", (l, m)))
            for m in range(MT):
                ins = dve.tensor_scalar(block(B8)[:, m, :], block(BB)[:, m, :], par("rw_ka", ri * 8 + m),
                                        PX[:, OMKA + ri * 8 + m:OMKA + ri * 8 + m + 1], ALU.mult, ALU.add)
            ins.then_inc(*to("k_gain", l))
            dve.wait_ge(*at("k_gain", l))
            dve.tensor_tensor(flat(BK), flat(BK), flat(B8), ALU.mult).then_inc(*to("k_mod", l))
            dve.wait_ge(*at("k_mod", l))
            for m in range(MT):
                dve.scalar_tensor_tensor(out=block(B8)[:, m, :], in0=block(B10)[:, m, :],
                                         scalar=par("rw_rk", ri * 8 + m), in1=block(BK)[:, m, :],
                                         op0=ALU.mult, op1=ALU.mult).then_inc(*to("rk", (l, m)))
            dve.wait_ge(*at("kk_rstd", (l, 7)))
            dve.tensor_tensor(flat(BA), flat(BA), flat(BBON), ALU.mult).then_inc(*to("kk", l))
            dve.wait_ge(*at("kk", l))
            dve.tensor_tensor(flat(BB), flat(BA), flat(BB), ALU.mult).then_inc(*to("b", l))
            dve.wait_ge(*at("b", l))
            dve.wait_ge(*at("decay_prev", l))
            dve.scalar_tensor_tensor(out=flat(BA), in0=flat(BA), scalar=-1.0, in1=flat(BR), op0=ALU.mult,
                                     op1=ALU.mult)
            dve.wait_ge(*at("decay", l))
            dve.tensor_copy(GE[:, :, 0:4], block(B7)[:, :, 63:SEQ:64])
            dve.tensor_copy(GE[:, :, 4:12], block(B7)[:, :, SEQ + 7::8]).then_inc(*to("a_scaled", l))
            dve.wait_ge(*at("a_scaled", l))
            dve.tensor_tensor(flat(BR), flat(B10), flat(B7), ALU.mult)
            dve.wait_ge(*at("decay_inv", l))
            dve.tensor_tensor(flat(BB), flat(BB), flat(B9), ALU.mult)
            dve.tensor_tensor(flat(BK), flat(BK), flat(B9), ALU.mult).then_inc(*to("prepared", l))
            for m in range(MT):
                dve.wait_ge(*at("bonus_summed", (l, m)))
                dve.tensor_tensor(block(BBON)[:, m, :], of(("bonus", l, m))[:, 0:NT], block(BV)[:, m, :], ALU.mult)\
                   .then_inc(*to("bonus_v", (l, m)))
            dve_rwkv_chunks(dve, l)
            for m in range(MT):
                dve.wait_ge(*at("ymean", (l, m)))
                dve.tensor_tensor(block(BR)[:, m, :], block(BR)[:, m, :], of(("ymean", l, m))[:, 0:NT], ALU.subtract)\
                   .then_inc(*to("y_centered", (l, m)))
            dve.wait_ge(*at("sout_stored", (l, 7)))
            for m in range(MT):
                dve.wait_ge(*at("y_rstd", (l, m)))
                t = block(B8)[:, m, :]
                dve.tensor_tensor(t, block(BR)[:, m, :], block(B7)[:, m, :], ALU.mult).then_inc(*to("y1", (l, m)))
                dve.wait_ge(*at("y1", (l, m)))
                dve.tensor_scalar(t, t, par("rw_lnx_w", ri * 8 + m), par("rw_lnx_b", ri * 8 + m), ALU.mult, ALU.add)\
                   .then_inc(*to("y2", (l, m)))
                dve.wait_ge(*at("y2", (l, m)))
                dve.tensor_tensor(t, t, block(BBON)[:, m, :], ALU.add).then_inc(*to("y3", (l, m)))
                dve.wait_ge(*at("y3", (l, m)))
                dve.tensor_tensor(block(BA)[:, m, :], t, block(BG)[:, m, :], ALU.mult).then_inc(*to("y_gated", (l, m)))
            dve_post_norm(dve, q + 1)

        rounds = [[("p", 2 * r), ("p", 2 * r + 1)] for r in range(4)] + [[("s", 0)], [("s", 1)]]

        def batches():
            n = 0
            for r, members in enumerate(rounds):
                for u, (kind, i) in enumerate(members):
                    yield n, r, u, kind, i
                    n += 1

        in_round = [[b for b in batches() if b[1] == r] for r in range(6)]

        def columns(kind, i, el):
            return (i, el * 64) if kind == "p" else (4 * i + el, SEQ)

        def levels(kind):
            return range(6 if kind == "p" else 3)

        def last_of(l, r, u):
            if r == 0:
                return None
            if r <= 4:
                return ("ymm", (l, "p", 2 * (r - 1) + u, 3))
            return ("smm", (l, 4 * (r - 5) + 3, 1))

        SIN = arena(u0 + U, DEC, P)
        M0 = arena(u0 + U + 1024, DEC, P)
        SAM = arena(u0 + U + 2048, DEC, P)
        VM = arena(u0 + U + 3072, DEC, P)
        PST = halves[1][:, 512:768].rearrange("p (u n) -> p u n", u=2)
        ring_at = [(n, el) for n, _, _, _, _ in batches() for el in range(4)]

        def pool_rwkv_chunks(pool, l):
            ri = rw_of[l]
            pool.wait_ge(*at("prepared", l))
            pool.wait_ge(*at("bonus_summed", (l, 7)))
            half = const("half")
            for r, members in enumerate(in_round):
                for n, _, u, kind, i in members:
                    if last_of(l, r, u):
                        pool.wait_ge(*at(*last_of(l, r, u)))
                    src = block(BA)[:, i, 0:SEQ].rearrange("p (c t) -> p c t", c=4) if kind == "p" else \
                        block(BA)[:, 4 * i:4 * i + 4, SEQ:NT]
                    pool.tensor_tensor(UNIT[u]["ea"].rearrange("p c (h t) -> p c h t", h=2),
                                       src.unsqueeze(2).broadcast_to([P, 4, 2, 64]),
                                       half.unsqueeze(1).unsqueeze(3).broadcast_to([P, 4, 2, 64]), ALU.mult)\
                        .then_inc(*to("ea", (l, n)))
                    for el in range(4):
                        g = 4 * n + el
                        if g >= 3:
                            pool.wait_ge(*at("amm", (l,) + ring_at[g - 3]))
                        tile, t0 = columns(kind, i, el)
                        src = A[:, BB * BLK:(BV + 1) * BLK].rearrange("p (b n) -> p b n", b=3)[
                            :, :, tile * NT + t0:tile * NT + t0 + 64]
                        pool.tensor_tensor(ERING[:, g % 3, :, :].rearrange("p c (h t) -> p c h t", h=2),
                                           src.unsqueeze(2).broadcast_to([P, 3, 2, 64]),
                                           half.unsqueeze(1).unsqueeze(3).broadcast_to([P, 3, 2, 64]), ALU.mult)\
                            .then_inc(*to("spread", (l, n, el)))
                kind = members[0][3]
                for lev in levels(kind):
                    for n, _, u, _, _ in members:
                        pool.wait_ge(*at("am", (l, n, 3)))
                        if lev:
                            pool.wait_ge(*at("pmm", (l, n, lev - 1)))
                            if lev == 1:
                                pool.wait_ge(*at("inv", (l, n, 0)))
                        pool.tensor_tensor(UNIT[u]["off"], UNIT[u]["am"][:, :, 0:P],
                                           const(f"lev{lev}").unsqueeze(1).broadcast_to([P, 4, P]), ALU.mult)\
                            .then_inc(*to("off", (l, n, lev)))
                if kind == "s":
                    if r == 4:
                        pool.wait_ge(*at("ymm", (l, "p", 7, 3)))
                        pool.memset(SIN, 0.0).then_inc(*to("sin_zero", l))
                        pool.wait_ge(*at("sin_zero", l))
                    for el in range(4):
                        j = 4 * members[0][4] + el
                        if j:
                            pool.wait_ge(*at("sout_stored", (l, j - 1)))
                        src = io["state_rwkv_wkv"][ri]
                        for side in range(2):
                            pool.dma_start(SIN[64 * side:64 * side + 64, :, 64 * side:64 * side + 64],
                                           src[:, 2 * j + side].rearrange("b v k -> v b k")).then_inc(*to("sin", (l, j), 16))
                        if j:
                            pool.wait_ge(*at("smm", (l, j - 1, 1)))
                        tv = UNIT[0]["tv"][:, el, 0:P]
                        pool.wait_ge(*at("tv", (l, members[0][0], el)))
                        mask = const("batch8")
                        pool.tensor_tensor(VM, tv.unsqueeze(1).broadcast_to([P, DEC, P]),
                                           mask.unsqueeze(2).broadcast_to([P, DEC, P]), ALU.mult).then_inc(*to("vm", (l, j)))
                        pool.wait_ge(*at("sa", (l, "s", j)))
                        pool.tensor_tensor(SAM, SAB[:, 0, :].unsqueeze(1).broadcast_to([P, DEC, P]),
                                           mask.unsqueeze(2).broadcast_to([P, DEC, P]), ALU.mult).then_inc(*to("sam", (l, j)))
                        pool.wait_ge(*at("sout", (l, j, 1)))
                        for side in range(2):
                            pool.dma_start(io["s_rwkv_wkv"][ri][:, 2 * j + side].rearrange("b v k -> v b k"),
                                           SIN[64 * side:64 * side + 64, :, 64 * side:64 * side + 64])\
                                .then_inc(*to("sout_stored", (l, j), 16))
            pool.wait_ge(*at("sout_stored", (l, 7)))

        def pe_rwkv_chunks(pe, l):
            pe.wait_ge(*at("prepared", l))
            for r, members in enumerate(in_round):
                kind = members[0][3]
                for n, _, u, _, i in members:
                    un = UNIT[u]
                    for el in range(4):
                        tile, t0 = columns(kind, i, el)
                        b, k, v = [ERING[:, (4 * n + el) % 3, x, :] for x in range(3)]
                        rt = block(BR)[:, tile, t0:t0 + 64]
                        pe.wait_ge(*at("spread", (l, n, el)))
                        ps = bank(pe, ("tv", l, n, el), ("tv", (l, n, el)))
                        for x, m in enumerate((v, b, k)):
                            ins = pe.transpose(ps[:, x * P:(x + 1) * P], m, ident)
                        ins.then_inc(*to("tv_done", (l, n, el)))
                        ps = bank(pe, ("am", l, n, el), ("am", (l, n, el)))
                        for x, m in enumerate((b, k)):
                            mm(pe, ps[:, x * 192:x * 192 + P], m, un["ea"][:, el, :], True, True)
                            ins = mm(pe, ps[:, x * 192 + P:x * 192 + 192], m, rt, True, True)
                        ins.then_inc(*to("amm", (l, n, el)))
                for lev in levels(kind):
                    for n, _, u, _, _ in members:
                        un = UNIT[u]
                        pe.wait_ge(*at("off", (l, n, lev)))
                        if lev:
                            pe.wait_ge(*at("inv", (l, n, lev - 1)))
                        ps = bank(pe, ("p", l, n, lev), ("p", (l, n, lev)) if lev else ("inv", (l, n, 0)))
                        for el in range(4):
                            ins = mm(pe, ps[:, el * P:(el + 1) * P], un["off"][:, el, :],
                                     un["inv"][:, el, 0:P] if lev else ident, True, True)
                        ins.then_inc(*to("pmm", (l, n, lev)))
                    if lev:
                        for n, _, u, _, _ in members:
                            un = UNIT[u]
                            pe.wait_ge(*at("p", (l, n, lev)))
                            for g in range(2):
                                ps = bank(pe, ("imm", l, n, lev, g), ("inv", (l, n, lev)))
                                for el in (2 * g, 2 * g + 1):
                                    o = (el % 2) * 256
                                    mm(pe, ps[:, o:o + P], un["inv"][:, el, P:256], un["p"][:, el, :], True, True)
                                    ins = mm(pe, ps[:, o + P:o + 256], un["p"][:, el, :], un["inv"][:, el, P:256], True, True)
                                ins.then_inc(*to("imm", (l, n, lev, g)))
                if kind == "p":
                    for c in range(4):
                        for n, _, u, _, j in members:
                            un = UNIT[u]
                            ps = bank(pe, ("rhs", l, "p", j, c), ("rhs", (l, "p", j, c)))
                            if c:
                                pe.wait_ge(*at("state", (l, j, c - 1)))
                                mm(pe, ps[:, 0:P], un["ea"][:, c, :], MST[:, u, :], True, False)
                            else:
                                pe.wait_ge(*at("inv", (l, n, levels(kind)[-1])))
                                pe.wait_ge(*at("tv", (l, n, 3)))
                            mm(pe, ps[:, 0:P], un["am"][:, c, 192:320], un["tv"][:, c, 0:P], not c, True)\
                                .then_inc(*to("rhs_done", (l, "p", j, c)))
                        for n, _, u, _, j in members:
                            pe.wait_ge(*at("rhs", (l, "p", j, c)))
                            ps = bank(pe, ("sa", l, "p", j, c), ("sa", (l, "p", j, c)))
                            mm(pe, ps[:, 0:P], UNIT[u]["inv"][:, c, P:256], RHS[:, u, :], True, True)\
                                .then_inc(*to("sa_done", (l, "p", j, c)))
                        for n, _, u, _, j in members:
                            un = UNIT[u]
                            pe.wait_ge(*at("sa", (l, "p", j, c)))
                            ps = bank(pe, ("ym", l, "p", j, c), ("y", (l, "p", j, c)))
                            if c:
                                mm(pe, ps[:, 0:64], MST[:, u, :], block(BR)[:, j, c * 64:c * 64 + 64], True, False)
                            mm(pe, ps[:, 0:64], SAB[:, u, :], un["am"][:, c, P:192], not c, False)
                            mm(pe, ps[:, 0:64], un["tv"][:, c, 0:P], un["am"][:, c, 320:384], False, True)\
                                .then_inc(*to("y_done", (l, "p", j, c)))
                            ps = bank(pe, ("mu", l, "p", j, c), ("mg", (l, j, c)))
                            mm(pe, ps[:, 0:P], un["tv"][:, c, P:256], SAB[:, u, :], True, False)
                            mm(pe, ps[:, 0:P], un["tv"][:, c, 256:384], un["tv"][:, c, 0:P], False, True)\
                                .then_inc(*to("ymm", (l, "p", j, c)))
                    for n, _, u, _, j in members:
                        pe.wait_ge(*at("state", (l, j, 3)))
                        ps = bank(pe, ("pst", l, j), ("pstate", (l, j)))
                        pe.transpose(ps[:, 0:P], MST[:, u, :], ident).then_inc(*to("pstate_turned", (l, j)))
                else:
                    n, un = members[0][0], UNIT[0]
                    for el in range(4):
                        j = 4 * members[0][4] + el
                        pe.wait_ge(*at("sin", (l, j)))
                        for g in range(2):
                            ps = bank(pe, ("sin", l, j, g), ("m0", (l, j, g)))
                            for b in range(4):
                                ins = pe.transpose(ps[:, b * P:(b + 1) * P], SIN[:, 4 * g + b, :], ident)
                            ins.then_inc(*to("sin_turned", (l, j, g)))
                        ps = bank(pe, ("z", l, j), ("z", (l, j)))
                        pe.wait_ge(*at("m0", (l, j, 1)))
                        ar = A[:, 0:5 * BLK].rearrange("p (b n) -> p b n", b=5)
                        for b in range(DEC):
                            c0 = j * NT + SEQ + 8 * b
                            ins = mm(pe, ps[:, 16 * b:16 * b + 16], M0[:, b, :], ar[:, 0:5:4, c0:c0 + 8], True, True)
                        ins.then_inc(*to("z_done", (l, j)))
                        pe.wait_ge(*at("z", (l, j)))
                        if el == 0:
                            pe.wait_ge(*at("inv", (l, n, levels(kind)[-1])))
                            pe.wait_ge(*at("tv", (l, n, 3)))
                        ps = bank(pe, ("rhs", l, "s", j), ("rhs", (l, "s", j)))
                        mm(pe, ps[:, 0:P], MG[:, 0, :], ident, True, False)
                        mm(pe, ps[:, 0:P], un["am"][:, el, 192:320], un["tv"][:, el, 0:P], False, True)\
                            .then_inc(*to("rhs_done", (l, "s", j)))
                        ps = bank(pe, ("sa", l, "s", j), ("sa", (l, "s", j)))
                        pe.wait_ge(*at("rhs", (l, "s", j)))
                        mm(pe, ps[:, 0:P], un["inv"][:, el, P:256], RHS[:, 0, :], True, True)\
                            .then_inc(*to("sa_done", (l, "s", j)))
                        ps = bank(pe, ("ym", l, "s", j), ("y", (l, "s", j)))
                        mm(pe, ps[:, 0:64], ident, MG[:, 1, 0:64], True, False)
                        mm(pe, ps[:, 0:64], un["tv"][:, el, 0:P], un["am"][:, el, 320:384], False, False)
                        pe.wait_ge(*at("sa", (l, "s", j)))
                        mm(pe, ps[:, 0:64], SAB[:, 0, :], un["am"][:, el, P:192], False, True)\
                            .then_inc(*to("ymm", (l, "s", j)))
                        pe.wait_ge(*at("vm", (l, j)))
                        for g in range(2):
                            ps = bank(pe, ("smm", l, j, g), ("m_sum", (l, j, g)))
                            mm(pe, ps, un["tv"][:, el, 256:384], VM[:, 4 * g:4 * g + 4, :], True, False)
                            if g == 0:
                                pe.wait_ge(*at("sam", (l, j)))
                            mm(pe, ps, un["tv"][:, el, P:256], SAM[:, 4 * g:4 * g + 4, :], False, True)\
                                .then_inc(*to("smm", (l, j, g)))
                        for g in range(2):
                            ps = bank(pe, ("sout", l, j, g), ("sout", (l, j, g)))
                            pe.wait_ge(*at("m_new", (l, j, g)))
                            for b in range(4):
                                ins = pe.transpose(ps[:, b * P:(b + 1) * P], M0[:, 4 * g + b, :], ident)
                            ins.then_inc(*to("sout_turned", (l, j, g)))

        def act_rwkv_chunks(act, l):
            ri = rw_of[l]
            for r, members in enumerate(in_round):
                kind = members[0][3]
                for n, _, u, _, _ in members:
                    if r > 0 and last_of(l, r, u):
                        act.wait_ge(*at(*last_of(l, r, u)))
                    elif r == 0 and u == 0:
                        act.wait_ge(*at("prepared", l))
                        act.wait_ge(*at("bonus_summed", (l, 7)))
                    for el in range(4):
                        act.wait_ge(*at("tv_done", (l, n, el)))
                        act.activation(UNIT[u]["tv"][:, el, :], of(("tv", l, n, el))[:, 0:384], ACT.Copy)\
                           .then_inc(*to("tv", (l, n, el)))
                for lev in levels(kind):
                    if lev:
                        for n, _, u, _, _ in members:
                            act.wait_ge(*at("pmm", (l, n, lev)))
                            if lev > 1:
                                act.wait_ge(*at("imm", (l, n, lev - 1, 1)))
                            act.activation(UNIT[u]["p"], of(("p", l, n, lev)), ACT.Copy).then_inc(*to("p", (l, n, lev)))
                if kind == "p":
                    for c in range(4):
                        for n, _, u, _, j in members:
                            act.wait_ge(*at("rhs_done", (l, "p", j, c)))
                            act.activation(RHS[:, u, :], of(("rhs", l, "p", j, c))[:, 0:P], ACT.Copy)\
                               .then_inc(*to("rhs", (l, "p", j, c)))
                        for n, _, u, _, j in members:
                            act.wait_ge(*at("sa_done", (l, "p", j, c)))
                            act.activation(SAB[:, u, :], of(("sa", l, "p", j, c))[:, 0:P], ACT.Copy)\
                               .then_inc(*to("sa", (l, "p", j, c)))
                        for n, _, u, _, j in members:
                            act.wait_ge(*at("ymm", (l, "p", j, c)))
                            if c or r:
                                act.wait_ge(*at("state", (l, j, c - 1) if c else (l, j - 2, 3)))
                            act.activation(MG[:, u, :], of(("mu", l, "p", j, c))[:, 0:P], ACT.Copy,
                                           scale=GE[:, j, c:c + 1]).then_inc(*to("mg", (l, j, c)))
                    for n, _, u, _, j in members:
                        act.wait_ge(*at("pstate_turned", (l, j)))
                        if r:
                            act.wait_ge(*at(f"pstate_stored{u}", (l, j - 2)))
                        act.activation(PST[:, u, :], of(("pst", l, j))[:, 0:P], ACT.Copy).then_inc(*to("pstate", (l, j)))
                        act.wait_ge(*at("pstate", (l, j)))
                        for half in range(2):
                            hs = slice(64 * half, 64 * half + 64)
                            act.dma_start(io["p_rwkv_wkv"][ri, 0, 2 * j + half], PST[hs, u, hs])\
                               .then_inc(*to(f"pstate_stored{u}", (l, j), 16))
                else:
                    if r == 4:
                        for u in range(2):
                            act.wait_ge(*at(f"pstate_stored{u}", (l, 6 + u)))
                        act.activation(MG[:, 0, :], ident, ACT.Copy, scale=0.0).then_inc(*to("z_zero", l))
                        act.wait_ge(*at("z_zero", l))
                    for el in range(4):
                        j = 4 * members[0][4] + el
                        for g in range(2):
                            act.wait_ge(*at("sin_turned", (l, j, g)))
                            act.activation(M0[:, 4 * g:4 * g + 4, :], of(("sin", l, j, g)), ACT.Copy)\
                               .then_inc(*to("m0", (l, j, g)))
                        act.wait_ge(*at("z_done", (l, j)))
                        z = of(("z", l, j))[:, 0:P].rearrange("p (b a s) -> p b a s", b=DEC, a=2)
                        for half in range(2):
                            hs = slice(64 * half, 64 * half + 64)
                            act.activation(MG[hs, 0, hs].rearrange("p (b s) -> p b s", b=DEC), z[hs, :, 0, :], ACT.Copy)
                        act.activation(MG[:, 1, 0:64].rearrange("p (b s) -> p b s", b=DEC), z[:, :, 1, :], ACT.Copy)\
                           .then_inc(*to("z", (l, j)))
                        act.wait_ge(*at("rhs_done", (l, "s", j)))
                        act.activation(RHS[:, 0, :], of(("rhs", l, "s", j))[:, 0:P], ACT.Copy).then_inc(*to("rhs", (l, "s", j)))
                        act.wait_ge(*at("sa_done", (l, "s", j)))
                        if j:
                            act.wait_ge(*at("sam", (l, j - 1)))
                        act.activation(SAB[:, 0, :], of(("sa", l, "s", j))[:, 0:P], ACT.Copy).then_inc(*to("sa", (l, "s", j)))
                        for g in range(2):
                            act.wait_ge(*at("sout_turned", (l, j, g)))
                            act.activation(SIN[:, 4 * g:4 * g + 4, :], of(("sout", l, j, g)), ACT.Copy)\
                               .then_inc(*to("sout", (l, j, g)))

        def dve_rwkv_chunks(dve, l):
            for r, members in enumerate(in_round):
                kind = members[0][3]
                for n, _, u, _, _ in members:
                    if last_of(l, r, u):
                        dve.wait_ge(*at(*last_of(l, r, u)))
                    for el in range(4):
                        dve.wait_ge(*at("amm", (l, n, el)))
                        dve.tensor_tensor(UNIT[u]["am"][:, el, :], of(("am", l, n, el))[:, 0:384],
                                          const("amask_" + kind), ALU.mult).then_inc(*to("am", (l, n, el)))
                idb = ident.unsqueeze(1).broadcast_to([P, 4, P])
                for lev in levels(kind):
                    for n, _, u, _, _ in members:
                        un = UNIT[u]
                        if lev == 0:
                            dve.wait_ge(*at("pmm", (l, n, 0)))
                            dve.tensor_tensor(un["inv"][:, :, 0:P], of(("p", l, n, 0))[:, :].rearrange("p (a b) -> p a b", a=4),
                                              idb, ALU.add)
                            dve.tensor_tensor(un["inv"][:, :, P:256], un["off"], idb, ALU.add)\
                               .then_inc(*to("inv", (l, n, 0)))
                        else:
                            dve.wait_ge(*at("inv", (l, n, lev - 1)))
                            for g in range(2):
                                dve.wait_ge(*at("imm", (l, n, lev, g)))
                                part = un["inv"][:, 2 * g:2 * g + 2, :]
                                ins = dve.tensor_tensor(part, part, of(("imm", l, n, lev, g))[:, :]
                                                        .rearrange("p (a b) -> p a b", a=2), ALU.add)
                            ins.then_inc(*to("inv", (l, n, lev)))
                if kind == "p":
                    for c in range(4):
                        for n, _, u, _, j in members:
                            dve.wait_ge(*at("y_done", (l, "p", j, c)))
                            dve.tensor_copy(block(BR)[:, j, c * 64:c * 64 + 64], of(("ym", l, "p", j, c))[:, 0:64])\
                               .then_inc(*to("y", (l, "p", j, c)))
                            dve.wait_ge(*at("mg", (l, j, c)))
                            if c == 0:
                                if r:
                                    dve.wait_ge(*at("pstate_turned", (l, j - 2)))
                                ins = dve.tensor_copy(MST[:, u, :], MG[:, u, :])
                            else:
                                dve.wait_ge(*at("state", (l, j, c - 1)))
                                ins = dve.scalar_tensor_tensor(out=MST[:, u, :], in0=MST[:, u, :], scalar=GE[:, j, c:c + 1],
                                                               in1=MG[:, u, :], op0=ALU.mult, op1=ALU.add)
                            ins.then_inc(*to("state", (l, j, c)))
                else:
                    for el in range(4):
                        j = 4 * members[0][4] + el
                        dve.wait_ge(*at("ymm", (l, "s", j)))
                        dve.tensor_copy(block(BR)[:, j, SEQ:NT], of(("ym", l, "s", j))[:, 0:64]).then_inc(*to("y", (l, "s", j)))
                        for g in range(2):
                            dve.wait_ge(*at("smm", (l, j, g)))
                            part = M0[:, 4 * g:4 * g + 4, :]
                            dve.tensor_tensor(part, part, of(("smm", l, j, g))[:, :].rearrange("p (a b) -> p a b", a=4),
                                              ALU.add).then_inc(*to("m_sum", (l, j, g)))
                        for g in range(2):
                            dve.wait_ge(*at("m_sum", (l, j, g)))
                            part = M0[:, 4 * g:4 * g + 4, :]
                            ge = GE[:, j, 4 + 4 * g:8 + 4 * g].unsqueeze(2).broadcast_to([P, 4, P])
                            dve.tensor_tensor(part, part, ge, ALU.mult).then_inc(*to("m_new", (l, j, g)))

        QKV = arena(0, 32, NT)
        Z = arena(4 * BLK, 16, NT)
        g0 = 6 * BLK
        XG = arena(g0, 4, 348)
        CTG, CVG, EXG, GDG = (arena(g0 + 1392 + i * 688, 2, 344) for i in range(4))
        ZE = arena(g0 + 4144, 2, NT)
        TAILG = arena(g0 + 4784, 864)
        TOUTG = arena(g0 + 5648, 7, P)
        ROWS = MID[0:16, :, :]
        GU = 3072
        def gunit(u):
            o = g0 + u * GU
            return dict(am=arena(o, 4, P), aq=arena(o + 512, 4, P), off=arena(o + 1024, 4, P), p=arena(o + 1536, 4, P),
                        vb=arena(o + 2048, 4, P), kg=arena(o + 2560, 4, P), inv=UNIT[u]["inv"])
        GUNIT = [gunit(0), gunit(1)]
        o_ = g0 + 2 * GU
        QG, EG, GCS, BS = (arena(o_ + i * 1280, 4, NT) for i in range(4))
        GS = arena(o_ + 5120, 4, P)
        GR = halves[0][:, 0:512].rearrange("p (u n) -> p u n", u=4)
        GV = halves[1][:, 0:512].rearrange("p (u n) -> p u n", u=4)
        TOK = MID[:, 0, :].bitcast(F32) if False else None
        SGS = [arena(g0 + GU, DEC, P), arena(g0 + GU + 1024, DEC, P)]
        VNM = arena(g0 + GU + 2048, DEC, P)
        KQ = halves[1][:, 512:640].rearrange("p (b a s) -> p b a s", b=DEC, a=2)
        ZG = halves[1][:, 640:768].rearrange("p (a t) -> p a t", a=2)
        TOKS = SMALL[:, 0:96]
        tokens3 = halves[1][:, 768:768 + 288].rearrange("p (c k h) -> p c k h", c=3, k=6)
        T_BETA, T_GC, T_EGL, T_NBE, T_EG, T_X = range(6)

        def g_window(s):
            return XG[:, s, 259:347].rearrange("p (b w) -> p b w", b=DEC)

        tailg_p = TAILG[:, 0:96].rearrange("p (j m) -> p j m", j=3)
        tailg_s = TAILG[:, 96:864].rearrange("p (b j m) -> p b j m", b=DEC, j=3)
        gq = 8

        g_rounds = [[("p", 2 * r), ("p", 2 * r + 1)] for r in range(4)] + [[("s", i)] for i in range(4)]
        g_in_round, _n = [], 0
        for r, members in enumerate(g_rounds):
            g_in_round.append([])
            for u, (kind, i) in enumerate(members):
                g_in_round[-1].append((_n, r, u, kind, i))
                _n += 1

        def g_head(kind, i, el):
            return 2 * i + el // 2 if kind == "p" else 4 * i + el

        def g_levels(kind):
            return range(7 if kind == "p" else 3)

        def g_last(r, u):
            if r == 0:
                return None
            if r <= 4:
                return ("g_mu", (2 * (2 * (r - 1) + u) + 1, 1))
            return ("gs_mm", (4 * (r - 5) + 3, 1))

        def pe_gdn(pe, l):
            pe_norm(pe, gq)
            for c in range(24):
                w = W[:, weight(pe, ("gin", c)), :]
                for j in range(2):
                    t = 2 * c + j
                    ps = bank(pe, ("gin", t), ("gxp", t) if t < 32 else ("z_out", t))
                    for k in range(MT):
                        if t == 0:
                            pe.wait_ge(*at("h", (gq, k)))
                        ins = mm(pe, ps[:, 0:NT], w[:, k * 256 + j * P:k * 256 + j * P + P], H[:, k, :], k == 0, k == 7)
                    ins.then_inc(*to("gin_done", t))
                weight_used[("gin", c)] = ("gin_done", t)
            w = W[:, weight(pe, ("gin", 24)), :]
            for x, name in enumerate(("beta", "dt")):
                ps = bank(pe, ("gin", name), ("g_e1", 0) if name == "beta" else ("g_t", 0))
                for k in range(MT):
                    ins = mm(pe, ps[0:16, 0:NT], w[:, k * 32 + 16 * x:k * 32 + 16 * x + 16], H[:, k, :], k == 0, k == 7)
                ins.then_inc(*to("gin_done", name))
            weight_used[("gin", 24)] = ("gin_done", "dt")
            for g, (first, n) in enumerate([(0, 4), (4, 3)]):
                ps = bank(pe, ("gtail", g), ("gtail_rows", g))
                for i in range(first, first + n):
                    a, b = (0, 96) if i == 0 else (96 + (i - 1) * P, 96 + i * P)
                    if i == 0:
                        pe.wait_ge(*at("gtail", 31))
                    ins = pe.transpose(ps[0:b - a, (i - first) * P:(i - first + 1) * P], TAILG[:, a:b], ident)
                ins.then_inc(*to("gtail_turned", g))
            for t in range(16):
                ps = bank(pe, ("l2", t), ("l2_ln", t))
                pe.wait_ge(*at("l2_sq", t))
                mm(pe, ps[:, 0:NT], ones, SQ[:, t % 4, :], True, True).then_inc(*to("l2_summed", t))
            ps = bank(pe, ("tok", 0), ("tok", 0))
            pe.wait_ge(*at("g_rows", 0))
            for c in range(3):
                n = P if c < 2 else 64
                for x, row in enumerate((0, 3, 4)):
                    ins = pe.transpose(ps[0:n, (c * 3 + x) * 16:(c * 3 + x) * 16 + 16], ROWS[:, row, c * P:c * P + n],
                                       ident[0:16, 0:16])
            ins.then_inc(*to("tok_turned", 0))
            for r, members in enumerate(g_in_round):
                kind = members[0][3]
                size = P if kind == "p" else 64
                t0 = 0 if kind == "p" else SEQ
                for n, _, u, _, i in members:
                    un = GUNIT[u]
                    for x in range(2 if kind == "p" else 4):
                        h = g_head(kind, i, 2 * x if kind == "p" else x)
                        sel = ident[0:16, h:h + 1].broadcast_to([16, P])
                        for what, row in (("gc", 3), ("bb", 0)):
                            ps = bank(pe, (what, n, x), (what, (n, x)))
                            mm(pe, ps[:, 0:NT], sel, ROWS[:, row, :], True, True).then_inc(*to(what + "_done", (n, x)))
                    if r == 0 and u == 0:
                        pe.wait_ge(*at("qk_normed", 15))
                    ps = bank(pe, ("kq", n), ("kq_read", n))
                    if kind == "p":
                        for c in range(2):
                            cs = slice(c * P, c * P + P)
                            mm(pe, ps[:, c * P:c * P + P], QKV[:, 8 + i, cs], QKV[:, 8 + i, cs], True, True)
                            ins = mm(pe, ps[:, 256 + c * P:384 + c * P], QKV[:, 8 + i, cs], QKV[:, i, cs], True, True)
                    else:
                        for x in range(2):
                            hq = 2 * i + x
                            mm(pe, ps[0:64, x * 64:x * 64 + 64], QKV[:, 8 + hq, SEQ:NT], QKV[:, 8 + hq, SEQ:NT], True, True)
                            ins = mm(pe, ps[0:64, 256 + x * 64:320 + x * 64], QKV[:, 8 + hq, SEQ:NT], QKV[:, hq, SEQ:NT],
                                     True, True)
                    ins.then_inc(*to("kq_done", n))
                    ps = bank(pe, ("vt", n), ("vt", n))
                    for el in range(4):
                        c = slice((el % 2) * P, (el % 2) * P + P) if kind == "p" else slice(SEQ, NT)
                        ins = pe.transpose(ps[0:size, el * P:el * P + P], QKV[:, 16 + g_head(kind, i, el), c], ident)
                    ins.then_inc(*to("vt_done", n))
                    ps = bank(pe, ("kt", n), ("kt", n))
                    for x in range(2):
                        src = QKV[:, 8 + i, x * P:x * P + P] if kind == "p" else QKV[:, 8 + 2 * i + x, SEQ:NT]
                        ins = pe.transpose(ps[0:size, x * P:x * P + P], src, ident)
                    ins.then_inc(*to("kt_done", n))
                for lev in g_levels(kind):
                    for n, _, u, _, _ in members:
                        un = GUNIT[u]
                        pe.wait_ge(*at("goff", (n, lev)))
                        if lev:
                            pe.wait_ge(*at("ginv", (n, lev - 1)))
                        ps = bank(pe, ("gp", n, lev), ("gp", (n, lev)) if lev else ("ginv", (n, 0)))
                        for el in range(4):
                            ins = mm(pe, ps[0:size, el * P:el * P + size], un["off"][0:size, el, 0:size],
                                     un["inv"][0:size, el, 0:size] if lev else ident[0:size, 0:size], True, True)
                        ins.then_inc(*to("gpmm", (n, lev)))
                    if lev:
                        for n, _, u, _, _ in members:
                            un = GUNIT[u]
                            pe.wait_ge(*at("gp", (n, lev)))
                            for g in range(2):
                                ps = bank(pe, ("gimm", n, lev, g), ("ginv", (n, lev)))
                                for el in (2 * g, 2 * g + 1):
                                    o = (el % 2) * 256
                                    it = un["inv"][0:size, el, P:P + size]
                                    mm(pe, ps[0:size, o:o + size], it, un["p"][0:size, el, 0:size], True, True)
                                    ins = mm(pe, ps[0:size, o + P:o + P + size], un["p"][0:size, el, 0:size], it, True, True)
                                ins.then_inc(*to("gimm", (n, lev, g)))
                if kind == "p":
                    for c in range(2):
                        for step in range(3):
                            for n, _, u, _, i in members:
                                un = GUNIT[u]
                                for x in range(2):
                                    h, el, s = 2 * i + x, 2 * x + c, 2 * u + x
                                    cs = slice(c * P, c * P + P)
                                    if step == 0 and c:
                                        pe.wait_ge(*at("g_state", (h, 0)))
                                        ps = bank(pe, ("ks", h), ("g_rhs", h))
                                        mm(pe, ps[:, 0:P], QKV[:, 8 + i, cs], GS[:, s, :], True, True)\
                                            .then_inc(*to("ks_done", h))
                                    if step == 1:
                                        if c == 0:
                                            pe.wait_ge(*at("ginv", (n, 6)))
                                            pe.wait_ge(*at("vt", n))
                                        else:
                                            pe.wait_ge(*at("g_rhs", h))
                                        ps = bank(pe, ("vn", h, c), ("vn", (h, c)))
                                        mm(pe, ps[:, 0:P], un["inv"][:, el, P:256], un["vb"][:, el, :] if c == 0 else GR[:, s, :],
                                           True, True).then_inc(*to("vn_done", (h, c)))
                                    if step == 2:
                                        pe.wait_ge(*at("vn", (h, c)))
                                        ps = bank(pe, ("go", h, c), ("go", (h, c)))
                                        if c:
                                            pe.wait_ge(*at("qg", (n, x)))
                                            mm(pe, ps[:, 0:P], GS[:, s, :], QG[:, s, cs], True, False)
                                        mm(pe, ps[:, 0:P], GV[:, s, :], un["aq"][:, el, :], not c, True)\
                                            .then_inc(*to("go_done", (h, c)))
                                        if c == 0:
                                            pe.wait_ge(*at("kt", n))
                                        ps = bank(pe, ("gmu", h, c), ("g_state", (h, c)))
                                        mm(pe, ps[:, 0:P], un["kg"][:, el, :], GV[:, s, :], True, True)\
                                            .then_inc(*to("g_mu", (h, c)))
                else:
                    n, _, _, _, i = members[0]
                    un = GUNIT[0]
                    for el in range(4):
                        h = 4 * i + el
                        S = SGS[h % 2]
                        pe.wait_ge(*at(f"gs_in{h % 2}", h))
                        pe.wait_ge(*at("kq8", h))
                        ps = bank(pe, ("gz", h), ("gz", h))
                        for b in range(DEC):
                            ins = mm(pe, ps[:, 16 * b:16 * b + 16], S[:, b, :], KQ[:, b, :, :], True, True)
                        ins.then_inc(*to("gz_done", h))
                        pe.wait_ge(*at("gz", h))
                        ps = bank(pe, ("gks", h), ("gs_rhs", h))
                        mm(pe, ps[0:64, 0:P], ZG[:, 0, :], ident, True, True).then_inc(*to("gks_done", h))
                        pe.wait_ge(*at("gs_rhs", h))
                        if el == 0:
                            pe.wait_ge(*at("ginv", (n, 2)))
                        ps = bank(pe, ("gvn", h), ("gs_vn", h))
                        mm(pe, ps[0:64, 0:P], un["inv"][0:64, el, P:P + 64], GR[0:64, 0, :], True, True)\
                            .then_inc(*to("gvn_done", h))
                        ps = bank(pe, ("gso", h), ("gs_o", h))
                        mm(pe, ps[:, 0:64], ident, ZG[:, 1, :], True, False)
                        pe.wait_ge(*at("gs_vn", h))
                        mm(pe, ps[:, 0:64], GV[0:64, 0, :], un["aq"][0:64, el, 0:64], False, True).then_inc(*to("gso_done", h))
                        if el == 0:
                            pe.wait_ge(*at("kt", n))
                        pe.wait_ge(*at("vnm", h))
                        for g in range(2):
                            ps = bank(pe, ("gsm", h, g), ("gs_new", (h, g)))
                            mm(pe, ps, un["kg"][0:64, el, :], VNM[0:64, 4 * g:4 * g + 4, :], True, True)\
                                .then_inc(*to("gs_mm", (h, g)))
            for h in range(16):
                ps = bank(pe, ("gn", h), ("gn_ln", h))
                pe.wait_ge(*at("go_sq", h))
                mm(pe, ps[:, 0:NT], ones, SQ[:, h % 4, :], True, True).then_inc(*to("go_summed", h))
            pe_out(pe, gq + 1, [[("gwo", c)] for c in range(8)], 16, lambda n: [("g_gated", n)], lambda n: Z[:, n, :])
            pe_norm(pe, gq + 1)

        def act_gdn(act, l):
            act_pre_norm(act, gq)
            act.wait_ge(*at("heads_in", 0))
            act.activation(AH[:, 2:3], AH[:, 0:1], ACT.Exp).then_inc(*to("exp_alog", 0))

            def e_minus(t):
                act.wait_ge(*at("gconv", t))
                if t >= 2:
                    act.wait_ge(*at("g_1e", t - 2))
                act.activation(EXG[:, t % 2, :], CVG[:, t % 2, :], ACT.Exp, scale=-1.0).then_inc(*to("g_e", t))

            for t in range(32):
                if t >= 4:
                    act.wait_ge(*at("gconv", t - 4))
                    act.wait_ge(*at("gtail", t - 4))
                act.wait_ge(*at("gin_done", t))
                ps = of(("gin", t))
                act.activation(XG[:, t % 4, 3:259], ps[:, 0:SEQ], ACT.Copy)
                act.activation(g_window(t % 4)[:, :, 3:11], sample(ps[:, SEQ:NT]), ACT.Copy).then_inc(*to("gxp", t))
                if t:
                    e_minus(t - 1)
            e_minus(31)
            for t in range(32, 48):
                act.wait_ge(*at("gin_done", t))
                if t >= 34:
                    act.wait_ge(*at("z_1e", t - 2))
                act.activation(ZE[:, t % 2, :], of(("gin", t))[:, 0:NT], ACT.Exp, scale=-1.0)
                act.activation(Z[:, t - 32, :], of(("gin", t))[:, 0:NT], ACT.Copy).then_inc(*to("z_out", t))
            act.wait_ge(*at("gin_done", "beta"))
            act.activation(ROWS[:, 0, :], of(("gin", "beta"))[0:16, 0:NT], ACT.Exp, scale=-1.0).then_inc(*to("g_e1", 0))
            act.wait_ge(*at("g_abs", 0))
            act.activation(ROWS[:, 2, :], ROWS[:, 2, :], ACT.Exp, scale=-1.0).then_inc(*to("g_sp", 0))
            act.wait_ge(*at("g_sp", 0))
            act.activation(ROWS[:, 2, :], ROWS[:, 2, :], ACT.Ln, bias=1.0).then_inc(*to("g_sp", 1))
            for g, n in ((0, 4), (1, 3)):
                act.wait_ge(*at("gtail_turned", g))
                act.activation(TOUTG[:, 4 * g:4 * g + n, :], of(("gtail", g))[:, 0:n * P], ACT.Copy)\
                   .then_inc(*to("gtail_rows", g))
            act.wait_ge(*at("gtail_rows", 1))
            act.dma_start(io["p_gdn_conv"][0, 0].rearrange("j (m p) -> (j m) p", p=P), TOUTG[0:96, 0, :])\
               .then_inc(*to("gtail_stored", 0, 16))
            rows = io["s_gdn_conv"][0].rearrange("b j (m p) -> (b j m) p", p=P)
            act.dma_start(rows.rearrange("(i r) p -> r i p", r=P), TOUTG[:, 1:7, :]).then_inc(*to("gtail_stored", 0, 16))
            for t in range(16):
                act.wait_ge(*at("g_silu", t))
                act_square(act, t, QKV[:, t, :], ("l2_sq", t), lambda n: ("l2_summed", n), 16)
                if t:
                    l2_rstd(act, t - 1)
            l2_rstd(act, 15)
            act.wait_ge(*at("tok_turned", 0))
            ps = of(("tok", 0))
            for c in range(3):
                m = P if c < 2 else 64
                view = ps[0:m, c * 48:c * 48 + 48].rearrange("p (k h) -> p k h", k=3)
                act.activation(tokens3[0:m, c, 0:2, :], view[:, 0:2, :], ACT.Copy)
                act.activation(tokens3[0:m, c, T_EG, :], view[:, 1, :], ACT.Exp)
                ins = act.activation(tokens3[0:m, c, T_EGL, :], view[:, 2, :], ACT.Exp)
            ins.then_inc(*to("tok", 0))
            act.wait_ge(*at("gtail_stored", 0))
            for r, members in enumerate(g_in_round):
                kind = members[0][3]
                size = P if kind == "p" else 64
                for n, _, u, _, i in members:
                    un = GUNIT[u]
                    if r == 0 and u == 0:
                        act.wait_ge(*at("z_silu", 47))
                    if g_last(r, u):
                        act.wait_ge(*at(*g_last(r, u)))
                    if kind == "s" and r == 4:
                        act.wait_ge(*at("g_state", (15, 1)))
                    for x in range(2 if kind == "p" else 4):
                        s = 2 * u + x
                        if r:
                            for step in g_rows_read(r, u, x):
                                act.wait_ge(*at(*step))
                        act.wait_ge(*at("gc_done", (n, x)))
                        act.activation(EG[:, s, :], of(("gc", n, x))[:, 0:NT], ACT.Exp)
                        act.activation(GCS[:, s, :], of(("gc", n, x))[:, 0:NT], ACT.Copy).then_inc(*to("gc", (n, x)))
                        act.wait_ge(*at("bb_done", (n, x)))
                        act.activation(BS[:, s, :], of(("bb", n, x))[:, 0:NT], ACT.Copy).then_inc(*to("bb", (n, x)))
                    act.wait_ge(*at("vt_done", n))
                    act.wait_ge(*at("tok", 0))
                    for el in range(4):
                        c, h = (el % 2, 2 * i + el // 2) if kind == "p" else (2, 4 * i + el)
                        ins = act.activation(un["vb"][0:size, el, :], of(("vt", n))[0:size, el * P:el * P + P], ACT.Copy,
                                             scale=tokens3[0:size, c, T_BETA, h:h + 1])
                    ins.then_inc(*to("vt", n))
                    act.wait_ge(*at("kt_done", n))
                    for el in range(4):
                        c, h = (el % 2, 2 * i + el // 2) if kind == "p" else (2, 4 * i + el)
                        x = el % 2 if kind == "p" else el // 2
                        ins = act.activation(un["kg"][0:size, el, :], of(("kt", n))[0:size, x * P:x * P + P], ACT.Copy,
                                             scale=tokens3[0:size, c, T_EGL, h:h + 1])
                    ins.then_inc(*to("kt", n))
                    act.wait_ge(*at("g_diff", n))
                    act.activation(un["p"][0:size, :, 0:size], un["p"][0:size, :, 0:size], ACT.Exp).then_inc(*to("g_decay", n))
                for lev in g_levels(kind):
                    if lev:
                        for n, _, u, _, _ in members:
                            act.wait_ge(*at("gpmm", (n, lev)))
                            if lev == 1:
                                act.wait_ge(*at("g_aq", n))
                            else:
                                act.wait_ge(*at("gimm", (n, lev - 1, 1)))
                            act.activation(GUNIT[u]["p"][0:size, :, 0:size],
                                           of(("gp", n, lev))[0:size, :].rearrange("p (a b) -> p a b", a=4)[:, :, 0:size],
                                           ACT.Copy).then_inc(*to("gp", (n, lev)))
                if kind == "p":
                    for c in range(2):
                        for n, _, u, _, i in members:
                            for x in range(2):
                                h, s = 2 * i + x, 2 * u + x
                                act.wait_ge(*at("vn_done", (h, c)))
                                if c == 0 and r:
                                    act.wait_ge(*at("g_mu", (h - 4, 1)))
                                if c == 1:
                                    act.wait_ge(*at("g_mu", (h, 0)))
                                act.activation(GV[:, s, :], of(("vn", h, c))[:, 0:P], ACT.Copy).then_inc(*to("vn", (h, c)))
                        for n, _, u, _, i in members:
                            for x in range(2):
                                h = 2 * i + x
                                act.wait_ge(*at("go_done", (h, c)))
                                act.activation(QKV[:, 16 + h, c * P:c * P + P], of(("go", h, c))[:, 0:P], ACT.Copy)\
                                   .then_inc(*to("go", (h, c)))
                    for n, _, u, _, i in members:
                        for x in range(2):
                            h, s = 2 * i + x, 2 * u + x
                            act.wait_ge(*at("g_state", (h, 1)))
                            act.dma_start(io["p_gdn_S"][0, 0, h], GS[:, s, :]).then_inc(*to(f"gps_stored{s}", h, 16))
                else:
                    i = members[0][4]
                    for el in range(4):
                        h = 4 * i + el
                        act.wait_ge(*at("gz_done", h))
                        z = of(("gz", h))[:, 0:P].rearrange("p (b a s) -> p a b s", b=DEC, a=2)
                        act.activation(ZG[:, 0, :].rearrange("p (b s) -> p b s", b=DEC), z[:, 0], ACT.Copy)
                        act.activation(ZG[:, 1, :].rearrange("p (b s) -> p b s", b=DEC), z[:, 1], ACT.Copy)\
                           .then_inc(*to("gz", h))
                        act.wait_ge(*at("gvn_done", h))
                        if h:
                            act.wait_ge(*at("vnm", h - 1))
                        act.activation(GV[0:64, 0, :], of(("gvn", h))[0:64, 0:P], ACT.Copy).then_inc(*to("gs_vn", h))
                        act.wait_ge(*at("gso_done", h))
                        act.activation(QKV[:, 16 + h, SEQ:NT], of(("gso", h))[:, 0:64], ACT.Copy).then_inc(*to("gs_o", h))
            act.wait_ge(*at("gs_o", 15))
            act.wait_ge(*at("gz_done", 15))
            act.wait_ge(*at("gs_mm", (15, 1)))
            act.wait_ge(*at("vnm", 15))
            for h in range(16):
                act_square(act, h, QKV[:, 16 + h, :], ("go_sq", h), lambda n: ("go_summed", n), 16)
                if h:
                    gn_rstd(act, h - 1)
            gn_rstd(act, 15)
            for i in range(2):
                act.wait_ge(*at(f"gs_out{i}", 14 + i))
            for s in range(4):
                act.wait_ge(*at(f"gps_stored{s}", 12 + s))
            act_outputs(act, gq + 1)

        def g_rows_read(r, u, x):
            if r <= 3:
                n, _, _, kind, i = g_in_round[r - 1][u]
                h = 2 * i + x
                return [("g_am", n), ("g_state", (h, 1))]
            if r == 4:
                return [("g_state", (15, 1)), ("g_am", 7)]
            n, _, _, kind, i = g_in_round[r - 1][0]
            return [("g_am", n), ("gs_new", (4 * i + 3, 1)), ("kq8", 4 * i + 3)]

        def l2_rstd(act, t):
            act.wait_ge(*at("l2_summed", t))
            if t:
                act.wait_ge(*at("l2_rstd", t - 1))
            act.activation(halves[0][:, 0:NT], of(("l2", t))[:, 0:NT], ACT.Ln, bias=EB[:, 0:1]).then_inc(*to("l2_ln", t))
            act.wait_ge(*at("l2_ln", t))
            if t:
                act.wait_ge(*at("qk_normed", t - 1))
            act.activation(halves[0][:, NT:2 * NT], halves[0][:, 0:NT], ACT.Exp, scale=-0.5).then_inc(*to("l2_rstd", t))

        def gn_rstd(act, h):
            act.wait_ge(*at("go_summed", h))
            if h:
                act.wait_ge(*at("gn_rstd", h - 1))
                act.wait_ge(*at("g_n1", h - 1))
            act.activation(RS[:, 0, :], of(("gn", h))[:, 0:NT], ACT.Ln, bias=EB[:, 0:1], scale=1.0 / P).then_inc(*to("gn_ln", h))
            act.wait_ge(*at("gn_ln", h))
            act.activation(RS[:, 1, :], RS[:, 0, :], ACT.Exp, scale=-0.5).then_inc(*to("gn_rstd", h))

        def dve_gdn(dve, l):
            dve_pre_norm(dve, gq)

            def silu(t):
                p = t % 2
                dve.wait_ge(*at("g_e", t))
                if t:
                    dve.wait_ge(*at("g_silu", t - 1))
                dve.tensor_scalar(GDG[:, 0, :], EXG[:, p, :], 1.0, None, ALU.add).then_inc(*to("g_1e", t))
                dve.wait_ge(*at("g_1e", t))
                dve.reciprocal(GDG[:, 1, :], GDG[:, 0, :]).then_inc(*to("g_sig", t))
                dve.wait_ge(*at("g_sig", t))
                dve.tensor_tensor(QKV[:, t, 0:SEQ], CVG[:, p, 0:SEQ], GDG[:, 1, 0:SEQ], ALU.mult)
                win = [v.rearrange("p (b w) -> p b w", b=DEC)[:, :, 3:11] for v in (CVG[:, p, 256:344], GDG[:, 1, 256:344])]
                dve.tensor_tensor(sample(QKV[:, t, SEQ:NT]), win[0], win[1], ALU.mult).then_inc(*to("g_silu", t))

            for t in range(32):
                w = lambda tap: par("gdn_conv_w", tap * 32 + t)
                x = XG[:, t % 4, :]
                dve.wait_ge(*at("gxp", t))
                dve.wait_ge(*at("gxp_state", t))
                if t:
                    dve.wait_ge(*at("gconv", t - 1))
                dve.tensor_scalar(CTG[:, 0, :], x[:, 3:347], w(3), None, ALU.mult).then_inc(*to("gtap3", t))
                dve.wait_ge(*at("gtap3", t))
                dve.scalar_tensor_tensor(out=CTG[:, 1, :], in0=x[:, 2:346], scalar=w(2), in1=CTG[:, 0, :],
                                         op0=ALU.mult, op1=ALU.add).then_inc(*to("gtap2", t))
                dve.wait_ge(*at("gtap2", t))
                dve.scalar_tensor_tensor(out=CTG[:, 0, :], in0=x[:, 1:345], scalar=w(1), in1=CTG[:, 1, :],
                                         op0=ALU.mult, op1=ALU.add).then_inc(*to("gtap1", t))
                dve.wait_ge(*at("gtap1", t))
                if t >= 2:
                    dve.wait_ge(*at("g_silu", t - 2))
                dve.scalar_tensor_tensor(out=CVG[:, t % 2, :], in0=x[:, 0:344], scalar=w(0), in1=CTG[:, 0, :],
                                         op0=ALU.mult, op1=ALU.add).then_inc(*to("gconv", t))
                if t:
                    silu(t - 1)
            silu(31)
            for t in range(32, 48):
                dve.wait_ge(*at("z_out", t))
                dve.tensor_scalar(ZE[:, t % 2, :], ZE[:, t % 2, :], 1.0, None, ALU.add).then_inc(*to("z_add", t))
                dve.wait_ge(*at("z_add", t))
                dve.reciprocal(ZE[:, t % 2, :], ZE[:, t % 2, :]).then_inc(*to("z_rec", t))
                dve.wait_ge(*at("z_rec", t))
                dve.tensor_tensor(Z[:, t - 32, :], Z[:, t - 32, :], ZE[:, t % 2, :], ALU.mult).then_inc(*to("z_1e", t))
            dve.wait_ge(*at("z_1e", 47))
            R = lambda k: ROWS[:, k, :]
            dve.wait_ge(*at("gin_done", "dt"))
            dve.tensor_scalar(R(1), of(("gin", "dt"))[0:16, 0:NT], AH[:, 1:2], None, ALU.add).then_inc(*to("g_t", 0))
            dve.wait_ge(*at("g_t", 0))
            dve.scalar_tensor_tensor(out=R(2), in0=R(1), scalar=-1.0, in1=R(1), op0=ALU.mult, op1=ALU.max)\
               .then_inc(*to("g_abs", 0))
            dve.wait_ge(*at("g_e1", 0))
            dve.tensor_scalar(R(0), R(0), 1.0, None, ALU.add).then_inc(*to("g_r", 0))
            dve.wait_ge(*at("g_r", 0))
            dve.reciprocal(R(0), R(0)).then_inc(*to("g_r", 1))
            dve.wait_ge(*at("g_sp", 1))
            dve.scalar_tensor_tensor(out=R(1), in0=R(1), scalar=0.0, in1=R(2), op0=ALU.max, op1=ALU.add)\
               .then_inc(*to("g_r", 2))
            dve.wait_ge(*at("g_r", 2))
            dve.wait_ge(*at("exp_alog", 0))
            dve.tensor_scalar(R(1), R(1), AH[:, 2:3], -1.0, ALU.mult, ALU.mult).then_inc(*to("g_r", 3))
            dve.wait_ge(*at("g_r", 3))
            dve.tensor_tensor_scan(R(3), const("seg128")[0:16, :], R(1), 0.0, ALU.mult, ALU.add).then_inc(*to("g_r", 4))
            dve.wait_ge(*at("g_r", 4))
            pr = R(3)[:, 0:SEQ].rearrange("p (c t) -> p c t", c=2)
            dve.tensor_tensor(R(4)[:, 0:SEQ].rearrange("p (c t) -> p c t", c=2),
                              pr[:, :, P - 1:P].broadcast_to([16, 2, P]), pr, ALU.subtract)
            sm = sample(R(3)[:, SEQ:NT])
            dve.tensor_tensor(sample(R(4)[:, SEQ:NT]), sm[:, :, 7:8].broadcast_to([16, DEC, 8]), sm, ALU.subtract)\
               .then_inc(*to("g_rows", 0))
            for t in range(16):
                dve.wait_ge(*at("l2_rstd", t))
                dve.scalar_tensor_tensor(out=QKV[:, t, :], in0=QKV[:, t, :], scalar=float(P ** -0.5) if t < 8 else 1.0,
                                         in1=halves[0][:, NT:2 * NT], op0=ALU.mult, op1=ALU.mult)\
                   .then_inc(*to("qk_normed", t))
            dve.wait_ge(*at("tok", 0))
            for c in range(3):
                m = P if c < 2 else 64
                ins = dve.scalar_tensor_tensor(out=tokens3[0:m, c, T_NBE, :], in0=tokens3[0:m, c, T_BETA, :], scalar=-1.0,
                                               in1=tokens3[0:m, c, T_EG, :], op0=ALU.mult, op1=ALU.mult)
            ins.then_inc(*to("g_nbe", 0))
            dve.sem_inc(*to("z_silu", 47))
            for r, members in enumerate(g_in_round):
                kind = members[0][3]
                size = P if kind == "p" else 64
                for n, _, u, _, i in members:
                    un = GUNIT[u]
                    if n == 0:
                        dve.wait_ge(*at("gtail_stored", 0))
                    if g_last(r, u):
                        dve.wait_ge(*at(*g_last(r, u)))
                    if kind == "s" and r == 4:
                        dve.wait_ge(*at("g_mu", (15, 1)))
                    for el in range(4):
                        x = el // 2 if kind == "p" else el
                        c, h = (el % 2, 2 * i + el // 2) if kind == "p" else (2, 4 * i + el)
                        dve.wait_ge(*at("gc", (n, x)))
                        ins = dve.tensor_scalar(un["p"][0:size, el, 0:size], GCS[0:size, 2 * u + x, c * P:c * P + size],
                                                tokens3[0:size, c, T_GC, h:h + 1], 0.0, ALU.subtract, ALU.min)
                    ins.then_inc(*to("g_diff", n))
                    dve.wait_ge(*at("g_decay", n))
                    dve.wait_ge(*at("kq_done", n))
                    kq = of(("kq", n))
                    def both(o):
                        if kind == "p":
                            return kq[:, o:o + 256].rearrange("p (c t) -> p c t", c=2).unsqueeze(1).broadcast_to([P, 2, 2, P])
                        return kq[0:64, o:o + 128].rearrange("p (q t) -> p q t", q=2).unsqueeze(2).broadcast_to([64, 2, 2, 64])
                    four = lambda v: v[0:size, :, 0:size].rearrange("p (a b) t -> p a b t", a=2)
                    if kind == "s":
                        mask = const("gincl_s")[0:64]
                    else:
                        mask = const("gincl")
                    dve.tensor_tensor(four(un["am"]), both(0), four(un["p"]), ALU.mult)
                    dve.tensor_tensor(four(un["aq"]), both(256), four(un["p"]), ALU.mult).then_inc(*to("kq_read", n))
                    dve.wait_ge(*at("kq_read", n))
                    for x in range(2 if kind == "p" else 4):
                        dve.wait_ge(*at("bb", (n, x)))
                    if kind == "p":
                        beta = BS[:, 2 * u:2 * u + 2, 0:SEQ].rearrange("p x (c t) -> p x c t", c=2)
                    else:
                        beta = BS[0:64, :, SEQ:NT].rearrange("p (a b) t -> p a b t", a=2)
                    dve.tensor_tensor(four(un["am"]), four(un["am"]), beta, ALU.mult)
                    dve.tensor_tensor(un["aq"][0:size, :, 0:size], un["aq"][0:size, :, 0:size],
                                      mask.unsqueeze(1).broadcast_to([size, 4, size]), ALU.mult).then_inc(*to("g_aq", n))
                    dve.wait_ge(*at("g_aq", n))
                    dve.tensor_scalar(un["am"][0:size, :, 0:size], un["am"][0:size, :, 0:size], -1.0, None, ALU.mult)\
                       .then_inc(*to("g_am", n))
                    if kind == "p":
                        for x in range(2):
                            dve.tensor_tensor(QG[:, 2 * u + x, P:SEQ], QKV[:, i, P:SEQ], EG[:, 2 * u + x, P:SEQ], ALU.mult)\
                               .then_inc(*to("qg", (n, x)))
                for lev in g_levels(kind):
                    for n, _, u, _, _ in members:
                        un = GUNIT[u]
                        inv = un["inv"][0:size].rearrange("p a (x t) -> p a x t", x=2)[:, :, :, 0:size]
                        if lev == 0:
                            idb = ident[0:size, 0:size].unsqueeze(1).broadcast_to([size, 4, size])
                            dve.wait_ge(*at("gpmm", (n, 0)))
                            dve.tensor_tensor(inv[:, :, 0], of(("gp", n, 0))[0:size, :].rearrange("p (a b) -> p a b", a=4)
                                              [:, :, 0:size], idb, ALU.add)
                            dve.tensor_tensor(inv[:, :, 1], un["off"][0:size, :, 0:size], idb, ALU.add)\
                               .then_inc(*to("ginv", (n, 0)))
                        else:
                            dve.wait_ge(*at("ginv", (n, lev - 1)))
                            for g in range(2):
                                dve.wait_ge(*at("gimm", (n, lev, g)))
                                src = of(("gimm", n, lev, g))[0:size, :].rearrange("p (a x t) -> p a x t", a=2, x=2)
                                ins = dve.tensor_tensor(inv[:, 2 * g:2 * g + 2], inv[:, 2 * g:2 * g + 2],
                                                        src[:, :, :, 0:size], ALU.add)
                            ins.then_inc(*to("ginv", (n, lev)))
                if kind == "p":
                    for c in range(2):
                        if c:
                            for n, _, u, _, i in members:
                                for x in range(2):
                                    h, s = 2 * i + x, 2 * u + x
                                    dve.wait_ge(*at("ks_done", h))
                                    dve.wait_ge(*at("g_nbe", 0))
                                    dve.scalar_tensor_tensor(out=GR[:, s, :], in0=of(("ks", h))[:, 0:P],
                                                             scalar=tokens3[:, 1, T_NBE, h:h + 1],
                                                             in1=GUNIT[u]["vb"][:, 2 * x + 1, :], op0=ALU.mult, op1=ALU.add)\
                                       .then_inc(*to("g_rhs", h))
                        for n, _, u, _, i in members:
                            for x in range(2):
                                h, s = 2 * i + x, 2 * u + x
                                dve.wait_ge(*at("g_mu", (h, c)))
                                if c == 0:
                                    if r:
                                        dve.wait_ge(*at(f"gps_stored{s}", h - 4))
                                    ins = dve.tensor_copy(GS[:, s, :], of(("gmu", h, c))[:, 0:P])
                                else:
                                    ins = dve.scalar_tensor_tensor(out=GS[:, s, :], in0=GS[:, s, :],
                                                                   scalar=EG[:, s, SEQ - 1:SEQ], in1=of(("gmu", h, c))[:, 0:P],
                                                                   op0=ALU.mult, op1=ALU.add)
                                ins.then_inc(*to("g_state", (h, c)))
                else:
                    i = members[0][4]
                    for el in range(4):
                        h = 4 * i + el
                        dve.wait_ge(*at("gks_done", h))
                        dve.scalar_tensor_tensor(out=GR[0:64, 0, :], in0=of(("gks", h))[0:64, 0:P],
                                                 scalar=tokens3[0:64, 2, T_NBE, h:h + 1], in1=GUNIT[0]["vb"][0:64, el, :],
                                                 op0=ALU.mult, op1=ALU.add).then_inc(*to("gs_rhs", h))
                        S = SGS[h % 2]
                        for g in range(2):
                            part = S[:, 4 * g:4 * g + 4, :]
                            gl = EG[:, el, SEQ + 7 + 32 * g:SEQ + 32 * g + 32:8].unsqueeze(2).broadcast_to([P, 4, P])
                            if g == 0:
                                dve.wait_ge(*at("gz_done", h))
                            dve.tensor_tensor(part, part, gl, ALU.mult).then_inc(*to("gs_scaled", (h, g)))
                        for g in range(2):
                            part = S[:, 4 * g:4 * g + 4, :]
                            dve.wait_ge(*at("gs_scaled", (h, g)))
                            dve.wait_ge(*at("gs_mm", (h, g)))
                            dve.tensor_tensor(part, part, of(("gsm", h, g)).rearrange("p (b v) -> p b v", b=4), ALU.add)\
                               .then_inc(*to("gs_new", (h, g)))
            for h in range(16):
                t = PS[:, h % 2, :]
                dve.wait_ge(*at("gn_rstd", h))
                dve.scalar_tensor_tensor(out=t, in0=QKV[:, 16 + h, :], scalar=par("gdn_norm_w", 0), in1=RS[:, 1, :],
                                         op0=ALU.mult, op1=ALU.mult).then_inc(*to("g_n1", h))
                dve.wait_ge(*at("g_n1", h))
                dve.tensor_tensor(Z[:, h, :], t, Z[:, h, :], ALU.mult).then_inc(*to("g_gated", h))
            dve.wait_ge(*at("g_gated", 15))
            dve_post_norm(dve, gq + 1)

        def pool_gdn(pool, l):
            pool.wait_ge(*at("rstd", gq))
            pool.memset(XG[:, :, 0:3], 0.0)
            for t in range(32):
                if t >= 4:
                    pool.wait_ge(*at("gconv", t - 4))
                st = gdn_state[:, :].rearrange("p (b j m) -> p b j m", b=DEC, j=3)[:, :, :, t]
                pool.tensor_copy(g_window(t % 4)[:, :, 0:3], st).then_inc(*to("gxp_state", t))
                pool.wait_ge(*at("gxp", t))
                pool.tensor_copy(tailg_p[:, :, t], XG[:, t % 4, 256:259])
                pool.tensor_copy(tailg_s[:, :, :, t], g_window(t % 4)[:, :, 8:11]).then_inc(*to("gtail", t))
            for r, members in enumerate(g_in_round):
                kind = members[0][3]
                size = P if kind == "p" else 64
                for lev in g_levels(kind):
                    for n, _, u, _, _ in members:
                        un = GUNIT[u]
                        pool.wait_ge(*at("g_am", n))
                        if lev:
                            pool.wait_ge(*at("gpmm", (n, lev - 1)))
                            if lev == 1:
                                pool.wait_ge(*at("ginv", (n, 0)))
                        pool.tensor_tensor(un["off"][0:size, :, 0:size], un["am"][0:size, :, 0:size],
                                           const(f"lev{lev}")[0:size, 0:size].unsqueeze(1).broadcast_to([size, 4, size]),
                                           ALU.mult).then_inc(*to("goff", (n, lev)))
                if kind == "s":
                    i = members[0][4]
                    for el in range(4):
                        h = 4 * i + el
                        if h == 0:
                            pool.wait_ge(*at("g_mu", (15, 1)))
                            pool.wait_ge(*at("g_state", (15, 1)))
                            for k in range(2):
                                pool.dma_start(SGS[k], io["state_gdn_S"][0, :, k].rearrange("b k v -> k b v"))\
                                    .then_inc(*to(f"gs_in{k}", k, 16))
                        if h >= 1:
                            pool.wait_ge(*at("gz_done", h - 1))
                        kq = QKV[:, 8 + h // 2, SEQ:NT], QKV[:, h // 2, SEQ:NT]
                        pool.wait_ge(*at("gc", (members[0][0], el)))
                        pool.tensor_copy(KQ[:, :, 0, :], sample(kq[0]))
                        pool.tensor_tensor(KQ[:, :, 1, :], sample(kq[1]), sample(EG[:, el, SEQ:NT]), ALU.mult)\
                            .then_inc(*to("kq8", h))
                        pool.wait_ge(*at("gs_vn", h))
                        if h:
                            pool.wait_ge(*at("gs_mm", (h - 1, 1)))
                        pool.tensor_tensor(VNM[0:64], GV[0:64, 0, :].unsqueeze(1).broadcast_to([64, DEC, P]),
                                           const("batch8")[0:64].unsqueeze(2).broadcast_to([64, DEC, P]), ALU.mult)\
                            .then_inc(*to("vnm", h))
                        pool.wait_ge(*at("gs_new", (h, 1)))
                        pool.dma_start(io["s_gdn_S"][0, :, h].rearrange("b k v -> k b v"), SGS[h % 2])\
                            .then_inc(*to(f"gs_out{h % 2}", h, 16))
                        if h + 2 < 16:
                            pool.wait_ge(*at(f"gs_out{h % 2}", h))
                            pool.dma_start(SGS[h % 2], io["state_gdn_S"][0, :, h + 2].rearrange("b k v -> k b v"))\
                                .then_inc(*to(f"gs_in{h % 2}", h + 2, 16))

        ma = {"n": 0}

        def take(*dims):
            o = ma["n"]
            ma["n"] += int(np.prod(dims))
            return arena(o, *dims)

        CM = take(MLA_CONST.shape[1])

        def mla_const(name, a=0, b=None):
            off, n = MLA_CONST_AT[name]
            return CM[:, off + a:off + (n if b is None else b)]

        LT = take(2, NT)
        KR = take(NT)
        o_qn = ma["n"]
        QN = take(8, NT)
        OLS = arena(o_qn, 2, MH, 64)
        QR = take(4, NT)
        QLS = take(2, DEC, P)
        QRS = take(DEC, P)
        CTOK = take(3, LAT + ROPE)
        VT = take(8, NT)
        o_r1 = ma["n"]
        CQ = take(4, NT)
        UKT = take(8, LAT)
        PSB = arena(o_r1, PAGE * PAGES + 64)
        OL = arena(o_r1 + PAGE * PAGES + 64, LAT)
        o_r2 = ma["n"]
        VTOK = take(2, D)
        PPR = take(2, 384)
        PTP = take(2, 384)
        RT = arena(o_r2 + 2 * D, 2, NT)
        PTS = arena(o_r2, 17, P)
        PGS = take(2, PAGES, LAT)
        PGR = take(2, PAGES * ROPE)
        KN = H[:, :, :].rearrange("p m t -> p (m t)")[:, 0:8 * SEQ].rearrange("p (a t) -> p a t", a=8)
        CTB = [halves[1][:, 0:1024], SMALL[:, 0:1024]]
        RTB = [halves[0][:, 0:512], SMALL[:, 1024:1536]]
        MSUM = SMALL[:, 1536:1544].rearrange("p (s n) -> p s n", s=2)
        MMAX = SMALL[:, 1544:1552].rearrange("p (s n) -> p s n", s=2)
        SMX, SSM, SNM, SRC = SMALL[:, 1552:1557], SMALL[:, 1560:1565], SMALL[:, 1568:1570], SMALL[:, 1572:1574]
        mq = 4
        NPAST = PAGE * PAGES
        min_tiles = [(m // 2, m % 2) for m in range(6)]

        def mla_events():
            yield "turn", 0
            for n in range(4 * DEC):
                if n % 4:
                    yield "turn", n + 1 if n < 4 * DEC - 1 else None
                elif n == 0:
                    yield "turn", 1
                yield "score", n
                if n % 4 == 3:
                    yield "new", n // 4
                    yield "turn", n + 2 if n + 2 < 4 * DEC else None
                    yield "values", n // 4

        def mla_order():
            done = set()
            for kind, n in mla_events():
                if n is None or (kind, n) in done or kind == "turn" and n >= 4 * DEC:
                    continue
                done.add((kind, n))
                yield kind, n

        def sp_pages(sp, b):
            if b == 0:
                sp.wait_ge(*at("rstd", mq))
                sp.wait_ge(*at("pages_in", 0))
            if b >= 2:
                sp.wait_ge(*at("s_values", b - 2))
            for j in range(PAGES):
                i = b * PAGES + j
                page = sp.value_load(PG[0:1, i:i + 1], min_val=0, max_val=POOL - 1)
                sp.dma_start(PGS[:, b % 2, j, :], io["cache_mla_latent"][0][bass.ds(page, 1), :, :]
                             .rearrange("a p c -> (a p) c")).then_inc(*to(f"page{b % 2}", b, 16))
                sp.dma_start(PGR[:, b % 2, j * ROPE:(j + 1) * ROPE], io["cache_mla_krope"][0][bass.ds(page, 1), :, :]
                             .rearrange("a p c -> (a p) c")).then_inc(*to(f"page{b % 2}", b, 16))

        def pe_mla(pe, l):
            pe_norm(pe, mq)
            for m in range(7):
                key = ("min", m // 2)
                w = W[:, weight(pe, key), :]
                ps = bank(pe, ("min", m), ("min_raw", m))
                for k in range(MT):
                    if m == 0:
                        pe.wait_ge(*at("h", (mq, k)))
                    if m < 6:
                        lhsT = w[:, k * 256 + (m % 2) * P:k * 256 + (m % 2) * P + P]
                    else:
                        lhsT = w[:, k * P:k * P + P]
                    ins = mm(pe, ps[:, 0:NT], lhsT, H[:, k, :], k == 0, k == 7)
                ins.then_inc(*to("min_done", m))
                weight_used[key] = ("min_done", m)
            ps = bank(pe, ("ln", "q"), ("mla_ln", "q"))
            for m in range(4):
                pe.wait_ge(*at("mla_sq", m))
                mm(pe, ps[:, 0:NT], ones, SQ[:, m % 4, :], m == 0, m == 3).then_inc(*to("mla_summed", m))
            ps = bank(pe, ("ln", "c"), ("mla_ln", "c"))
            for m in range(4, 6):
                pe.wait_ge(*at("mla_sq", m))
                mm(pe, ps[:, 0:NT], ones, SQ[:, m % 4, :], m == 4, m == 5).then_inc(*to("mla_summed", m))
            ps = bank(pe, ("swap", "k"), ("rot_s", "k"))
            pe.wait_ge(*at("const_mla", 0))
            pe.wait_ge(*at("min_raw", 6))
            mm(pe, ps[:, 0:NT], mla_const("swap"), KR, True, True).then_inc(*to("swapped", "k"))
            for c in range(4):
                w = W[:, weight(pe, ("qb", c)), :]
                for j in range(3):
                    ps = bank(pe, ("q", c, j), ("q_raw", (c, j)))
                    for k in range(4):
                        if c == 0 and j == 0:
                            pe.wait_ge(*at("cq", k))
                        lhsT = w[:, k * 384 + j * P:k * 384 + j * P + P]
                        ins = mm(pe, ps[:, 0:NT], lhsT, CQ[:, k, :], k == 0, k == 3)
                    ins.then_inc(*to("q_done", (c, j)))
                weight_used[("qb", c)] = ("q_done", (c, 2))
            for c in range(4):
                ps = bank(pe, ("swap", c), ("rot_s", c))
                pe.wait_ge(*at("q_raw", (c, 2)))
                mm(pe, ps[:, 0:NT], mla_const("swap"), QR[:, c, :], True, True).then_inc(*to("swapped", c))
            w = W[:, weight(pe, ("uk",)), :]
            for g in range(4):
                ps = bank(pe, ("kn", g), ("kn", g))
                for j in range(2):
                    a = 2 * g + j
                    for ct in range(2):
                        if g == 0 and j == 0:
                            pe.wait_ge(*at("c", ct))
                        ins = mm(pe, ps[:, j * SEQ:(j + 1) * SEQ], w[:, ct * D + a * P:ct * D + a * P + P],
                                 LT[:, ct, 0:SEQ], ct == 0, ct == 1)
                ins.then_inc(*to("kn_done", g))
            for g in range(4):
                ps = bank(pe, ("ukt", g), ("ukt", g))
                for j in range(2):
                    for ct in range(2):
                        a = 2 * g + j
                        ins = pe.transpose(ps[:, j * 256 + ct * P:j * 256 + ct * P + P],
                                           w[:, ct * D + a * P:ct * D + a * P + P], ident)
                ins.then_inc(*to("ukt_done", g))
            weight_used[("uk",)] = ("ukt_done", 3)
            for t in range(3):
                n = P if t < 2 else 64
                ps = bank(pe, ("ctok", t), ("ctok", t))
                for ct in range(2):
                    pe.transpose(ps[0:n, ct * P:ct * P + P], LT[:, ct, t * P:t * P + n], ident)
                if t == 0:
                    pe.wait_ge(*at("rot", "k"))
                pe.transpose(ps[0:n, 256:288], KR[0:32, t * P:t * P + n], ident[0:32, 0:32]).then_inc(*to("ctok_done", t))
            w = W[:, weight(pe, ("uv",)), :]
            for t in range(2):
                for g in range(2):
                    ps = bank(pe, ("v", t, g), ("vtok", (t, g)))
                    for ct in range(2):
                        ins = mm(pe, ps[:, :], LT[:, ct, t * P:t * P + P], w[:, ct * D + g * 512:ct * D + g * 512 + 512],
                                 ct == 0, ct == 1)
                    ins.then_inc(*to("v_done", (t, g)))
            for g in range(4):
                ps = bank(pe, ("ql", g), ("ql", g))
                if g == 0:
                    pe.wait_ge(*at("ukt", 3))
                for j in range(4):
                    h = 8 * (g // 2) + 2 * j + g % 2
                    rows = slice(64 * (h % 2), 64 * (h % 2) + 64)
                    pe.wait_ge(*at("q_raw", (h // 4, (h // 2) % 2)))
                    for ct in range(2):
                        ins = mm(pe, ps[:, j * P + ct * 64:j * P + ct * 64 + 64], UKT[rows, h // 2, ct * P:ct * P + P],
                                 QN[rows, h // 2, SEQ:NT], True, True)
                ins.then_inc(*to("ql_done", g))
            for g in range(2):
                ps = bank(pe, ("qrs", g), ("qrs", g))
                for j in range(8):
                    h = 8 * g + j
                    if h % 4 == 0:
                        pe.wait_ge(*at("rot", h // 4))
                    sel = mla_const("spread", P * (h % 4), P * (h % 4) + P)
                    ins = mm(pe, ps[:, j * 64:j * 64 + 64], sel, QR[:, h // 4, SEQ:NT], True, True)
                ins.then_inc(*to("qrs_done", g))
            for i in range(MH + 2):
                if i < MH:
                    h = i
                    ps = bank(pe, ("ps", h), ("p_exp", h))
                    if h == 0:
                        pe.wait_ge(*at("kn", 3))
                    nope, rot = slice(64 * (h % 2), 64 * (h % 2) + 64), slice(32 * (h % 4), 32 * (h % 4) + 32)
                    for qb, cols in ((0, slice(0, P)), (1, slice(P, 384))):
                        qs = slice(qb * P, qb * P + P)
                        ks = slice(0, P * (qb + 1))
                        mm(pe, ps[:, cols], QN[nope, h // 2, qs], KN[nope, h // 2, ks], True, False)
                        ins = mm(pe, ps[:, cols], QR[rot, h // 4, qs], KR[rot, ks], False, True)
                    ins.then_inc(*to("ps_done", h))
                if 1 <= i <= MH:
                    h = i - 1
                    ps = bank(pe, ("pt", h), ("pt", h))
                    pe.wait_ge(*at("p_norm", h))
                    for j in range(3):
                        ins = pe.transpose(ps[:, j * P:j * P + P], PPR[:, h % 2, j * P:j * P + P], ident)
                    ins.then_inc(*to("pt_done", h))
                if i >= 2:
                    h = i - 2
                    if h % 2 == 0:
                        ps_v = bank(pe, ("po", h // 2), ("po", h // 2))
                    rows = slice(64 * (h % 2), 64 * (h % 2) + 64)
                    if h == 0:
                        pe.wait_ge(*at("vtok", (1, 1)))
                    pe.wait_ge(*at("pt", h))
                    mm(pe, ps_v[rows, 0:SEQ], VTOK[:, 0, h * 64:h * 64 + 64], PTP[:, h % 2, 0:SEQ], True, False)
                    mm(pe, ps_v[rows, P:SEQ], VTOK[:, 1, h * 64:h * 64 + 64], PTP[:, h % 2, SEQ:384], False, True)\
                        .then_inc(*to("po_done", h))
            moving = {"n": 0}

            def moving_bank(key, *read_by):
                moving["n"] += 1
                return bank(pe, key, *read_by, which=5 + moving["n"] % 3)

            pe.wait_ge(*at("ql", 3))
            pe.wait_ge(*at("qrs", 1))
            pe.wait_ge(*at("ctok", 2))
            for kind, n in mla_order():
                b, g = divmod(n, 4) if kind in ("turn", "score") else (n, 0)
                cT = CTB[n % 2]
                if kind == "turn":
                    if g == 0:
                        pe.wait_ge(*at(f"page{b % 2}", b))
                    for ct in range(2):
                        ps = moving_bank(("turn", n, ct), ("c_turned_a" if ct == 0 else "c_turned", (n, ct)))
                        for j in range(4):
                            ins = pe.transpose(ps[:, j * P:j * P + P], PGS[:, b % 2, 4 * g + j, ct * P:ct * P + P], ident)
                        ins.then_inc(*to("turn_done", (n, ct)))
                    ps = moving_bank(("turn", n, 2), ("c_turned", (n, 2)))
                    pe.transpose(ps[:, 0:P], PGR[:, b % 2, g * P:g * P + P], ident).then_inc(*to("turn_done", (n, 2)))
                elif kind == "score":
                    ps = bank(pe, ("score", b, g), ("s_exp", (b, g)), which=g)
                    for ct in range(2):
                        pe.wait_ge(*at("c_turned_a" if ct == 0 else "c_turned", (n, ct)))
                        mm(pe, ps, QLS[:, ct, b, :], cT[:, ct * 512:ct * 512 + 512], ct == 0, False)
                    pe.wait_ge(*at("c_turned", (n, 2)))
                    mm(pe, ps, QRS[:, b, :], RTB[n % 2], False, True).then_inc(*to("score_done", (b, g)))
                elif kind == "new":
                    ps = bank(pe, ("score", b, 4), ("s_exp", (b, 4)), which=4)
                    for ct in range(2):
                        mm(pe, ps[:, 0:64], QLS[:, ct, b, :], LT[:, ct, SEQ:NT], ct == 0, False)
                    mm(pe, ps[:, 0:64], QRS[0:32, b, :], KR[0:32, SEQ:NT], False, True).then_inc(*to("score_done", (b, 4)))
                else:
                    for g in range(5):
                        ps = moving_bank(("sp", b, g), (sp_name(g), (b, g)))
                        pe.wait_ge(*at("s_exp", (b, g)))
                        if g < 4:
                            for j in range(4):
                                k = 4 * g + j
                                ins = pe.transpose(ps[:, j * P:j * P + P], PSB[:, k * P:k * P + P], ident)
                        else:
                            ins = pe.transpose(ps[0:64, 0:P], PSB[:, NPAST:NPAST + 64], ident)
                        ins.then_inc(*to("sp_done", (b, g)))
                    ps = bank(pe, ("so", b), ("s_out", b), which=4)
                    for k in range(PAGES):
                        if k % 4 == 0:
                            pe.wait_ge(*at(sp_name(k // 4), (b, k // 4)))
                        mm(pe, ps[:, 0:LAT], PTS[:, k, :], PGS[:, b % 2, k, :], k == 0, False)
                    pe.wait_ge(*at(sp_name(4), (b, 4)))
                    mm(pe, ps[:, 0:LAT], PTS[0:64, 16, :], CTOK[0:64, 2, 0:LAT], False, True).then_inc(*to("s_values", b))
                    ps = moving_bank(("ol", b), ("ol_turned", b))
                    pe.wait_ge(*at("s_out", b))
                    for ct in range(2):
                        ins = pe.transpose(ps[:, ct * P:ct * P + P], OL[:, ct * P:ct * P + P], ident)
                    ins.then_inc(*to("ol_done", b))
            ps = bank(pe, ("vs", 0), ("vs", 0))
            pe.wait_ge(*at("ol_turned", 7))
            w = W[:, where[("uv",)] % NS, :]
            for h in range(MH):
                rows = slice(64 * (h % 2), 64 * (h % 2) + 64)
                for ct in range(2):
                    ins = mm(pe, ps[rows, (h // 2) * 64:(h // 2) * 64 + 64], w[:, ct * D + h * 64:ct * D + h * 64 + 64],
                             OLS[:, ct, h, :], ct == 0, ct == 1)
            ins.then_inc(*to("vs_done", 0))
            weight_used[("uv",)] = ("vs_done", 0)
            pe_out(pe, mq + 1, [[("wo", l, c)] for c in range(4)], 8, lambda n: [("po", n), ("vs", 0)], lambda n: VT[:, n, :])
            pe_norm(pe, mq + 1)

        def sp_name(g):
            return "sp_turned" if g % 2 == 0 else "sp_turned_d"

        def act_mla(act, l):
            act.dma_start(CM, io["const_mla"]).then_inc(*to("const_mla", 0, 16))
            act_pre_norm(act, mq)
            for m in range(7):
                act.wait_ge(*at("min_done", m))
                src = of(("min", m))[:, 0:NT]
                dst = CQ[:, m, :] if m < 4 else LT[:, m - 4, :] if m < 6 else KR
                if m < 6:
                    act_square(act, m, src, ("mla_sq", m), lambda n: ("mla_summed", n), count=6)
                act.activation(dst, src, ACT.Copy).then_inc(*to("min_raw", m))
                for name, last, count, r in (("q", 3, 512, RS), ("c", 5, 256, PS)):
                    if m == last:
                        act.wait_ge(*at("mla_summed", last))
                        act.activation(r[:, 0, :], of(("ln", name))[:, 0:NT], ACT.Ln, bias=EB[:, 0:1], scale=1.0 / count)\
                           .then_inc(*to("mla_ln", name))
                        act.wait_ge(*at("mla_ln", name))
                        act.activation(r[:, 1, :], r[:, 0, :], ACT.Exp, scale=-0.5).then_inc(*to("mla_rstd", name))
            for c in range(4):
                for j in range(3):
                    act.wait_ge(*at("q_done", (c, j)))
                    dst = QN[:, 2 * c + j, :] if j < 2 else QR[:, c, :]
                    act.activation(dst, of(("q", c, j))[:, 0:NT], ACT.Copy).then_inc(*to("q_raw", (c, j)))
            for g in range(4):
                act.wait_ge(*at("kn_done", g))
                act.activation(KN[:, 2 * g:2 * g + 2, :], of(("kn", g)).rearrange("p (a t) -> p a t", a=2), ACT.Copy)\
                   .then_inc(*to("kn", g))
            for g in range(4):
                act.wait_ge(*at("ukt_done", g))
                act.activation(UKT[:, 2 * g:2 * g + 2, :], of(("ukt", g)).rearrange("p (a t) -> p a t", a=2), ACT.Copy)\
                   .then_inc(*to("ukt", g))
            for t in range(3):
                n = P if t < 2 else 64
                act.wait_ge(*at("ctok_done", t))
                act.activation(CTOK[0:n, t, :], of(("ctok", t))[0:n, 0:288], ACT.Copy).then_inc(*to("ctok", t))
            act.wait_ge(*at("ctok", 2))
            for part, (a, b) in enumerate(((0, LAT), (LAT, LAT + ROPE))):
                name = ("mla_latent", "mla_krope")[part]
                act.dma_start(io["p_" + name][0, 0].rearrange("(c t) f -> t c f", c=2), CTOK[:, 0:2, a:b])\
                   .then_inc(*to("mla_stored", l, 16))
                act.dma_start(io["s_" + name][0].rearrange("b s f -> (b s) f"), CTOK[0:64, 2, a:b])\
                   .then_inc(*to("mla_stored", l, 16))
            for t in range(2):
                for g in range(2):
                    act.wait_ge(*at("v_done", (t, g)))
                    if (t, g) == (0, 0):
                        act.wait_ge(*at("rot", 3))
                    act.activation(VTOK[:, t, g * 512:(g + 1) * 512], of(("v", t, g)), ACT.Copy).then_inc(*to("vtok", (t, g)))
            for g in range(4):
                act.wait_ge(*at("ql_done", g))
                src = of(("ql", g)).rearrange("p (h c b s) -> p h c b s", h=4, c=2, b=DEC)
                for ct in range(2):
                    h0 = 8 * (g // 2) + g % 2
                    dst = QLS[:, ct].rearrange("p b (h s) -> p h b s", h=MH)[:, h0:min(h0 + 8, MH):2]
                    ins = act.activation(dst, src[:, :, ct], ACT.Copy)
                ins.then_inc(*to("ql", g))
            for g in range(2):
                act.wait_ge(*at("qrs_done", g))
                dst = QRS.rearrange("p b (h s) -> p h b s", h=MH)[:, 8 * g:8 * g + 8]
                act.activation(dst, of(("qrs", g)).rearrange("p (h b s) -> p h b s", h=8, b=DEC), ACT.Copy)\
                   .then_inc(*to("qrs", g))
            for i in range(MH + 2):
                if i < MH:
                    h = i
                    act.wait_ge(*at("p_max", h))
                    if h >= 2:
                        act.wait_ge(*at("pt_done", h - 2))
                        act.wait_ge(*at("p_norm", h - 2))
                    for qb, cols in ((0, slice(0, P)), (1, slice(P, 384))):
                        ins = act.activation(PPR[:, h % 2, cols], of(("ps", h))[:, cols], ACT.Exp, bias=MMAX[:, h % 2, 2 + qb:3 + qb],
                                             scale=SCALE, accum_out=MSUM[:, h % 2, qb:qb + 1])
                    ins.then_inc(*to("p_exp", h))
                if 1 <= i <= MH:
                    h = i - 1
                    act.wait_ge(*at("pt_done", h))
                    if h >= 2:
                        act.wait_ge(*at("po_done", h - 2))
                    ps = of(("pt", h))[:, 0:384]
                    act.activation(PTP[:, h % 2, 0:P], ps[:, 0:P], ACT.Copy)
                    act.activation(PTP[:, h % 2, P:384], ps[:, P:384], ACT.Copy).then_inc(*to("pt", h))
                if i >= 2 and i % 2:
                    a = (i - 2) // 2
                    act.wait_ge(*at("po_done", i - 2))
                    act.activation(VT[:, a, 0:SEQ], of(("po", a))[:, 0:SEQ], ACT.Copy).then_inc(*to("po", a))
            for kind, n in mla_order():
                if kind == "turn":
                    act.wait_ge(*at("turn_done", (n, 0)))
                    if n >= 2:
                        act.wait_ge(*at("score_done", divmod(n - 2, 4)))
                    act.activation(CTB[n % 2][:, 0:512], of(("turn", n, 0)), ACT.Copy).then_inc(*to("c_turned_a", (n, 0)))
                elif kind == "new":
                    b = n
                    act.wait_ge(*at("s_max", b))
                    for g in range(5):
                        if b:
                            act.wait_ge(*at("sp_done", (b - 1, g)))
                            act.wait_ge(*at("s_rec", b - 1))
                        w = 512 if g < 4 else 64
                        act.activation(PSB[:, g * 512:g * 512 + w], of(("score", b, g))[:, 0:w], ACT.Exp, bias=SNM[:, 1:2],
                                       scale=SCALE, accum_out=SSM[:, g:g + 1]).then_inc(*to("s_exp", (b, g)))
                elif kind == "values":
                    b = n
                    for g in (0, 2, 4):
                        act.wait_ge(*at("sp_done", (b, g)))
                        if b:
                            act.wait_ge(*at("s_values", b - 1))
                        if g < 4:
                            act.activation(PTS[:, 4 * g:4 * g + 4, :].rearrange("p a t -> p (a t)"), of(("sp", b, g)), ACT.Copy)\
                               .then_inc(*to("sp_turned", (b, g)))
                        else:
                            act.activation(PTS[0:64, 16, :], of(("sp", b, g))[0:64, 0:P], ACT.Copy).then_inc(*to("sp_turned", (b, g)))
                    act.wait_ge(*at("ol_done", b))
                    dst = OLS.rearrange("p c h (b s) -> p c h b s", b=DEC)[:, :, :, b, :]
                    act.activation(dst, of(("ol", b))[:, 0:LAT].rearrange("p (c h s) -> p c h s", c=2, h=MH), ACT.Copy)\
                       .then_inc(*to("ol_turned", b))
            act.wait_ge(*at("vs_done", 0))
            act.activation(VT[:, :, SEQ:NT], of(("vs", 0)).rearrange("p (a t) -> p a t", a=8), ACT.Copy).then_inc(*to("vs", 0))
            act_outputs(act, mq + 1, ("mla_stored", l))

        def dve_mla(dve, l):
            dve_pre_norm(dve, mq)
            for m in range(6):
                name, r = ("q", RS) if m < 4 else ("c", PS)
                x = CQ[:, m, :] if m < 4 else LT[:, m - 4, :]
                dve.wait_ge(*at("min_raw", m))
                dve.wait_ge(*at("mla_rstd", name))
                dve.scalar_tensor_tensor(out=x, in0=x, scalar=par("mla_q_norm", m) if m < 4 else par("mla_kv_norm", m - 4),
                                         in1=r[:, 1, :], op0=ALU.mult, op1=ALU.mult)\
                   .then_inc(*(to("cq", m) if m < 4 else to("c", m - 4)))
            for n, key in enumerate(("k", 0, 1, 2, 3)):
                x = KR if key == "k" else QR[:, key, :]
                if n == 0:
                    dve.wait_ge(*at("const_mla", 0))
                dve.wait_ge(*at("swapped", key))
                if n >= 2:
                    dve.wait_ge(*at("rot", (None, "k", 0, 1, 2)[n - 1]))
                dve.tensor_tensor(RT[:, n % 2, :], of(("swap", key))[:, 0:NT], mla_const("sin"), ALU.mult).then_inc(*to("rot_s", key))
                dve.tensor_tensor(x, x, mla_const("cos"), ALU.mult).then_inc(*to("rot_c", key))
                dve.wait_ge(*at("rot_c", key))
                dve.tensor_tensor(x, x, RT[:, n % 2, :], ALU.add).then_inc(*to("rot", key))
            causal = mla_const("causal")
            for i in range(MH + 1):
                if i < MH:
                    h = i
                    dve.wait_ge(*at("ps_done", h))
                    ps = of(("ps", h))
                    diag = ps[:, 0:512].rearrange("p (a t) -> p a t", a=4)[:, 0:3:2, :]
                    dve.tensor_tensor(diag, diag, causal.unsqueeze(1).broadcast_to([P, 2, P]), ALU.add).then_inc(*to("p_masked", h))
                    dve.wait_ge(*at("p_masked", h))
                    if h >= 2:
                        dve.wait_ge(*at("p_exp", h - 2))
                    s = h % 2
                    dve.tensor_reduce(MMAX[:, s, 0:1], ps[:, 0:P], AX.X, ALU.max)
                    dve.tensor_reduce(MMAX[:, s, 1:2], ps[:, P:384], AX.X, ALU.max).then_inc(*to("p_maxr", h))
                    dve.wait_ge(*at("p_maxr", h))
                    dve.tensor_scalar(MMAX[:, s, 2:4], MMAX[:, s, 0:2], -SCALE, None, ALU.mult).then_inc(*to("p_max", h))
                if i:
                    h = i - 1
                    s = h % 2
                    dve.wait_ge(*at("p_exp", h))
                    dve.reciprocal(MSUM[:, s, 2:4], MSUM[:, s, 0:2]).then_inc(*to("p_rec", h))
                    dve.wait_ge(*at("p_rec", h))
                    dve.tensor_scalar(PPR[:, s, 0:P], PPR[:, s, 0:P], MSUM[:, s, 2:3], None, ALU.mult)
                    dve.tensor_scalar(PPR[:, s, P:384], PPR[:, s, P:384], MSUM[:, s, 3:4], None, ALU.mult)\
                       .then_inc(*to("p_norm", h))
            causal8 = mla_const("causal8")
            for kind, n in mla_order():
                if kind == "turn":
                    if n >= 2:
                        dve.wait_ge(*at("score_done", divmod(n - 2, 4)))
                    dve.wait_ge(*at("turn_done", (n, 1)))
                    dve.tensor_copy(CTB[n % 2][:, 512:1024], of(("turn", n, 1))).then_inc(*to("c_turned", (n, 1)))
                    dve.wait_ge(*at("turn_done", (n, 2)))
                    dve.tensor_tensor(RTB[n % 2].rearrange("p (j t) -> p j t", j=4),
                                      of(("turn", n, 2))[:, 0:P].unsqueeze(1).broadcast_to([P, 4, P]),
                                      mla_const("group4").unsqueeze(2).broadcast_to([P, 4, P]), ALU.mult)\
                       .then_inc(*to("c_turned", (n, 2)))
                elif kind == "score":
                    b, g = divmod(n, 4)
                    dve.wait_ge(*at("score_done", (b, g)))
                    if b and g == 0:
                        dve.wait_ge(*at("s_max", b - 1))
                    dve.tensor_reduce(SMX[:, g:g + 1], of(("score", b, g)), AX.X, ALU.max).then_inc(*to("s_gmax", (b, g)))
                elif kind == "new":
                    b = n
                    ps = of(("score", b, 4))[:, 0:64]
                    dve.wait_ge(*at("score_done", (b, 4)))
                    dve.tensor_tensor(ps, ps, causal8[:, 56 - 8 * b:120 - 8 * b], ALU.add).then_inc(*to("s_masked", b))
                    dve.wait_ge(*at("s_masked", b))
                    dve.tensor_reduce(SMX[:, 4:5], ps, AX.X, ALU.max).then_inc(*to("s_gmax", (b, 4)))
                    dve.wait_ge(*at("s_gmax", (b, 4)))
                    if b:
                        dve.wait_ge(*at("s_exp", (b - 1, 4)))
                    dve.tensor_reduce(SNM[:, 0:1], SMX, AX.X, ALU.max).then_inc(*to("s_maxr", b))
                    dve.wait_ge(*at("s_maxr", b))
                    dve.tensor_scalar(SNM[:, 1:2], SNM[:, 0:1], -SCALE, None, ALU.mult).then_inc(*to("s_max", b))
                else:
                    b = n
                    for g in (1, 3):
                        dve.wait_ge(*at("sp_done", (b, g)))
                        if b:
                            dve.wait_ge(*at("s_values", b - 1))
                        dve.tensor_copy(PTS[:, 4 * g:4 * g + 4, :].rearrange("p a t -> p (a t)"), of(("sp", b, g)))\
                           .then_inc(*to("sp_turned_d", (b, g)))
                    dve.wait_ge(*at("s_exp", (b, 4)))
                    if b:
                        dve.wait_ge(*at("s_out", b - 1))
                    dve.tensor_reduce(SRC[:, 0:1], SSM, AX.X, ALU.add).then_inc(*to("s_sum", b))
                    dve.wait_ge(*at("s_sum", b))
                    dve.reciprocal(SRC[:, 1:2], SRC[:, 0:1]).then_inc(*to("s_rec", b))
                    dve.wait_ge(*at("s_rec", b))
                    dve.wait_ge(*at("s_values", b))
                    if b:
                        dve.wait_ge(*at("ol_done", b - 1))
                    dve.tensor_scalar(OL, of(("so", b))[:, 0:LAT], SRC[:, 1:2], None, ALU.mult).then_inc(*to("s_out", b))
            dve_post_norm(dve, mq + 1)

        def pool_mla(pool, l):
            pass

        block_ = ctx.enter_context(nc.Block())
        mixer_of = lambda l: "rwkv" if l in rw_of else "mla" if l == 1 else "gdn"

        @block_.tensor
        def _(pe):
            pe_prologue(pe)
            for l in range(layers):
                (pe_rwkv if l in rw_of else pe_mla if l == 1 else pe_gdn)(pe, l)
                pe_ffn(pe, l)
            pe_final(pe)

        @block_.sync
        def _(sp):
            sp_prologue(sp)
            for i, (key, loads) in enumerate(plan):
                if i >= NS:
                    sp.wait_ge(*at(*weight_used[plan[i - NS][0]]))
                for dst, src in loads:
                    sp.dma_start(dst, src).then_inc(*to(f"slot{i % NS}", key, 16))
                if key in (("qb", 0), ("wo", 1, 0)):
                    for b in range(2) if key[0] == "qb" else range(2, DEC):
                        sp_pages(sp, b)

        @block_.scalar
        def _(act):
            act.preload_act_table_set("natural_log_exp_and_others")
            act_loads(act)
            for l in range(layers):
                (act_rwkv if l in rw_of else act_mla if l == 1 else act_gdn)(act, l)
                act_ffn(act, l)
            act_final(act)

        @block_.vector
        def _(dve):
            dve_prologue(dve)
            for l in range(layers):
                (dve_rwkv if l in rw_of else dve_mla if l == 1 else dve_gdn)(dve, l)
                dve_ffn(dve, l)

        @block_.gpsimd
        def _(pool):
            for l in range(layers):
                if mixer_of(l) == "rwkv":
                    pool_rwkv_chunks(pool, l)
                elif mixer_of(l) == "mla":
                    pool_mla(pool, l)
                else:
                    pool_gdn(pool, l)
                pool_ffn(pool, l)

    return sig.found


INPUTS = ["x_prompt", "x_sample", "state_rwkv_wkv", "state_rwkv_shift", "cache_mla_latent", "cache_mla_krope",
          "state_gdn_S", "state_gdn_conv", "state_ffn_conv", "page_table", "norm_w", "rw_mu", "rw_wrkv", "rw_w0",
          "rw_w1", "rw_w2", "rw_a0", "rw_a1", "rw_a2", "rw_v0", "rw_v1", "rw_v2", "rw_g1", "rw_g2", "rw_kk",
          "rw_ka", "rw_rk", "rw_lnx_w", "rw_lnx_b", "rw_wo", "mla_w_in", "mla_q_norm", "mla_kv_norm", "mla_w_qb",
          "mla_w_uk", "mla_w_uv", "mla_wo", "gdn_w_in", "gdn_conv_w", "gdn_a_log", "gdn_dt_bias", "gdn_norm_w",
          "gdn_wo", "ffn_w_up", "ffn_conv_w", "ffn_conv_b", "ffn_w_down"]
OUTPUTS = [("y_prompt", (1, SEQ, D)), ("y_sample", (DEC, STEPS, D)),
           ("p_rwkv_wkv", (2, 1, 16, 64, 64)), ("p_rwkv_shift", (2, 1, D)), ("p_mla_latent", (1, 1, SEQ, LAT)),
           ("p_mla_krope", (1, 1, SEQ, ROPE)), ("p_gdn_S", (1, 1, GH, P, P)), ("p_gdn_conv", (1, 1, 3, 4096)),
           ("p_ffn_conv", (DEPTH, 1, 2, 2 * DFF)),
           ("s_rwkv_wkv", (2, DEC, 16, 64, 64)), ("s_rwkv_shift", (2, DEC, D)), ("s_mla_latent", (1, DEC, STEPS, LAT)),
           ("s_mla_krope", (1, DEC, STEPS, ROPE)), ("s_gdn_S", (1, DEC, GH, P, P)), ("s_gdn_conv", (1, DEC, 3, 4096)),
           ("s_ffn_conv", (DEPTH, DEC, 2, 2 * DFF))]
LAYERS = DEPTH


def declare(nc, arrays):
    io = {name: nc.dram_tensor(name, a.shape, mybir.dt.from_np(a.dtype), kind="ExternalInput").ap()
          for name, a in arrays.items()}
    for name, shape in OUTPUTS:
        io[name] = nc.dram_tensor("out_" + name, shape, F32, kind="ExternalOutput").ap()
    io["ffn_state_t"] = nc.dram_tensor("ffn_state_t", (P, DEPTH * 704), F32, kind="Internal").ap()
    io["v_first"] = nc.dram_tensor("v_first", (P, BLK), F32, kind="Internal").ap()
    return io


def kernel(**inputs):
    import concourse.bacc as bacc
    from concourse.bass_utils import run_bass_kernel_spmd

    arrays = {name: np.ascontiguousarray(inputs[name]) for name in INPUTS}
    arrays["const"] = CONST
    arrays["const_mla"] = MLA_CONST
    counted = bacc.Bacc("TRN2", target_bir_lowering=False, num_devices=1)
    values = build(counted, declare(counted, arrays), None, LAYERS)
    nc = bacc.Bacc("TRN2", target_bir_lowering=False, num_devices=1)
    build(nc, declare(nc, arrays), values, LAYERS)
    result = run_bass_kernel_spmd(nc, [arrays], core_ids=[0]).results[0]
    return tuple(result["out_" + name] for name, _ in OUTPUTS)
```

```python
from contextlib import ExitStack

import numpy as np
import concourse.bass as bass
from concourse import mybir

F32 = mybir.dt.float32
I32 = mybir.dt.int32
ALU = mybir.AluOpType
ACT = mybir.ActivationFunctionType
AX = mybir.AxisListType

P = 128
D, SEQ, DEC, STEPS = 1024, 256, 8, 8
DEPTH, DFF = 4, 2816
NT = SEQ + DEC * STEPS
MT = D // P
FT = DFF // P
BLK = MT * NT
NS = 4
SLOT = 2048
EPS = 1e-6
LNX_EPS = 64e-5
C64 = 64
PAGE, PAGES, LAT, ROPE = 128, 16, 256, 32
POOL = 160
MH, NOPE = 16, 64
SCALE = (NOPE + ROPE) ** -0.5
GH, GQK = 16, 8
NEG = -1e30


def constants():
    i = np.arange(P)
    cols = {}
    cols["ident"] = np.eye(P)
    cols["ones"] = np.ones((P, P))
    cols["onesB"] = np.kron(np.eye(2), np.ones((64, 64)))
    cols["mean64"] = cols["onesB"] / 64.0
    sw = np.zeros((P, P))
    for b in range(0, P, ROPE):
        for r in range(ROPE // 2):
            sw[b + 16 + r, b + r] = -1.0
            sw[b + r, b + 16 + r] = 1.0
    cols["swap"] = sw
    cols["spread"] = np.concatenate([np.tile(np.eye(P)[:, 32 * j:32 * j + 32], (1, 4)) for j in range(4)], 1)
    cols["group4"] = (i[:, None] // 32) == np.arange(4)[None, :]
    for lev in range(7):
        w = 2 ** lev
        same = (i[:, None] // (2 * w)) == (i[None, :] // (2 * w))
        cols[f"lev{lev}"] = same & ((i[:, None] // w) % 2 == 0) & ((i[None, :] // w) % 2 == 1)
    j, t = i[:, None], i[None, :]
    t64 = np.arange(64)[None, :]
    for name, w in (("p", 64), ("s", 8)):
        strict = (j < t) & (j // w == t // w) & (j // 64 == t // 64)
        incl = ((j % 64) <= t64) & ((j % 64) // w == t64 // w)
        cols["amask_" + name] = np.concatenate([strict, incl, strict, incl], 1)
    cols["gincl"] = j <= t
    cols["gincl_s"] = np.where(j < 64, (j <= t64) & (j // 8 == t64 // 8), 0)
    cols["causal"] = np.where(t <= j, 0.0, NEG)
    c8 = np.full((P, 120), NEG)
    c8[:, 56:64] = np.where(np.arange(8)[None, :] <= (j % 8), 0.0, NEG)
    cols["causal8"] = c8
    seg = np.ones(NT)
    seg[0:SEQ:C64] = 0
    seg[SEQ::8] = 0
    cols["seg64"] = np.tile(seg, (P, 1))
    seg = np.ones(NT)
    seg[0:SEQ:P] = 0
    seg[SEQ::8] = 0
    cols["seg128"] = np.tile(seg, (P, 1))
    pos = np.concatenate([np.arange(SEQ), np.tile(PAGE * PAGES + np.arange(8), 8)]).astype(np.float32)
    inv = (np.float32(10000.0) ** (-np.arange(16, dtype=np.float32) / np.float32(16))).astype(np.float32)
    ang = (pos[None, :] * inv[(i % 16)][:, None]).astype(np.float32)
    cols["cos"] = np.cos(ang)
    cols["sin"] = np.sin(ang)
    cols["batch8"] = (i[:, None] % 64) // 8 == np.arange(8)[None, :]
    cols["half"] = (i[:, None] // 64) == np.arange(2)[None, :]
    tables = []
    for mla in (False, True):
        at, out, off = {}, [], 0
        for k, v in cols.items():
            if (k in ("swap", "spread", "group4", "causal", "causal8", "cos", "sin")) == mla:
                v = np.asarray(v, np.float32)
                at[k] = (off, v.shape[1])
                off += v.shape[1]
                out.append(v)
        tables += [at, np.ascontiguousarray(np.concatenate(out, 1))]
    return tables


CONST_AT, CONST, MLA_CONST_AT, MLA_CONST = constants()
NCONST = CONST.shape[1]

PARAM_ROWS = [("norm_w", 128), ("rw_mu", 96), ("rw_w0", 16), ("rw_a0", 16), ("rw_kk", 16), ("rw_ka", 16),
              ("rw_rk", 16), ("rw_lnx_w", 16), ("rw_lnx_b", 16), ("rw_v0", 8), ("mla_q_norm", 4),
              ("mla_kv_norm", 2), ("gdn_norm_w", 1), ("gdn_conv_w", 128), ("ffn_conv_w", 528), ("ffn_conv_b", 176)]
PARAM_AT, _n = {}, 0
for _name, _rows in PARAM_ROWS:
    PARAM_AT[_name] = _n
    _n += _rows
NPARAM = _n



SHARED = {
    "products": "out_done half_done rkv_done lora1_done lora2_done up_done min_done q_done kn_done v_done ql_done qrs_done "
                "swapped gin_done vs_done",
    "turned": "pro_turned tail_turned shift_turned y_turned gtail_turned tok_turned ukt_done ctok_done",
    "sums": "kk_summed bonus_summed ymean yvar mla_summed l2_summed go_summed sq_summed",
    "rwkv_inverse_products": "amm pmm imm",
    "rwkv_chunk_products": "tv_done rhs_done sa_done y_done ymm pstate_turned",
    "rwkv_sample_products": "sin_turned z_done smm sout_turned",
    "gdn_inverse_products": "gpmm gimm kq_done gc_done bb_done",
    "gdn_turned": "vt_done kt_done",
    "gdn_chunk_products": "ks_done vn_done go_done g_mu",
    "gdn_sample_products": "gks_done gvn_done gso_done gs_mm",
    "prompt_attention_products": "ps_done pt_done po_done",
    "sample_attention_products": "turn_done score_done sp_done s_values ol_done",
    "norm_rstd": "rstd_ln rstd",
    "squares": "sq kk_sq y_sq mla_sq l2_sq go_sq",
    "rows_copied": "tail_rows shift_rows gtail_rows y_rows",
    "products_copied": "rkv lora_copied lora2_out q_raw min_raw kn ukt ctok vtok ql qrs z_out vs",
    "head_rstd": "kk_ln kk_rstd y_ln y_rstd l2_ln l2_rstd gn_ln gn_rstd mla_ln mla_rstd",
    "decays": "decay_prev decay decay_inv",
    "rwkv_chunk_copies": "tv p rhs sa mg pstate",
    "rwkv_sample_copies": "z_zero m0 z sout",
    "gdn_gates": "gtap3 g_1e exp_alog g_e1 g_sp g_e",
    "gdn_copies": "tok gc bb vt kt g_decay gp",
    "gdn_chunk_copies": "vn go gs_vn gs_o",
    "prompt_attention_copies": "p_exp pt po",
    "sample_attention_copies": "c_turned_a s_exp sp_turned ol_turned",
    "prologue": "pro_copied eps params2",
    "rwkv_mix": "shift_kept dx_run dx",
    "lora": "mid_sum mid_recip lora_mid",
    "log_decays": "sig_sum log_decay log_sum log_prev",
    "rwkv_values": "v_diff v_part v_mixed",
    "rwkv_keys": "kkr k_gain k_mod rk kk b a_decayed a_scaled prepared",
    "group_norm": "bonus_v y_centered y1 y2 y3 y_gated",
    "rwkv_chunk_sums": "am inv y state m_sum m_new",
    "ffn_taps": "tap1 tap2 conv",
    "ffn_gate": "gate_d gate_gu gate_r hff",
    "residual": "x post",
    "gdn_taps": "gtap1 gtap2 gconv",
    "gdn_silu": "g_sig g_silu z_add z_rec z_1e",
    "gdn_rows": "g_abs g_r g_t g_rows g_nbe",
    "gdn_inverse": "g_diff kq_read g_am1 g_aq g_am qg ginv",
    "gdn_states": "g_rhs g_state gs_rhs gs_z gs_scaled gs_new",
    "gdn_scaled": "g_n1 g_gated qk_normed",
    "mla_scaled": "cq c rot rot_c rot_s",
    "prompt_softmax": "p_masked p_max p_maxr p_rec p_norm",
    "sample_softmax": "c_turned s_gmax s_masked s_maxr s_max sp_turned_d s_sum s_rec s_out",
}
SEMAPHORE_OF = {step: name for name, steps in SHARED.items() for step in steps.split()}


class Signals:

    def __init__(self, nc, ctx, values):
        self.nc, self.ctx, self.values = nc, ctx, values
        self.sems, self.count, self.found = {}, {}, {}

    def sem(self, name):
        if name not in self.sems:
            self.sems[name] = self.ctx.enter_context(self.nc.semaphore(name))
        return self.sems[name]

    def to(self, name, step, n=1):
        sem = SEMAPHORE_OF.get(name, name)
        self.count[sem] = self.count.get(sem, 0) + n
        self.found[name, step] = self.count[sem]
        return self.sem(sem), n

    def at(self, name, step):
        return self.sem(SEMAPHORE_OF.get(name, name)), (self.values[name, step] if self.values else 1)


def build(nc, io, values, layers=DEPTH):
    ctx = ExitStack()
    with ctx:
        sig = Signals(nc, ctx, values)
        to, at = sig.to, sig.at

        def sb(name, shape, dt=F32):
            return ctx.enter_context(nc.sbuf_tensor(name, shape, dt))

        psum = [ctx.enter_context(nc.psum_tensor(f"bank{b}", [P, 512], F32)) for b in range(8)]

        C = sb("consts", [P, NCONST])
        PT = sb("params", [P, NPARAM])
        PX = sb("param_products", [P, 64])
        AH = sb("head_rows", [16, 4])
        EB = sb("eps_cols", [P, 8])
        ffn_state = sb("ffn_state", [P, 16 * 44])
        gdn_state = sb("gdn_state", [P, 24 * 32])
        shift_state = sb("shift_state", [P, P])
        X = sb("x", [P, MT, NT])
        H = sb("h", [P, MT, NT])
        W = sb("weights", [P, NS, SLOT])
        SQ = sb("squares", [P, 4, NT])
        RS = sb("rstd", [P, 2, NT])
        PS = sb("post_scaled", [P, 2, NT])
        SMALL = sb("small", [P, 1936])
        PG = sb("pages", [1, DEC * PAGES], I32)
        AR = (nc.sbuf_usable_end - nc.sbuf_base) // 4 - 32
        A = sb("arena", [P, AR])

        def const(name, a=0, b=None):
            off, n = CONST_AT[name]
            return C[:, off + a:off + (n if b is None else b)]

        def par(name, i):
            return PT[:, PARAM_AT[name] + i:PARAM_AT[name] + i + 1]

        def block(i):
            return A[:, i * BLK:(i + 1) * BLK].rearrange("p (m t) -> p m t", m=MT)

        def flat(i):
            return A[:, i * BLK:(i + 1) * BLK]

        def arena(off, *dims):
            n = int(np.prod(dims))
            assert off + n <= AR, (off, n, AR)
            ap = A[:, off:off + n]
            if len(dims) == 2:
                ap = ap.rearrange("p (a b) -> p a b", a=dims[0])
            if len(dims) == 3:
                ap = ap.rearrange("p (a b c) -> p a b c", a=dims[0], b=dims[1])
            if len(dims) == 4:
                ap = ap.rearrange("p (a b c d) -> p a b c d", a=dims[0], b=dims[1], c=dims[2])
            return ap

        ident, ones, onesB, mean64 = const("ident"), const("ones"), const("onesB"), const("mean64")

        NW0, NA0, NV0, OMKA = 0, 16, 32, 40
        rw_of = {0: 0, 3: 1}

        plan = []

        def slot_view(i, k, n):
            return W[:, i % NS, 0:k * n].rearrange("p (k n) -> p k n", k=k)

        def add_weight(key, w, k, n0, n1, k0=0):
            i = len(plan)
            src = w[k0 * P:(k0 + k) * P, n0:n1].rearrange("(k p) n -> p k n", p=P)
            plan.append((key, [(slot_view(i, k, n1 - n0), src)]))

        def add_rows(key, parts):
            i = len(plan)
            loads, off = [], 0
            for src in parts:
                r, n = src.shape
                loads.append((W[0:r, i % NS, off:off + n], src))
                off += n
            plan.append((key, loads))

        for l in range(layers):
            if l in rw_of:
                ri = rw_of[l]
                def add_projection(i, columns):
                    for c in columns:
                        add_weight(("rkv", l, i, c), io["rw_wrkv"][ri, i], 8, c * 256, c * 256 + 256)

                add_weight(("w1", l), io["rw_w1"][ri], 8, 0, 64)
                add_weight(("a1", l), io["rw_a1"][ri], 8, 0, 64)
                add_weight(("g1", l), io["rw_g1"][ri], 8, 0, 160)
                add_rows(("w2", l), [io["rw_w2"][ri]])
                add_rows(("a2", l), [io["rw_a2"][ri]])
                add_rows(("g2", l), [io["rw_g2"][ri, 0:P], io["rw_g2"][ri, P:160]])
                add_projection(2, range(4))
                if ri:
                    add_weight(("v1", l), io["rw_v1"][0], 8, 0, 32)
                add_projection(1, range(1))
                if ri:
                    add_rows(("v2", l), [io["rw_v2"][0]])
                add_projection(1, range(1, 4))
                add_projection(0, range(4))
                for c in range(4):
                    add_weight(("wo", l, c), io["rw_wo"][ri], 8, c * 256, c * 256 + 256)
            elif l == 1:
                for c in range(3):
                    add_weight(("min", c), io["mla_w_in"][0], 8, c * 256, c * 256 + 256)
                src = io["mla_w_in"][0][:, 768:800].rearrange("(k p) n -> p k n", p=P)
                plan.append((("min", 3), [(slot_view(len(plan), 8, P)[:, :, 32 * j:32 * j + 32], src) for j in range(4)]))
                for c in range(4):
                    dst, loads = slot_view(len(plan), 4, 384), []
                    for k in range(4):
                        src = io["mla_w_qb"][0][k * P:(k + 1) * P, c * 384:c * 384 + 384].rearrange("p (h n) -> p h n", h=4)
                        loads.append((dst[:, k, 0:256].rearrange("p (h n) -> p h n", h=4), src[:, :, 0:NOPE]))
                        loads.append((dst[:, k, 256:384].rearrange("p (h n) -> p h n", h=4), src[:, :, NOPE:NOPE + ROPE]))
                    plan.append((("qb", c), loads))
                add_weight(("uk",), io["mla_w_uk"][0].rearrange("c h n -> c (h n)"), 2, 0, 1024)
                add_weight(("uv",), io["mla_w_uv"][0].rearrange("c h n -> c (h n)"), 2, 0, 1024)
                for c in range(4):
                    add_weight(("wo", l, c), io["mla_wo"][0], 8, c * 256, c * 256 + 256)
            else:
                for c in range(24):
                    add_weight(("gin", c), io["gdn_w_in"][0], 8, c * 256, c * 256 + 256)
                add_weight(("gin", 24), io["gdn_w_in"][0], 8, 6144, 6176)
                for c in range(8):
                    add_weight(("gwo", c), io["gdn_wo"][0], 16, c * P, c * P + P)
            for c in range(11):
                for half in range(2):
                    add_weight(("up", l, half, c), io["ffn_w_up"][l], 8, half * DFF + c * 256, half * DFF + c * 256 + 256)
            for m in range(MT):
                for kk in range(2):
                    add_weight(("down", l, m, kk), io["ffn_w_down"][l], 11, m * P, m * P + P, k0=kk * 11)
        where = {key: i for i, (key, _) in enumerate(plan)}
        weight_used = {}

        banks = {"n": 0, "free": [[] for _ in range(8)], "of": {}}

        def bank(pe, key, *read_by, which=None):
            b = banks["n"] % 8 if which is None else which
            banks["n"] += which is None
            for step in banks["free"][b]:
                pe.wait_ge(*at(*step))
            banks["free"][b] = read_by
            banks["of"][key] = b
            return psum[b][:, :]

        def of(key):
            return psum[banks["of"][key]][:, :]

        def mm(pe, out, lhsT, rhs, first, last):
            return pe.matmul(out, lhsT, rhs, start=first, stop=last, skip_group_check=True)

        def sample(ap3):
            return ap3.rearrange("p (b s) -> p b s", b=DEC)

        def x_step(q, m):
            return ("x", (-1, 4)) if q == 0 else ("x", (q - 1, m))

        def pe_norm(pe, q):
            ps = bank(pe, ("norm", q), ("rstd_ln", q))
            if q % 2:
                pe.wait_ge(*at("added", (q, 6)))
                mm(pe, ps[:, 0:NT], ones, RS[:, 0, :], True, False)
                pe.wait_ge(*at("sq", (q, 7)))
                mm(pe, ps[:, 0:NT], ones, SQ[:, 3, :], False, True).then_inc(*to("sq_summed", (q, 7)))
                return
            for m in range(MT):
                pe.wait_ge(*at("sq", (q, m)))
                mm(pe, ps[:, 0:NT], ones, SQ[:, m % 4, :], m == 0, m == 7).then_inc(*to("sq_summed", (q, m)))

        def pool_squares(pool, q):
            pool.wait_ge(*at("sq", (q, 0)))
            for m in range(1, 7):
                pool.wait_ge(*at("sq", (q, m)))
                if m > 1:
                    pool.wait_ge(*at("added", (q, m - 1)))
                pool.tensor_tensor(RS[:, 0, :], SQ[:, 0, :] if m == 1 else RS[:, 0, :], SQ[:, m % 4, :], ALU.add)\
                    .then_inc(*to("added", (q, m)))

        squares = {"last": None}

        def act_square(act, m, src, made, summed, count=MT):
            last = summed(m - 4) if m >= 4 else squares["last"]
            if last is not None:
                act.wait_ge(*at(*last))
            act.activation(SQ[:, m % 4, :], src, ACT.Square).then_inc(*to(*made))
            if m == count - 1:
                squares["last"] = summed(m)

        def act_rstd(act, q, scale):
            act.wait_ge(*at("sq_summed", (q, 7)))
            act.activation(RS[:, 0, :], of(("norm", q))[:, 0:NT], ACT.Ln, bias=EB[:, 0:1], scale=scale)\
               .then_inc(*to("rstd_ln", q))
            act.wait_ge(*at("rstd_ln", q))
            act.activation(RS[:, 1, :], RS[:, 0, :], ACT.Exp, scale=-0.5).then_inc(*to("rstd", q))

        def act_pre_norm(act, q):
            for m in range(MT):
                act.wait_ge(*at(*x_step(q, m)))
                act_square(act, m, X[:, m, :], ("sq", (q, m)), lambda n: ("sq_summed", (q, n)))
            if q == 0:
                act.wait_ge(*at("eps", 0))
            act_rstd(act, q, 1.0 / D)

        def dve_pre_norm(dve, q):
            dve.wait_ge(*at("rstd", q))
            for m in range(MT):
                dve.scalar_tensor_tensor(out=H[:, m, :], in0=X[:, m, :], scalar=par("norm_w", q * 8 + m),
                                         in1=RS[:, 1, :], op0=ALU.mult, op1=ALU.mult).then_inc(*to("h", (q, m)))

        def act_outputs(act, q, stored=None):
            for m in range(MT):
                act.wait_ge(*at("out_done", (q, m)))
                act_square(act, m, of(("out", q, m))[:, 0:NT], ("sq", (q, m)),
                           lambda n: ("added", (q, max(n, 1))) if n < 7 else ("sq_summed", (q, 7)))
                act.activation(H[:, m, :], of(("out", q, m))[:, 0:NT], ACT.Copy).then_inc(*to("out", (q, m)))
            if stored:
                act.wait_ge(*at(*stored))
            act_rstd(act, q, 1.0 / D)

        def dve_post_norm(dve, q):
            dve.wait_ge(*at("rstd", q))
            for m in range(MT):
                dve.wait_ge(*at("out", (q, m)))
                dve.scalar_tensor_tensor(out=PS[:, m % 2, :], in0=H[:, m, :], scalar=par("norm_w", q * 8 + m),
                                         in1=RS[:, 1, :], op0=ALU.mult, op1=ALU.mult).then_inc(*to("post", (q, m)))
                dve.wait_ge(*at("post", (q, m)))
                dve.tensor_tensor(X[:, m, :], X[:, m, :], PS[:, m % 2, :], ALU.add).then_inc(*to("x", (q, m)))

        def weight(pe, key):
            i = where[key]
            pe.wait_ge(*at(f"slot{i % NS}", key))
            return i % NS

        def pe_out(pe, q, keys, k, ready, rhs):
            for c, slot_keys in enumerate(keys):
                two = len(slot_keys) == 1 and k == 8
                for j in range(2 if two else 1):
                    m = 2 * c + j if two else c
                    ps = bank(pe, ("out", q, m), ("out", (q, m)))
                    n, total = 0, k * len(slot_keys)
                    for key in slot_keys:
                        w = W[:, weight(pe, key), :]
                        for kt in range(k):
                            if c == 0 and j == 0:
                                for step in ready(n):
                                    pe.wait_ge(*at(*step))
                            width = 256 if two else P
                            ins = mm(pe, ps[:, 0:NT], w[:, kt * width + j * P:kt * width + j * P + P], rhs(n),
                                     n == 0, n == total - 1)
                            n += 1
                            if kt == k - 1 and key != slot_keys[-1]:
                                ins.then_inc(*to("half_done", (q, m)))
                                weight_used[key] = ("half_done", (q, m))
                    ins.then_inc(*to("out_done", (q, m)))
                    weight_used[slot_keys[-1]] = ("out_done", (q, m))

        HFF = arena(0, FT, NT)
        CV0 = FT * NT
        CONV = arena(CV0, 2, 2, 336)
        CT = arena(CV0 + 4 * 336, 2, 336)
        EGATE = arena(CV0 + 6 * 336, 2, 336)
        GD = arena(CV0 + 8 * 336, 3, 336)
        XP = arena(CV0 + 11 * 336, 4, 344)
        TAIL = arena(CV0 + 11 * 336 + 4 * 344, 792)
        TOUT = arena(CV0 + 11 * 336 + 4 * 344 + 792, 7, P)
        tail_p = TAIL[:, 0:88].rearrange("p (j m) -> p j m", j=2)
        tail_s = TAIL[:, 88:792].rearrange("p (b j m) -> p b j m", b=DEC, j=2)

        def ffn_tiles():
            for c in range(11):
                for half in range(2):
                    for j in range(2):
                        yield c, half, j, 2 * c + j

        def pe_ffn(pe, l):
            q = 4 * l + 2
            pe_norm(pe, q)
            for c, half, j, m in ffn_tiles():
                key = ("up", l, half, c)
                w = W[:, weight(pe, key), :]
                ps = bank(pe, ("up", l, half, m), ("xp", (l, half, m)))
                for k in range(MT):
                    if (c, half, j) == (0, 0, 0):
                        pe.wait_ge(*at("h", (q, k)))
                    ins = mm(pe, ps[:, 0:NT], w[:, k * 256 + j * P:k * 256 + j * P + P], H[:, k, :], k == 0, k == 7)
                ins.then_inc(*to("up_done", (l, half, m)))
                weight_used[key] = ("up_done", (l, half, m))
            for g, (first, n) in enumerate([(0, 4), (4, 3)]):
                ps = bank(pe, ("tail", l, g), ("tail_rows", (l, g)))
                for i in range(first, first + n):
                    a, b = (0, 88) if i == 0 else (88 + (i - 1) * P, min(88 + i * P, 792))
                    if i == 0:
                        pe.wait_ge(*at("tail", (l, 1, FT - 1)))
                    ins = pe.transpose(ps[0:b - a, (i - first) * P:(i - first + 1) * P], TAIL[:, a:b], ident)
                ins.then_inc(*to("tail_turned", (l, g)))
            pe_out(pe, q + 1, [[("down", l, m, 0), ("down", l, m, 1)] for m in range(MT)], 11,
                   lambda n: [("hff", (l, n))], lambda n: HFF[:, n, :])
            pe_norm(pe, q + 1)

        def act_ffn(act, l):
            q = 4 * l + 2
            if l:
                act.wait_ge(*at("tail", (l - 1, 1, FT - 1)))
            else:
                act.wait_ge(*at("ffn_state_t", 0))
            act.dma_start(ffn_state[:, :], io["ffn_state_t"][:, l * 704:(l + 1) * 704])\
               .then_inc(*to("ffn_state_in", l, 16))
            act_pre_norm(act, q)
            for n, (c, half, j, m) in enumerate(ffn_tiles()):
                for step in conv_users(l, n):
                    act.wait_ge(*at(*step))
                act.wait_ge(*at("up_done", (l, half, m)))
                ps = of(("up", l, half, m))
                act.activation(XP[:, n % 4, 2:258], ps[:, 0:SEQ], ACT.Copy)
                act.activation(sample_window(n % 4)[:, :, 2:10], sample(ps[:, SEQ:NT]), ACT.Copy)\
                   .then_inc(*to("xp", (l, half, m)))
                if half == 1:
                    act.wait_ge(*at("conv", (l, 0, m)))
                    if m >= 2:
                        act.wait_ge(*at("gate_d", (l, m - 2)))
                    act.activation(EGATE[:, m % 2, :], CONV[:, 0, m % 2, :], ACT.Exp, scale=-1.0).then_inc(*to("gate_e", (l, m)))
            for g, n in ((0, 4), (1, 3)):
                act.wait_ge(*at("tail_turned", (l, g)))
                act.activation(TOUT[:, 4 * g:4 * g + n, :], of(("tail", l, g))[:, 0:n * P], ACT.Copy)\
                   .then_inc(*to("tail_rows", (l, g)))
            act.wait_ge(*at("tail_rows", (l, 1)))
            rows = io["p_ffn_conv"][l, 0].rearrange("j (m p) -> (j m) p", p=P)
            act.dma_start(rows, TOUT[0:88, 0, :]).then_inc(*to("tail_stored", l, 16))
            rows = io["s_ffn_conv"][l].rearrange("b j (m p) -> (b j m) p", p=P)
            for i in range(6):
                r = min(P, 704 - i * P)
                act.dma_start(rows[i * P:i * P + r, :], TOUT[0:r, 1 + i, :]).then_inc(*to("tail_stored", l, 16))
            act_outputs(act, q + 1, ("tail_stored", l))

        def sample_window(s):
            return XP[:, s, 258:338].rearrange("p (b w) -> p b w", b=DEC)

        order = list(ffn_tiles())

        def conv_users(l, n):
            if n >= 4:
                c, half, j, m = order[n - 4]
                return [("conv", (l, half, m)), ("tail", (l, half, m))]
            return []

        def pool_ffn(pool, l):
            pool.wait_ge(*at("rstd", 4 * l + 2))
            pool.memset(XP[:, :, 0:2], 0.0)
            for n, (c, half, j, m) in enumerate(order):
                for step in conv_users(l, n):
                    pool.wait_ge(*at(*step))
                m2 = half * FT + m
                st = ffn_state[:, :].rearrange("p (b j m) -> p b j m", b=DEC, j=2)[:, :, :, m2]
                if n == 0:
                    pool.wait_ge(*at("ffn_state_in", l))
                pool.tensor_copy(sample_window(n % 4)[:, :, 0:2], st).then_inc(*to("xp_state", (l, half, m)))
                pool.wait_ge(*at("xp", (l, half, m)))
                pool.tensor_copy(tail_p[:, :, m2], XP[:, n % 4, 256:258])
                pool.tensor_copy(tail_s[:, :, :, m2], sample_window(n % 4)[:, :, 8:10]).then_inc(*to("tail", (l, half, m)))

        def dve_ffn(dve, l):
            q = 4 * l + 2
            dve_pre_norm(dve, q)

            def gate(m):
                g, u = CONV[:, 0, m % 2, :], CONV[:, 1, m % 2, :]
                dve.wait_ge(*at("gate_e", (l, m)))
                if m:
                    dve.wait_ge(*at("hff", (l, m - 1)))
                dve.tensor_scalar(GD[:, 0, :], EGATE[:, m % 2, :], 1.0, None, ALU.add).then_inc(*to("gate_d", (l, m)))
                dve.wait_ge(*at("conv", (l, 1, m)))
                dve.tensor_tensor(GD[:, 2, :], g, u, ALU.mult).then_inc(*to("gate_gu", (l, m)))
                dve.wait_ge(*at("gate_d", (l, m)))
                dve.reciprocal(GD[:, 1, :], GD[:, 0, :]).then_inc(*to("gate_r", (l, m)))
                dve.wait_ge(*at("gate_r", (l, m)))
                dve.tensor_tensor(HFF[:, m, 0:SEQ], GD[:, 2, 0:SEQ], GD[:, 1, 0:SEQ], ALU.mult)
                win = [GD[:, i, 256:336].rearrange("p (b w) -> p b w", b=DEC)[:, :, 2:10] for i in (2, 1)]
                dve.tensor_tensor(sample(HFF[:, m, SEQ:NT]), win[0], win[1], ALU.mult).then_inc(*to("hff", (l, m)))

            for n, (c, half, j, m) in enumerate(order):
                w = lambda tap: par("ffn_conv_w", (l * 3 + tap) * 44 + half * FT + m)
                dve.wait_ge(*at("xp", (l, half, m)))
                dve.wait_ge(*at("xp_state", (l, half, m)))
                if half == 0 and m >= 2:
                    dve.wait_ge(*at("gate_e", (l, m - 2)))
                dve.tensor_scalar(CT[:, 0, :], XP[:, n % 4, 2:338], w(2), par("ffn_conv_b", l * 44 + half * FT + m),
                                  ALU.mult, ALU.add).then_inc(*to("tap2", (l, half, m)))
                dve.wait_ge(*at("tap2", (l, half, m)))
                if n:
                    dve.wait_ge(*at("conv", (l, order[n - 1][1], order[n - 1][3])))
                dve.scalar_tensor_tensor(out=CT[:, 1, :], in0=XP[:, n % 4, 1:337], scalar=w(1), in1=CT[:, 0, :],
                                         op0=ALU.mult, op1=ALU.add).then_inc(*to("tap1", (l, half, m)))
                dve.wait_ge(*at("tap1", (l, half, m)))
                dve.scalar_tensor_tensor(out=CONV[:, half, m % 2, :], in0=XP[:, n % 4, 0:336], scalar=w(0),
                                         in1=CT[:, 1, :], op0=ALU.mult, op1=ALU.add).then_inc(*to("conv", (l, half, m)))
                if half == 1 and j == 1:
                    gate(m - 1)
                    gate(m)
            dve_post_norm(dve, q + 1)

        stage_x = arena(0, 20, P)
        stage_state = arena(20 * P, 29, P)
        stage_par = arena(49 * P, 10, P)
        n_state = 22 + 6 + 1
        turns = [("x", i) for i in range(20)] + [("par", i) for i in range(10)] + [("state", i) for i in range(n_state)]
        groups = [turns[i:i + 4] for i in range(0, 20, 4)] + [turns[i:min(i + 4, 30)] for i in range(20, 30, 4)] + \
                 [turns[i:i + 4] for i in range(30, len(turns), 4)]

        def param_segments():
            row = 0
            for name, n in PARAM_ROWS:
                done = 0
                while done < n:
                    r = min(n - done, P - row % P)
                    yield name, done, r, row // P, row % P
                    done += r
                    row += r

        def stored_rows(name):
            ap = io[name]
            names = " ".join("abcd"[:len(ap.shape)])
            flat_ap = ap.rearrange(f"{names} -> ({names})")
            return flat_ap.rearrange("(r p) -> r p", p=P)

        def sp_prologue(sp):
            sp.dma_start(stage_x[:, 0:16, :], io["x_prompt"].rearrange("o t (m p) -> (o t m) p", p=P)
                         .rearrange("(i r) p -> r i p", r=P)).then_inc(*to("x_in", 0, 16))
            sp.dma_start(stage_x[:, 16:20, :], io["x_sample"].rearrange("o t (m p) -> (o t m) p", p=P)
                         .rearrange("(i r) p -> r i p", r=P)).then_inc(*to("x_in", 0, 16))

        def act_loads(act):
            act.dma_start(C[:, :], io["const"]).then_inc(*to("const_in", 0, 16))
            for name, first, r, tile, p0 in param_segments():
                act.dma_start(stage_par[p0:p0 + r, tile, :], stored_rows(name)[first:first + r, :])\
                   .then_inc(*to("param_in", 0, 16))
            act.dma_start(stage_state[:, 28, :], stored_rows("state_rwkv_shift")).then_inc(*to("states_in", 0, 16))
            act.dma_start(stage_state[:, 22:28, :], stored_rows("state_gdn_conv").rearrange("(i r) p -> r i p", r=P))\
               .then_inc(*to("states_in", 0, 16))
            act.dma_start(stage_state[:, 0:22, :], stored_rows("state_ffn_conv").rearrange("(i r) p -> r i p", r=P))\
               .then_inc(*to("states_in", 0, 16))
            act.dma_start(PG[:, :], io["page_table"].rearrange("(o b) n -> o (b n)", o=1)).then_inc(*to("pages_in", 0, 16))
            act.dma_start(AH[:, 0:1], io["gdn_a_log"].rearrange("o h -> h o")).then_inc(*to("heads_in", 0, 16))
            act.dma_start(AH[:, 1:2], io["gdn_dt_bias"].rearrange("o h -> h o")).then_inc(*to("heads_in", 0, 16))

        def stage_tile(kind, i):
            return {"x": stage_x, "par": stage_par, "state": stage_state}[kind][:, i, :]

        def pe_prologue(pe):
            pe.wait_ge(*at("const_in", 0))
            pe.wait_ge(*at("x_in", 0))
            for g, group in enumerate(groups):
                if group[0] == ("par", 0):
                    pe.wait_ge(*at("param_in", 0))
                if group[0] == ("state", 0):
                    pe.wait_ge(*at("states_in", 0))
                ps = bank(pe, ("pro", g), prologue_step(g))
                for n, (kind, i) in enumerate(group):
                    r = NPARAM - 9 * P if (kind, i) == ("par", 9) else P
                    ins = pe.transpose(ps[:, n * P:n * P + r], stage_tile(kind, i)[0:r, :], ident[0:r, 0:r])
                ins.then_inc(*to("pro_turned", g))

        def prologue_step(g):
            return ("x", (-1, g)) if g < 5 else ("pro_copied", g)

        turned_state = arena(59 * P, 22 * P)
        state_dst = [turned_state[:, i * P:(i + 1) * P] for i in range(22)] + \
                    [gdn_state[:, i * P:(i + 1) * P] for i in range(6)] + [shift_state[:, :]]

        def dve_prologue(dve):
            dve.memset(EB[:, 0:1], EPS)
            dve.memset(EB[:, 1:2], LNX_EPS).then_inc(*to("eps", 0))
            for g, group in enumerate(groups):
                dve.wait_ge(*at("pro_turned", g))
                ps = of(("pro", g))
                if g < 5:
                    dve.tensor_copy(X[:, :, g * 64:(g + 1) * 64],
                                    ps[:, :].rearrange("p (t m) -> p m t", m=MT)).then_inc(*to("x", (-1, g)))
                elif group[0][0] == "par":
                    a = group[0][1] * P
                    b = min(a + 512, NPARAM)
                    dve.tensor_copy(PT[:, a:b], ps[:, 0:b - a]).then_inc(*to("pro_copied", g))
                else:
                    for n, (_, i) in enumerate(group):
                        ins = dve.tensor_copy(state_dst[i], ps[:, n * P:(n + 1) * P])
                    ins.then_inc(*to("pro_copied", g))
                if group[-1] == ("par", 9):
                    dve.wait_ge(*at("pro_copied", g))
                    for dst, name in ((NW0, "rw_w0"), (NA0, "rw_a0"), (NV0, "rw_v0")):
                        n = 8 if name == "rw_v0" else 16
                        o = PARAM_AT[name]
                        dve.tensor_scalar(PX[:, dst:dst + n], PT[:, o:o + n], -1.0, None, ALU.mult)
                    o = PARAM_AT["rw_ka"]
                    dve.tensor_scalar(PX[:, OMKA:OMKA + 16], PT[:, o:o + 16], -1.0, 1.0, ALU.mult, ALU.add)\
                       .then_inc(*to("params2", 0))

        def act_keep_states(act):
            act.wait_ge(*at("pro_copied", len(groups) - 1))
            act.dma_start(io["ffn_state_t"], turned_state).then_inc(*to("ffn_state_t", 0, 16))
            act.wait_ge(*at("ffn_state_t", 0))

        Y = arena(0, 3, D)

        def pe_final(pe):
            q = 4 * layers - 1
            for g in range(6):
                t, half = divmod(g, 2)
                n = P if t < 2 else 64
                ps = bank(pe, ("y", g), ("y_rows", g))
                for i in range(4):
                    m = half * 4 + i
                    if t == 0:
                        pe.wait_ge(*at("x", (q, m)))
                    ins = pe.transpose(ps[0:n, i * P:(i + 1) * P], X[:, m, t * P:t * P + n], ident)
                ins.then_inc(*to("y_turned", g))

        def act_final(act):
            for g in range(6):
                t, half = divmod(g, 2)
                n = P if t < 2 else 64
                act.wait_ge(*at("y_turned", g))
                act.activation(Y[0:n, t, half * 512:(half + 1) * 512], of(("y", g))[0:n, :], ACT.Copy)\
                   .then_inc(*to("y_rows", g))
                if half:
                    act.wait_ge(*at("y_rows", g))
                    dst = io["y_prompt"][0, t * P:(t + 1) * P, :] if t < 2 else io["y_sample"].rearrange("b s d -> (b s) d")
                    act.dma_start(dst, Y[0:n, t, :]).then_inc(*to("y_stored", 0, 16))
            act.wait_ge(*at("y_stored", 0))

        BA, BB, BK, BV, BR, BG, BBON, B7, B8, B9, B10 = range(11)
        GE = SMALL[:, 0:96].rearrange("p (m c) -> p m c", m=MT)
        MID = SMALL[:, 96:96 + 5 * NT].rearrange("p (a t) -> p a t", a=5)
        mids = {"w": MID[0:64, 0, :], "a": MID[0:64, 1, :], "v": MID[0:32, 2, :]}
        SHO = SMALL[:, 1696:1768]
        SHR = SMALL[0:72, 1808:1936]
        U = 4608
        u0 = 7 * BLK

        def unit(u):
            o = u0 + u * U
            return dict(ea=arena(o, 4, P), am=arena(o + 512, 4, 384), tv=arena(o + 2048, 4, 384),
                        p=arena(o + 3584, 4, P), off=arena(o + 4096, 4, P),
                        inv=H[:, :, :].rearrange("p m t -> p (m t)")[:, u * 1024:(u + 1) * 1024]
                        .rearrange("p (a b) -> p a b", a=4))

        UNIT = [unit(0), unit(1)]
        ERING = arena(u0 + 2 * U, 3, 3, P)
        halves = PS[:, :, :].rearrange("p a t -> p (a t)"), SQ[:, :, :].rearrange("p a t -> p (a t)")
        MST = halves[0][:, 0:256].rearrange("p (u n) -> p u n", u=2)
        RHS = halves[0][:, 256:512].rearrange("p (u n) -> p u n", u=2)
        SAB = halves[1][:, 0:256].rearrange("p (u n) -> p u n", u=2)
        MG = halves[1][:, 256:512].rearrange("p (u n) -> p u n", u=2)

        def heads(ap3):
            return ap3[0:64, :, 0:64], ap3[64:128, :, 64:128]

        def rw_expect(l):
            return rw_of[l], 4 * l

        projections = [B10, BK, BV]
        mix_order = [3, 4, 5, 2, 1, 0]
        mix_slot = {i: n % 2 for n, i in enumerate(mix_order)}

        def pe_rwkv(pe, l):
            ri, q = rw_expect(l)
            pe_norm(pe, q)
            ps = bank(pe, ("shift", l), ("shift_rows", l))
            pe.wait_ge(*at("shift_kept", l))
            pe.transpose(ps[0:72, 0:P], SHO, ident).then_inc(*to("shift_turned", l))
            XM = [block(B8), block(B9)]
            for i, name, width in ((3, "w", 64), (4, "a", 64), (5, "g", 160)):
                w = W[:, weight(pe, (name + "1", l)), :]
                for part, n in enumerate((min(width, P), width - P)[:2 if width > P else 1]):
                    ps = bank(pe, ("lora1", l, name, part), ("lora_copied", (l, name)))
                    for k in range(MT):
                        if part == 0:
                            pe.wait_ge(*at("mixed", (l, i, k)))
                        ins = mm(pe, ps[0:n, 0:NT], w[:, k * width + part * P:k * width + part * P + n],
                                 XM[mix_slot[i]][:, k, :], k == 0, k == 7)
                ins.then_inc(*to("lora1_done", (l, name)))
                weight_used[(name + "1", l)] = ("lora1_done", (l, name))

            def lora2(name):
                w = W[:, weight(pe, (name + "2", l)), :]
                pe.wait_ge(*at("lora_mid" if name in "wg" else "lora_copied", (l, name)))
                for m in range(MT):
                    ps = bank(pe, ("lora2", l, name, m), ("lora2_out", (l, name, m)))
                    if name == "g":
                        mm(pe, ps[:, 0:NT], w[:, m * P:m * P + P], MID[:, 3, :], True, False)
                        ins = mm(pe, ps[:, 0:NT], w[0:32, D + m * P:D + m * P + P], MID[0:32, 4, :], False, True)
                    else:
                        n = 32 if name == "v" else 64
                        ins = mm(pe, ps[:, 0:NT], w[0:n, m * P:m * P + P], mids[name], True, True)
                    ins.then_inc(*to("lora2_done", (l, name, m)))
                weight_used[(name + "2", l)] = ("lora2_done", (l, name, m))

            def project(i, columns):
                for c in columns:
                    key = ("rkv", l, i, c)
                    w = W[:, weight(pe, key), :]
                    for j in range(2):
                        m = 2 * c + j
                        ps = bank(pe, ("rkv", l, i, m), ("rkv", (l, i, m)))
                        for k in range(MT):
                            if c == 0 and j == 0:
                                pe.wait_ge(*at("mixed", (l, i, k)))
                            ins = mm(pe, ps[:, 0:NT], w[:, k * 256 + j * P:k * 256 + j * P + P], XM[mix_slot[i]][:, k, :],
                                     k == 0, k == 7)
                        ins.then_inc(*to("rkv_done", (l, i, m)))
                    weight_used[key] = ("rkv_done", (l, i, m))

            for name in "wag":
                lora2(name)
            project(2, range(4))
            if ri:
                w = W[:, weight(pe, ("v1", l)), :]
                ps = bank(pe, ("lora1", l, "v", 0), ("lora_copied", (l, "v")))
                for k in range(MT):
                    ins = mm(pe, ps[0:32, 0:NT], w[:, k * 32:k * 32 + 32], XM[mix_slot[2]][:, k, :], k == 0, k == 7)
                ins.then_inc(*to("lora1_done", (l, "v")))
                weight_used[("v1", l)] = ("lora1_done", (l, "v"))
            project(1, range(1))
            if ri:
                lora2("v")
            project(1, range(1, 4))
            project(0, range(2))
            for m in range(MT):
                ps = bank(pe, ("kkss", l, m), ("kk_ln", (l, m)))
                pe.wait_ge(*at("kk_sq", (l, m)))
                mm(pe, ps[:, 0:NT], onesB, SQ[:, m % 4, :], True, True).then_inc(*to("kk_summed", (l, m)))
            project(0, range(2, 4))
            for m in range(MT):
                ps = bank(pe, ("bonus", l, m), ("bonus_v", (l, m)))
                pe.wait_ge(*at("rk", (l, m)))
                mm(pe, ps[:, 0:NT], onesB, H[:, m, :], True, True).then_inc(*to("bonus_summed", (l, m)))
            pe_rwkv_chunks(pe, l)
            for m in range(MT):
                ps = bank(pe, ("ymean", l, m), ("y_centered", (l, m)))
                pe.wait_ge(*at("y", (l, "s", m)))
                mm(pe, ps[:, 0:NT], mean64, block(BR)[:, m, :], True, True).then_inc(*to("ymean", (l, m)))
            for m in range(MT):
                ps = bank(pe, ("yvar", l, m), ("y_ln", (l, m)))
                pe.wait_ge(*at("y_sq", (l, m)))
                mm(pe, ps[:, 0:NT], mean64, SQ[:, m % 4, :], True, True).then_inc(*to("yvar", (l, m)))
            pe_out(pe, q + 1, [[("wo", l, c)] for c in range(4)], 8, lambda n: [("y_gated", (l, n))],
                   lambda n: block(BA)[:, n, :])
            pe_norm(pe, q + 1)

        def act_rwkv(act, l):
            ri, q = rw_expect(l)
            act_pre_norm(act, q)
            if l == 0:
                act_keep_states(act)
            act.wait_ge(*at("shift_turned", l))
            act.activation(SHR, of(("shift", l))[0:72, 0:P], ACT.Copy).then_inc(*to("shift_rows", l))
            act.wait_ge(*at("shift_rows", l))
            act.dma_start(io["p_rwkv_shift"][ri].rearrange("o (m p) -> (o m) p", p=P), SHR[0:8, :])\
               .then_inc(*to("shift_stored", l, 16))
            act.dma_start(io["s_rwkv_shift"][ri].rearrange("b (m p) -> (b m) p", p=P), SHR[8:72, :])\
               .then_inc(*to("shift_stored", l, 16))
            if ri == 0:
                act.wait_ge(*at("params2", 0))

            def copy_out(i, tiles):
                for m in tiles:
                    act.wait_ge(*at("rkv_done", (l, i, m)))
                    act.activation(block(projections[i])[:, m, :], of(("rkv", l, i, m))[:, 0:NT], ACT.Copy)\
                       .then_inc(*to("rkv", (l, i, m)))

            def lora2_out(name):
                for m in range(MT):
                    act.wait_ge(*at("lora2_done", (l, name, m)))
                    src = of(("lora2", l, name, m))[:, 0:NT]
                    if name == "g":
                        ins = act.activation(block(BG)[:, m, :], src, ACT.Copy)
                    else:
                        dst, bias = {"w": (BR, NW0 + ri * 8), "a": (BB, NA0 + ri * 8), "v": (BBON, NV0)}[name]
                        ins = act.activation(block(dst)[:, m, :], src, ACT.Exp, scale=-1.0,
                                             bias=PX[:, bias + m:bias + m + 1])
                    ins.then_inc(*to("lora2_out", (l, name, m)))

            for name, scale in (("w", -2.0), ("a", None), ("g", -1.0)):
                act.wait_ge(*at("lora1_done", (l, name)))
                if name == "a":
                    ins = act.activation(mids["a"], of(("lora1", l, "a", 0))[0:64, 0:NT], ACT.Copy)
                elif name == "w":
                    ins = act.activation(mids["w"], of(("lora1", l, "w", 0))[0:64, 0:NT], ACT.Exp, scale=scale)
                else:
                    act.activation(MID[:, 3, :], of(("lora1", l, "g", 0))[:, 0:NT], ACT.Exp, scale=scale)
                    ins = act.activation(MID[0:32, 4, :], of(("lora1", l, "g", 1))[0:32, 0:NT], ACT.Exp, scale=scale)
                ins.then_inc(*to("lora_copied", (l, name)))
            for name in "wag":
                lora2_out(name)
            copy_out(2, range(8))
            if ri == 0:
                act.wait_ge(*at("rkv", (l, 2, 7)))
                act.dma_start(io["v_first"], flat(BV)).then_inc(*to("v_first_stored", 0, 16))
            else:
                act.wait_ge(*at("v_first_stored", 0))
                act.dma_start(flat(BA), io["v_first"]).then_inc(*to("v_first_in", 0, 16))
                act.wait_ge(*at("lora1_done", (l, "v")))
                act.activation(mids["v"], of(("lora1", l, "v", 0))[0:32, 0:NT], ACT.Copy)\
                   .then_inc(*to("lora_copied", (l, "v")))
            copy_out(1, range(2))
            if ri:
                lora2_out("v")
            copy_out(1, range(2, 8))
            for m in range(4):
                act.wait_ge(*at("kkr", (l, m)))
                act_square(act, m, block(BA)[:, m, :], ("kk_sq", (l, m)), lambda n: ("kk_summed", (l, n)))
            copy_out(0, range(4))
            for m in range(4, MT):
                act.wait_ge(*at("kkr", (l, m)))
                act_square(act, m, block(BA)[:, m, :], ("kk_sq", (l, m)), lambda n: ("kk_summed", (l, n)))
                kk_rstd(act, l, m - 4)
            for m in range(4, MT):
                kk_rstd(act, l, m)
            act.wait_ge(*at("log_prev", l))
            act.activation(flat(BR), flat(BR), ACT.Exp).then_inc(*to("decay_prev", l))
            act.activation(flat(B8), flat(B7), ACT.Exp, scale=-1.0).then_inc(*to("decay_inv", l))
            act.wait_ge(*at("decay_inv", l))
            act.activation(flat(B7), flat(B7), ACT.Exp).then_inc(*to("decay", l))
            copy_out(0, range(4, 8))
            act_rwkv_chunks(act, l)
            for m in range(MT):
                act.wait_ge(*at("y_centered", (l, m)))
                act_square(act, m, block(BR)[:, m, :], ("y_sq", (l, m)), lambda n: ("yvar", (l, n)))
                if m >= 2:
                    y_rstd(act, l, m - 2)
            y_rstd(act, l, 6)
            y_rstd(act, l, 7)
            act_outputs(act, q + 1, ("shift_stored", l))

        def kk_rstd(act, l, m):
            act.wait_ge(*at("kk_summed", (l, m)))
            if m == 0 and rw_of[l]:
                act.wait_ge(*at("v_mixed", l))
            act.activation(block(BBON)[:, m, :], of(("kkss", l, m))[:, 0:NT], ACT.Ln, bias=EB[:, 0:1])\
               .then_inc(*to("kk_ln", (l, m)))
            act.wait_ge(*at("kk_ln", (l, m)))
            act.activation(block(BBON)[:, m, :], block(BBON)[:, m, :], ACT.Exp, scale=-0.5)\
               .then_inc(*to("kk_rstd", (l, m)))

        def y_rstd(act, l, m):
            act.wait_ge(*at("yvar", (l, m)))
            act.activation(block(B7)[:, m, :], of(("yvar", l, m))[:, 0:NT], ACT.Ln, bias=EB[:, 1:2])\
               .then_inc(*to("y_ln", (l, m)))
            act.wait_ge(*at("y_ln", (l, m)))
            act.activation(block(B7)[:, m, :], block(B7)[:, m, :], ACT.Exp, scale=-0.5)\
               .then_inc(*to("y_rstd", (l, m)))

        def dve_rwkv(dve, l):
            ri, q = rw_expect(l)
            dve_pre_norm(dve, q)
            dve.wait_ge(*at("h", (q, 7)))
            sho = SHO.rearrange("p (b m) -> p m b", m=MT)
            dve.tensor_copy(sho[:, :, 0:1], H[:, :, 255:256])
            dve.tensor_copy(sho[:, :, 1:9], H[:, :, SEQ + 7::8]).then_inc(*to("shift_kept", l))
            dx = block(B7)
            dve.tensor_tensor(dx[:, :, 1:NT], H[:, :, 0:NT - 1], H[:, :, 1:NT], ALU.subtract).then_inc(*to("dx_run", l))
            dve.wait_ge(*at("dx_run", l))
            dve.tensor_scalar(dx[:, :, 0:1], H[:, :, 0:1], -1.0, None, ALU.mult)
            st = shift_state[:, ri * 64:(ri + 1) * 64].rearrange("p (b m) -> p m b", m=MT)
            if l == 0:
                dve.wait_ge(*at("pro_copied", len(groups) - 1))
            dve.tensor_tensor(dx[:, :, SEQ::8], st, H[:, :, SEQ::8], ALU.subtract).then_inc(*to("dx", l))
            dve.wait_ge(*at("dx", l))

            def mix(i):
                n = mix_order.index(i)
                if n >= 2:
                    last = mix_order[n - 2]
                    dve.wait_ge(*(at("rkv_done", (l, last, 7)) if last < 3 else at("lora1_done", (l, "rkvwag"[last]))))
                    if last == 2 and ri:
                        dve.wait_ge(*at("lora1_done", (l, "v")))
                for k in range(MT):
                    dve.scalar_tensor_tensor(out=block(B8 + n % 2)[:, k, :], in0=dx[:, k, :],
                                             scalar=par("rw_mu", (ri * 6 + i) * 8 + k), in1=H[:, k, :],
                                             op0=ALU.mult, op1=ALU.add).then_inc(*to("mixed", (l, i, k)))

            def mid(name, views):
                dve.wait_ge(*at("lora_copied", (l, name)))
                for v in views:
                    dve.tensor_scalar(v, v, 1.0, None, ALU.add).then_inc(*to("mid_sum", (l, name)))
                dve.wait_ge(*at("mid_sum", (l, name)))
                for v in views:
                    ins = dve.reciprocal(v, v)
                if name == "w":
                    ins.then_inc(*to("mid_recip", l))
                    dve.wait_ge(*at("mid_recip", l))
                    ins = dve.tensor_scalar(mids["w"], mids["w"], 2.0, -1.0, ALU.mult, ALU.add)
                ins.then_inc(*to("lora_mid", (l, name)))

            def sigmoid(b, name, step):
                dve.wait_ge(*at("lora2_out", (l, name, 7)))
                dve.tensor_scalar(flat(b), flat(b), 1.0, None, ALU.add).then_inc(*to("sig_sum", (l, name)))
                dve.wait_ge(*at("sig_sum", (l, name)))
                dve.reciprocal(flat(b), flat(b)).then_inc(*to(step, l))
                dve.wait_ge(*at(step, l))

            mix(3)
            mix(4)
            mid("w", [mids["w"]])
            mix(5)
            mid("g", [MID[:, 3, :], MID[0:32, 4, :]])
            mix(2)
            mix(1)
            sigmoid(BR, "w", "w_sig")
            dve.tensor_scalar(flat(BR), flat(BR), -float(np.exp(-0.5)), None, ALU.mult).then_inc(*to("log_decay", l))
            sigmoid(BB, "a", "a_sig")
            if ri:
                sigmoid(BBON, "v", "v_sig")
                dve.wait_ge(*at("v_first_in", 0))
                dve.tensor_tensor(flat(BA), flat(BA), flat(BV), ALU.subtract).then_inc(*to("v_diff", l))
                dve.wait_ge(*at("v_diff", l))
                dve.tensor_tensor(flat(BA), flat(BA), flat(BBON), ALU.mult).then_inc(*to("v_part", l))
                dve.wait_ge(*at("v_part", l))
                dve.tensor_tensor(flat(BV), flat(BV), flat(BA), ALU.add).then_inc(*to("v_mixed", l))
                dve.wait_ge(*at("v_mixed", l))
            mix(0)
            dve.wait_ge(*at("log_decay", l))
            dve.wait_ge(*at("mixed", (l, 0, 7)))
            for m in range(MT):
                ins = dve.tensor_tensor_scan(block(B7)[:, m, :], const("seg64"), block(BR)[:, m, :], 0.0, ALU.mult, ALU.add)
            ins.then_inc(*to("log_sum", l))
            dve.wait_ge(*at("log_sum", l))
            dve.tensor_tensor(flat(BR), flat(B7), flat(BR), ALU.subtract).then_inc(*to("log_prev", l))
            for m in range(MT):
                ins = dve.tensor_scalar(H[:, m, :], block(BB)[:, m, :], par("rw_ka", ri * 8 + m),
                                        PX[:, OMKA + ri * 8 + m:OMKA + ri * 8 + m + 1], ALU.mult, ALU.add)
            ins.then_inc(*to("k_gain", l))
            for m in range(MT):
                dve.wait_ge(*at("rkv", (l, 1, m)))
                dve.tensor_scalar(block(BA)[:, m, :], block(BK)[:, m, :], par("rw_kk", ri * 8 + m), None, ALU.mult)\
                   .then_inc(*to("kkr", (l, m)))
            dve.wait_ge(*at("k_gain", l))
            dve.wait_ge(*at("kkr", (l, 7)))
            h_rows = H[:, :, :].rearrange("p m t -> p (m t)")
            dve.tensor_tensor(flat(BK), flat(BK), h_rows, ALU.mult).then_inc(*to("k_mod", l))
            dve.wait_ge(*at("kk_rstd", (l, 7)))
            dve.tensor_tensor(flat(BA), flat(BA), flat(BBON), ALU.mult).then_inc(*to("kk", l))
            dve.wait_ge(*at("kk", l))
            dve.tensor_tensor(flat(BB), flat(BA), flat(BB), ALU.mult).then_inc(*to("b", l))
            dve.wait_ge(*at("b", l))
            dve.wait_ge(*at("decay_prev", l))
            dve.scalar_tensor_tensor(out=flat(BA), in0=flat(BA), scalar=-1.0, in1=flat(BR), op0=ALU.mult,
                                     op1=ALU.mult).then_inc(*to("a_decayed", l))
            dve.wait_ge(*at("k_mod", l))
            for m in range(MT):
                dve.wait_ge(*at("rkv", (l, 0, m)))
                dve.scalar_tensor_tensor(out=H[:, m, :], in0=block(B10)[:, m, :],
                                         scalar=par("rw_rk", ri * 8 + m), in1=block(BK)[:, m, :],
                                         op0=ALU.mult, op1=ALU.mult).then_inc(*to("rk", (l, m)))
            dve.wait_ge(*at("rk", (l, 7)))
            dve.wait_ge(*at("decay_inv", l))
            dve.tensor_tensor(flat(BB), flat(BB), flat(B8), ALU.mult)
            dve.tensor_tensor(flat(BK), flat(BK), flat(B8), ALU.mult)
            dve.wait_ge(*at("decay", l))
            dve.tensor_copy(GE[:, :, 0:4], block(B7)[:, :, 63:SEQ:64])
            dve.tensor_copy(GE[:, :, 4:12], block(B7)[:, :, SEQ + 7::8]).then_inc(*to("a_scaled", l))
            dve.wait_ge(*at("a_decayed", l))
            dve.tensor_tensor(flat(BR), flat(B10), flat(B7), ALU.mult).then_inc(*to("prepared", l))
            for m in range(MT):
                dve.wait_ge(*at("bonus_summed", (l, m)))
                dve.tensor_tensor(block(BBON)[:, m, :], of(("bonus", l, m))[:, 0:NT], block(BV)[:, m, :], ALU.mult)\
                   .then_inc(*to("bonus_v", (l, m)))
            dve_rwkv_chunks(dve, l)
            for m in range(MT):
                dve.wait_ge(*at("ymean", (l, m)))
                dve.tensor_tensor(block(BR)[:, m, :], block(BR)[:, m, :], of(("ymean", l, m))[:, 0:NT], ALU.subtract)\
                   .then_inc(*to("y_centered", (l, m)))
            for j in (5, 6, 7):
                dve.wait_ge(*at(f"sout_stored{j % 3}", (l, j)))
            for m in range(MT):
                dve.wait_ge(*at("y_rstd", (l, m)))
                t = block(B8)[:, m, :]
                dve.tensor_tensor(t, block(BR)[:, m, :], block(B7)[:, m, :], ALU.mult).then_inc(*to("y1", (l, m)))
                dve.wait_ge(*at("y1", (l, m)))
                dve.tensor_scalar(t, t, par("rw_lnx_w", ri * 8 + m), par("rw_lnx_b", ri * 8 + m), ALU.mult, ALU.add)\
                   .then_inc(*to("y2", (l, m)))
                dve.wait_ge(*at("y2", (l, m)))
                dve.tensor_tensor(t, t, block(BBON)[:, m, :], ALU.add).then_inc(*to("y3", (l, m)))
                dve.wait_ge(*at("y3", (l, m)))
                dve.tensor_tensor(block(BA)[:, m, :], t, block(BG)[:, m, :], ALU.mult).then_inc(*to("y_gated", (l, m)))
            dve_post_norm(dve, q + 1)

        rounds = [[("p", 2 * r), ("p", 2 * r + 1)] for r in range(4)] + [[("s", 0)], [("s", 1)]]

        def batches():
            n = 0
            for r, members in enumerate(rounds):
                for u, (kind, i) in enumerate(members):
                    yield n, r, u, kind, i
                    n += 1

        in_round = [[b for b in batches() if b[1] == r] for r in range(6)]

        def columns(kind, i, el):
            return (i, el * 64) if kind == "p" else (4 * i + el, SEQ)

        def levels(kind):
            return range(6 if kind == "p" else 3)

        def last_of(l, r, u):
            if r == 0:
                return None
            if r <= 4:
                return ("ymm", (l, "p", 2 * (r - 1) + u, 3))
            return ("smm", (l, 4 * (r - 5) + 3, 1))

        def pe_pair_in(pe, l, j):
            pe.wait_ge(*at(f"sin{j % 3}", (l, j)))
            for g in range(2):
                ps = bank(pe, ("sin", l, j, g), ("m0", (l, j, g)))
                for b in range(4):
                    ins = pe.transpose(ps[:, b * P:(b + 1) * P], SIN[j % 3][:, 4 * g + b, :], ident)
                ins.then_inc(*to("sin_turned", (l, j, g)))

        def pe_pair_read(pe, l, j):
            ps = bank(pe, ("z", l, j), ("z", (l, j)))
            pe.wait_ge(*at("m0", (l, j, 1)))
            ar = A[:, 0:5 * BLK].rearrange("p (b n) -> p b n", b=5)
            for b in range(DEC):
                c0 = j * NT + SEQ + 8 * b
                ins = mm(pe, ps[:, 16 * b:16 * b + 16], M0[j % 2][:, b, :], ar[:, 0:5:4, c0:c0 + 8], True, True)
            ins.then_inc(*to("z_done", (l, j)))

        def pe_pair_out(pe, l, j):
            for g in range(2):
                ps = bank(pe, ("sout", l, j, g), ("sout", (l, j, g)))
                pe.wait_ge(*at("m_new", (l, j, g)))
                for b in range(4):
                    ins = pe.transpose(ps[:, b * P:(b + 1) * P], M0[j % 2][:, 4 * g + b, :], ident)
                ins.then_inc(*to("sout_turned", (l, j, g)))

        def act_pair_in(act, l, j):
            for g in range(2):
                act.wait_ge(*at("sin_turned", (l, j, g)))
                if j >= 2:
                    act.wait_ge(*at("sout_turned", (l, j - 2, 1)))
                act.activation(M0[j % 2][:, 4 * g:4 * g + 4, :], of(("sin", l, j, g)), ACT.Copy).then_inc(*to("m0", (l, j, g)))

        def act_pair_read(act, l, j):
            act.wait_ge(*at("z_done", (l, j)))
            if j >= 2:
                act.wait_ge(*at("ymm", (l, "s", j - 2)))
            z = of(("z", l, j))[:, 0:P].rearrange("p (b a s) -> p b a s", b=DEC, a=2)
            for half in range(2):
                hs = slice(64 * half, 64 * half + 64)
                act.activation(ZB[j % 2][hs, 0, hs].rearrange("p (b s) -> p b s", b=DEC), z[hs, :, 0, :], ACT.Copy)
            act.activation(ZB[j % 2][:, 1, 0:64].rearrange("p (b s) -> p b s", b=DEC), z[:, :, 1, :], ACT.Copy)\
               .then_inc(*to("z", (l, j)))

        def act_pair_out(act, l, j):
            for g in range(2):
                act.wait_ge(*at("sout_turned", (l, j, g)))
                act.activation(SIN[j % 3][:, 4 * g:4 * g + 4, :], of(("sout", l, j, g)), ACT.Copy)\
                   .then_inc(*to("sout", (l, j, g)))

        up_, low_ = u0 + U, H[:, :, :].rearrange("p m t -> p (m t)")
        eight = lambda ap: ap.rearrange("p (b n) -> p b n", n=P)
        SIN = [arena(up_, DEC, P), arena(up_ + 1024, DEC, P), arena(u0 + 2 * U + 1152, DEC, P)]
        M0 = [eight(low_[:, 1024:2048]), arena(up_ + 2048, DEC, P)]
        BM = [arena(up_ + 3072, 4, P), arena(up_ + 3584, 4, P)]
        KM = [arena(up_ + 4096, 4, P), eight(low_[:, 2048:2560])]
        ZB = [halves[1][:, 256:512].rearrange("p (u n) -> p u n", u=2), halves[1][:, 512:768].rearrange("p (u n) -> p u n", u=2)]
        PST = halves[1][:, 512:768].rearrange("p (u n) -> p u n", u=2)
        ring_at = [(n, el) for n, _, _, _, _ in batches() for el in range(4)]

        def pool_rwkv_chunks(pool, l):
            ri = rw_of[l]
            pool.wait_ge(*at("prepared", l))
            half = const("half")
            for r, members in enumerate(in_round):
                for n, _, u, kind, i in members:
                    if last_of(l, r, u):
                        pool.wait_ge(*at(*last_of(l, r, u)))
                    src = block(BA)[:, i, 0:SEQ].rearrange("p (c t) -> p c t", c=4) if kind == "p" else \
                        block(BA)[:, 4 * i:4 * i + 4, SEQ:NT]
                    pool.tensor_tensor(UNIT[u]["ea"].rearrange("p c (h t) -> p c h t", h=2),
                                       src.unsqueeze(2).broadcast_to([P, 4, 2, 64]),
                                       half.unsqueeze(1).unsqueeze(3).broadcast_to([P, 4, 2, 64]), ALU.mult)\
                        .then_inc(*to("ea", (l, n)))
                    for el in range(4):
                        g = 4 * n + el
                        if g >= 3:
                            pool.wait_ge(*at("amm", (l,) + ring_at[g - 3]))
                        tile, t0 = columns(kind, i, el)
                        src = A[:, BB * BLK:(BV + 1) * BLK].rearrange("p (b n) -> p b n", b=3)[
                            :, :, tile * NT + t0:tile * NT + t0 + 64]
                        pool.tensor_tensor(ERING[:, g % 3, :, :].rearrange("p c (h t) -> p c h t", h=2),
                                           src.unsqueeze(2).broadcast_to([P, 3, 2, 64]),
                                           half.unsqueeze(1).unsqueeze(3).broadcast_to([P, 3, 2, 64]), ALU.mult)\
                            .then_inc(*to("spread", (l, n, el)))
                kind = members[0][3]
                if r == 4:
                    pool.wait_ge(*at("ymm", (l, "p", 7, 3)))
                    for buffer in SIN:
                        ins = pool.memset(buffer, 0.0)
                    ins.then_inc(*to("sin_zero", l))
                for lev in levels(kind):
                    for n, _, u, _, _ in members:
                        pool.wait_ge(*at("am", (l, n, 3)))
                        if lev:
                            pool.wait_ge(*at("pmm", (l, n, lev - 1)))
                            if lev == 1:
                                pool.wait_ge(*at("inv", (l, n, 0)))
                        pool.tensor_tensor(UNIT[u]["off"], UNIT[u]["am"][:, :, 0:P],
                                           const(f"lev{lev}").unsqueeze(1).broadcast_to([P, 4, P]), ALU.mult)\
                            .then_inc(*to("off", (l, n, lev)))
                if kind == "s":
                    for el in range(4):
                        j = 4 * members[0][4] + el
                        if j:
                            pool.wait_ge(*at("smm", (l, j - 1, 1)))
                        pool.wait_ge(*at("tv", (l, members[0][0], el)))
                        for g in range(2):
                            for x, dst in ((1, BM), (2, KM)):
                                ins = pool.tensor_tensor(
                                    dst[g], UNIT[0]["tv"][:, el, x * P:(x + 1) * P].unsqueeze(1).broadcast_to([P, 4, P]),
                                    const("batch8", 4 * g, 4 * g + 4).unsqueeze(2).broadcast_to([P, 4, P]), ALU.mult)
                        ins.then_inc(*to("bkm", (l, j)))

        def sp_rwkv_states(sp, l):
            ri = rw_of[l]

            def load(j):
                for side in range(2):
                    hs = slice(64 * side, 64 * side + 64)
                    sp.dma_start(SIN[j % 3][hs, :, hs], io["state_rwkv_wkv"][ri][:, 2 * j + side].rearrange("b v k -> v b k"))\
                        .then_inc(*to(f"sin{j % 3}", (l, j), 16))

            sp.wait_ge(*at("sin_zero", l))
            for j in range(3):
                load(j)
            for j in range(8):
                sp.wait_ge(*at("sout", (l, j, 1)))
                for side in range(2):
                    hs = slice(64 * side, 64 * side + 64)
                    sp.dma_start(io["s_rwkv_wkv"][ri][:, 2 * j + side].rearrange("b v k -> v b k"), SIN[j % 3][hs, :, hs])\
                        .then_inc(*to(f"sout_stored{j % 3}", (l, j), 16))
                if j + 3 < 8:
                    sp.wait_ge(*at(f"sout_stored{j % 3}", (l, j)))
                    load(j + 3)

        def pe_rwkv_chunks(pe, l):
            pe.wait_ge(*at("prepared", l))
            for r, members in enumerate(in_round):
                kind = members[0][3]
                for n, _, u, _, i in members:
                    un = UNIT[u]
                    for el in range(4):
                        tile, t0 = columns(kind, i, el)
                        b, k, v = [ERING[:, (4 * n + el) % 3, x, :] for x in range(3)]
                        rt = block(BR)[:, tile, t0:t0 + 64]
                        pe.wait_ge(*at("spread", (l, n, el)))
                        ps = bank(pe, ("tv", l, n, el), ("tv", (l, n, el)))
                        for x, m in enumerate((v, b, k)):
                            ins = pe.transpose(ps[:, x * P:(x + 1) * P], m, ident)
                        ins.then_inc(*to("tv_done", (l, n, el)))
                        ps = bank(pe, ("am", l, n, el), ("am", (l, n, el)))
                        for x, m in enumerate((b, k)):
                            mm(pe, ps[:, x * 192:x * 192 + P], m, un["ea"][:, el, :], True, True)
                            ins = mm(pe, ps[:, x * 192 + P:x * 192 + 192], m, rt, True, True)
                        ins.then_inc(*to("amm", (l, n, el)))
                if r == 4:
                    pe_pair_in(pe, l, 0)
                for lev in levels(kind):
                    for n, _, u, _, _ in members:
                        un = UNIT[u]
                        pe.wait_ge(*at("off", (l, n, lev)))
                        if lev:
                            pe.wait_ge(*at("inv", (l, n, lev - 1)))
                        ps = bank(pe, ("p", l, n, lev), ("p", (l, n, lev)) if lev else ("inv", (l, n, 0)))
                        for el in range(4):
                            ins = mm(pe, ps[:, el * P:(el + 1) * P], un["off"][:, el, :],
                                     un["inv"][:, el, 0:P] if lev else ident, True, True)
                        ins.then_inc(*to("pmm", (l, n, lev)))
                    if lev:
                        for n, _, u, _, _ in members:
                            un = UNIT[u]
                            pe.wait_ge(*at("p", (l, n, lev)))
                            for g in range(2):
                                ps = bank(pe, ("imm", l, n, lev, g), ("inv", (l, n, lev)))
                                for el in (2 * g, 2 * g + 1):
                                    o = (el % 2) * 256
                                    if lev < levels(kind)[-1]:
                                        mm(pe, ps[:, o:o + P], un["inv"][:, el, P:256], un["p"][:, el, :], True, True)
                                    ins = mm(pe, ps[:, o + P:o + 256], un["p"][:, el, :], un["inv"][:, el, P:256], True, True)
                                ins.then_inc(*to("imm", (l, n, lev, g)))
                if kind == "p":
                    for c in range(4):
                        for n, _, u, _, j in members:
                            un = UNIT[u]
                            ps = bank(pe, ("rhs", l, "p", j, c), ("rhs", (l, "p", j, c)))
                            if c:
                                pe.wait_ge(*at("state", (l, j, c - 1)))
                                mm(pe, ps[:, 0:P], un["ea"][:, c, :], MST[:, u, :], True, False)
                            else:
                                pe.wait_ge(*at("inv", (l, n, levels(kind)[-1])))
                                pe.wait_ge(*at("tv", (l, n, 3)))
                            mm(pe, ps[:, 0:P], un["am"][:, c, 192:320], un["tv"][:, c, 0:P], not c, True)\
                                .then_inc(*to("rhs_done", (l, "p", j, c)))
                        for n, _, u, _, j in members:
                            pe.wait_ge(*at("rhs", (l, "p", j, c)))
                            ps = bank(pe, ("sa", l, "p", j, c), ("sa", (l, "p", j, c)))
                            mm(pe, ps[:, 0:P], UNIT[u]["inv"][:, c, P:256], RHS[:, u, :], True, True)\
                                .then_inc(*to("sa_done", (l, "p", j, c)))
                        for n, _, u, _, j in members:
                            un = UNIT[u]
                            pe.wait_ge(*at("sa", (l, "p", j, c)))
                            ps = bank(pe, ("ym", l, "p", j, c), ("y", (l, "p", j, c)))
                            if c:
                                mm(pe, ps[:, 0:64], MST[:, u, :], block(BR)[:, j, c * 64:c * 64 + 64], True, False)
                            mm(pe, ps[:, 0:64], SAB[:, u, :], un["am"][:, c, P:192], not c, False)
                            mm(pe, ps[:, 0:64], un["tv"][:, c, 0:P], un["am"][:, c, 320:384], False, True)\
                                .then_inc(*to("y_done", (l, "p", j, c)))
                            ps = bank(pe, ("mu", l, "p", j, c), ("mg", (l, j, c)))
                            mm(pe, ps[:, 0:P], un["tv"][:, c, P:256], SAB[:, u, :], True, False)
                            mm(pe, ps[:, 0:P], un["tv"][:, c, 256:384], un["tv"][:, c, 0:P], False, True)\
                                .then_inc(*to("ymm", (l, "p", j, c)))
                    for n, _, u, _, j in members:
                        pe.wait_ge(*at("state", (l, j, 3)))
                        ps = bank(pe, ("pst", l, j), ("pstate", (l, j)))
                        pe.transpose(ps[:, 0:P], MST[:, u, :], ident).then_inc(*to("pstate_turned", (l, j)))
                else:
                    n, un = members[0][0], UNIT[0]
                    if r == 4:
                        pe_pair_read(pe, l, 0)
                    for el in range(4):
                        j = 4 * members[0][4] + el
                        if j < 7:
                            pe_pair_in(pe, l, j + 1)
                        pe.wait_ge(*at("z", (l, j)))
                        if el == 0:
                            pe.wait_ge(*at("inv", (l, n, levels(kind)[-1])))
                            pe.wait_ge(*at("tv", (l, n, 3)))
                        ps = bank(pe, ("rhs", l, "s", j), ("rhs", (l, "s", j)))
                        mm(pe, ps[:, 0:P], ZB[j % 2][:, 0, :], ident, True, False)
                        mm(pe, ps[:, 0:P], un["am"][:, el, 192:320], un["tv"][:, el, 0:P], False, True)\
                            .then_inc(*to("rhs_done", (l, "s", j)))
                        if el:
                            pe_pair_out(pe, l, j - 1)
                        ps = bank(pe, ("sa", l, "s", j), ("sa", (l, "s", j)))
                        pe.wait_ge(*at("rhs", (l, "s", j)))
                        mm(pe, ps[:, 0:P], un["inv"][:, el, P:256], RHS[:, j % 2, :], True, True)\
                            .then_inc(*to("sa_done", (l, "s", j)))
                        if j < 7:
                            pe_pair_read(pe, l, j + 1)
                        ps = bank(pe, ("ym", l, "s", j), ("y", (l, "s", j)))
                        mm(pe, ps[:, 0:64], ident, ZB[j % 2][:, 1, 0:64], True, False)
                        mm(pe, ps[:, 0:64], un["tv"][:, el, 0:P], un["am"][:, el, 320:384], False, False)
                        pe.wait_ge(*at("sa", (l, "s", j)))
                        mm(pe, ps[:, 0:64], SAB[:, j % 2, :], un["am"][:, el, P:192], False, True)\
                            .then_inc(*to("ymm", (l, "s", j)))
                        pe.wait_ge(*at("bkm", (l, j)))
                        for g in range(2):
                            ps = bank(pe, ("smm", l, j, g), ("m_sum", (l, j, g)))
                            for b in range(4):
                                out = ps[:, b * P:b * P + P]
                                mm(pe, out, KM[g][:, b, :], un["tv"][:, el, 0:P], True, False)
                                ins = mm(pe, out, BM[g][:, b, :], SAB[:, j % 2, :], False, True)
                            ins.then_inc(*to("smm", (l, j, g)))
                        if el == 3:
                            pe_pair_out(pe, l, j)

        def act_rwkv_chunks(act, l):
            ri = rw_of[l]
            for r, members in enumerate(in_round):
                kind = members[0][3]
                for n, _, u, _, _ in members:
                    if r > 0 and last_of(l, r, u):
                        act.wait_ge(*at(*last_of(l, r, u)))
                    elif r == 0 and u == 0:
                        act.wait_ge(*at("prepared", l))
                        act.wait_ge(*at("bonus_summed", (l, 7)))
                    for el in range(4):
                        act.wait_ge(*at("tv_done", (l, n, el)))
                        act.activation(UNIT[u]["tv"][:, el, :], of(("tv", l, n, el))[:, 0:384], ACT.Copy)\
                           .then_inc(*to("tv", (l, n, el)))
                if r == 4:
                    act_pair_in(act, l, 0)
                for lev in levels(kind):
                    if lev:
                        for n, _, u, _, _ in members:
                            act.wait_ge(*at("pmm", (l, n, lev)))
                            if lev > 1:
                                act.wait_ge(*at("imm", (l, n, lev - 1, 1)))
                            act.activation(UNIT[u]["p"], of(("p", l, n, lev)), ACT.Copy).then_inc(*to("p", (l, n, lev)))
                if kind == "p":
                    for c in range(4):
                        for n, _, u, _, j in members:
                            act.wait_ge(*at("rhs_done", (l, "p", j, c)))
                            act.activation(RHS[:, u, :], of(("rhs", l, "p", j, c))[:, 0:P], ACT.Copy)\
                               .then_inc(*to("rhs", (l, "p", j, c)))
                        for n, _, u, _, j in members:
                            act.wait_ge(*at("sa_done", (l, "p", j, c)))
                            act.activation(SAB[:, u, :], of(("sa", l, "p", j, c))[:, 0:P], ACT.Copy)\
                               .then_inc(*to("sa", (l, "p", j, c)))
                        for n, _, u, _, j in members:
                            act.wait_ge(*at("ymm", (l, "p", j, c)))
                            if c or r:
                                act.wait_ge(*at("state", (l, j, c - 1) if c else (l, j - 2, 3)))
                            act.activation(MG[:, u, :], of(("mu", l, "p", j, c))[:, 0:P], ACT.Copy,
                                           scale=GE[:, j, c:c + 1]).then_inc(*to("mg", (l, j, c)))
                    for n, _, u, _, j in members:
                        act.wait_ge(*at("pstate_turned", (l, j)))
                        if r:
                            act.wait_ge(*at(f"pstate_stored{u}", (l, j - 2)))
                        act.activation(PST[:, u, :], of(("pst", l, j))[:, 0:P], ACT.Copy).then_inc(*to("pstate", (l, j)))
                        act.wait_ge(*at("pstate", (l, j)))
                        for half in range(2):
                            hs = slice(64 * half, 64 * half + 64)
                            act.dma_start(io["p_rwkv_wkv"][ri, 0, 2 * j + half], PST[hs, u, hs])\
                               .then_inc(*to(f"pstate_stored{u}", (l, j), 16))
                else:
                    if r == 4:
                        for u in range(2):
                            act.wait_ge(*at(f"pstate_stored{u}", (l, 6 + u)))
                        act.activation(ZB[0][:, 0, :], ident, ACT.Copy, scale=0.0)
                        act.activation(ZB[1][:, 0, :], ident, ACT.Copy, scale=0.0).then_inc(*to("z_zero", l))
                        act.wait_ge(*at("z_zero", l))
                        act_pair_read(act, l, 0)
                    for el in range(4):
                        j = 4 * members[0][4] + el
                        act.wait_ge(*at("rhs_done", (l, "s", j)))
                        act.activation(RHS[:, j % 2, :], of(("rhs", l, "s", j))[:, 0:P], ACT.Copy).then_inc(*to("rhs", (l, "s", j)))
                        if j < 7:
                            act_pair_in(act, l, j + 1)
                        act.wait_ge(*at("sa_done", (l, "s", j)))
                        if j >= 2:
                            act.wait_ge(*at("smm", (l, j - 2, 1)))
                        act.activation(SAB[:, j % 2, :], of(("sa", l, "s", j))[:, 0:P], ACT.Copy).then_inc(*to("sa", (l, "s", j)))
                        if el:
                            act_pair_out(act, l, j - 1)
                        if j < 7:
                            act_pair_read(act, l, j + 1)
                        if el == 3:
                            act_pair_out(act, l, j)

        def dve_rwkv_chunks(dve, l):
            for r, members in enumerate(in_round):
                kind = members[0][3]
                for n, _, u, _, _ in members:
                    if last_of(l, r, u):
                        dve.wait_ge(*at(*last_of(l, r, u)))
                    for el in range(4):
                        dve.wait_ge(*at("amm", (l, n, el)))
                        dve.tensor_tensor(UNIT[u]["am"][:, el, :], of(("am", l, n, el))[:, 0:384],
                                          const("amask_" + kind), ALU.mult).then_inc(*to("am", (l, n, el)))
                idb = ident.unsqueeze(1).broadcast_to([P, 4, P])
                for lev in levels(kind):
                    for n, _, u, _, _ in members:
                        un = UNIT[u]
                        if lev == 0:
                            dve.wait_ge(*at("pmm", (l, n, 0)))
                            dve.tensor_tensor(un["inv"][:, :, 0:P], of(("p", l, n, 0))[:, :].rearrange("p (a b) -> p a b", a=4),
                                              idb, ALU.add)
                            dve.tensor_tensor(un["inv"][:, :, P:256], un["off"], idb, ALU.add)\
                               .then_inc(*to("inv", (l, n, 0)))
                        else:
                            dve.wait_ge(*at("inv", (l, n, lev - 1)))
                            for g in range(2):
                                dve.wait_ge(*at("imm", (l, n, lev, g)))
                                first = P if lev == levels(kind)[-1] else 0
                                part = un["inv"][:, 2 * g:2 * g + 2, first:256]
                                ins = dve.tensor_tensor(part, part, of(("imm", l, n, lev, g))[:, :]
                                                        .rearrange("p (a b) -> p a b", a=2)[:, :, first:256], ALU.add)
                            ins.then_inc(*to("inv", (l, n, lev)))
                if kind == "p":
                    for c in range(4):
                        for n, _, u, _, j in members:
                            dve.wait_ge(*at("y_done", (l, "p", j, c)))
                            dve.tensor_copy(block(BR)[:, j, c * 64:c * 64 + 64], of(("ym", l, "p", j, c))[:, 0:64])\
                               .then_inc(*to("y", (l, "p", j, c)))
                            dve.wait_ge(*at("mg", (l, j, c)))
                            if c == 0:
                                if r:
                                    dve.wait_ge(*at("pstate_turned", (l, j - 2)))
                                ins = dve.tensor_copy(MST[:, u, :], MG[:, u, :])
                            else:
                                dve.wait_ge(*at("state", (l, j, c - 1)))
                                ins = dve.scalar_tensor_tensor(out=MST[:, u, :], in0=MST[:, u, :], scalar=GE[:, j, c:c + 1],
                                                               in1=MG[:, u, :], op0=ALU.mult, op1=ALU.add)
                            ins.then_inc(*to("state", (l, j, c)))
                else:
                    for el in range(4):
                        j = 4 * members[0][4] + el
                        dve.wait_ge(*at("ymm", (l, "s", j)))
                        dve.tensor_copy(block(BR)[:, j, SEQ:NT], of(("ym", l, "s", j))[:, 0:64]).then_inc(*to("y", (l, "s", j)))
                        for g in range(2):
                            dve.wait_ge(*at("smm", (l, j, g)))
                            part = M0[j % 2][:, 4 * g:4 * g + 4, :]
                            dve.tensor_tensor(part, part, of(("smm", l, j, g))[:, :].rearrange("p (a b) -> p a b", a=4),
                                              ALU.add).then_inc(*to("m_sum", (l, j, g)))
                        for g in range(2):
                            dve.wait_ge(*at("m_sum", (l, j, g)))
                            part = M0[j % 2][:, 4 * g:4 * g + 4, :]
                            ge = GE[:, j, 4 + 4 * g:8 + 4 * g].unsqueeze(2).broadcast_to([P, 4, P])
                            dve.tensor_tensor(part, part, ge, ALU.mult).then_inc(*to("m_new", (l, j, g)))

        QKV = arena(0, 32, NT)
        Z = arena(4 * BLK, 16, NT)
        g0 = 6 * BLK
        XG = arena(g0, 4, 348)
        CTG, CVG, EXG, GDG = (arena(g0 + 1392 + i * 688, 2, 344) for i in range(4))
        ZE = arena(g0 + 4144, 2, NT)
        TAP3 = arena(g0 + 6600, 2, 344)
        TAILG = arena(g0 + 4784, 864)
        TOUTG = arena(g0 + 5648, 7, P)
        ROWS = MID[0:16, :, :]
        GU = 3072
        def gunit(u):
            o = g0 + u * GU
            return dict(am=arena(o, 4, P), aq=arena(o + 512, 4, P), off=arena(o + 1024, 4, P), p=arena(o + 1536, 4, P),
                        vb=arena(o + 2048, 4, P), kg=arena(o + 2560, 4, P), inv=UNIT[u]["inv"])
        GUNIT = [gunit(0), gunit(1)]
        o_ = g0 + 2 * GU
        QG, EG, GCS, BS = (arena(o_ + i * 1280, 4, NT) for i in range(4))
        GS = arena(o_ + 5120, 4, P)
        GR = halves[0][:, 0:512].rearrange("p (u n) -> p u n", u=4)
        GV = halves[1][:, 0:512].rearrange("p (u n) -> p u n", u=4)
        h_flat = H[:, :, :].rearrange("p m t -> p (m t)")
        four_states = lambda ap: ap.rearrange("p (b v) -> p b v", b=4)
        SGS = [[arena(g0 + GU, 4, P), arena(g0 + GU + 512, 4, P)], [arena(g0 + GU + 1024, 4, P), arena(g0 + GU + 1536, 4, P)],
               [four_states(h_flat[:, 1024:1536]), four_states(h_flat[:, 1536:2048])],
               [four_states(h_flat[:, 2048:2560]), GS]]
        KGM = [arena(g0 + GU + 2048, DEC, P), arena(o_, DEC, P)]
        KQM = [arena(o_ + 5632 + i * 1088, 1088) for i in range(2)]
        ZC = halves[1][:, 512:768].rearrange("p (u n) -> p u n", u=2)
        tokens3 = halves[1][:, 768:768 + 288].rearrange("p (c k h) -> p c k h", c=3, k=6)
        T_BETA, T_GC, T_EGL, T_NBE, T_EG, T_X = range(6)

        def g_window(s):
            return XG[:, s, 259:347].rearrange("p (b w) -> p b w", b=DEC)

        tailg_p = TAILG[:, 0:96].rearrange("p (j m) -> p j m", j=3)
        tailg_s = TAILG[:, 96:864].rearrange("p (b j m) -> p b j m", b=DEC, j=3)
        gq = 8

        g_rounds = [[("p", 2 * r), ("p", 2 * r + 1)] for r in range(4)] + [[("s", i)] for i in range(4)]
        g_in_round, _n = [], 0
        for r, members in enumerate(g_rounds):
            g_in_round.append([])
            for u, (kind, i) in enumerate(members):
                g_in_round[-1].append((_n, r, u, kind, i))
                _n += 1

        def g_head(kind, i, el):
            return 2 * i + el // 2 if kind == "p" else 4 * i + el

        def g_levels(kind):
            return range(7 if kind == "p" else 3)

        def g_last(r, u):
            if r == 0:
                return None
            if r <= 4:
                return ("g_mu", (2 * (2 * (r - 1) + u) + 1, 1))
            return ("gs_mm", (4 * (r - 5) + 3, 1))

        def pe_states_read(pe, h):
            pe.wait_ge(*at(f"gs_in{h % 4}", h))
            pe.wait_ge(*at("km", h))
            ps = bank(pe, ("gks", h), ("gs_z", h))
            for b in range(DEC):
                ins = mm(pe, ps[:, 0:P], KQM[h % 2][:, b * P:b * P + P], SGS[h % 4][b // 4][:, b % 4, :], b == 0, b == DEC - 1)
            ins.then_inc(*to("gks_done", h))

        def sp_states(sp):
            def load(h):
                for g in range(2):
                    sp.dma_start(SGS[h % 4][g], io["state_gdn_S"][0, 4 * g:4 * g + 4, h].rearrange("b k v -> k b v"))\
                        .then_inc(*to(f"gs_in{h % 4}", h, 16))
            sp.wait_ge(*at("g_mu", (15, 1)))
            sp.wait_ge(*at("g_state", (15, 1)))
            for h in range(4):
                if h == 3:
                    for s in range(4):
                        sp.wait_ge(*at(f"gps_stored{s}", 12 + s))
                load(h)
            for h in range(16):
                for g in range(2):
                    sp.wait_ge(*at("gs_new", (h, g)))
                    sp.dma_start(io["s_gdn_S"][0, 4 * g:4 * g + 4, h].rearrange("b k v -> k b v"), SGS[h % 4][g])\
                        .then_inc(*to(f"gs_out{h % 4}", h, 16))
                if h and h + 3 < 16:
                    sp.wait_ge(*at(f"gs_out{(h - 1) % 4}", h - 1))
                    load(h + 3)

        def pe_gdn(pe, l):
            def l2_sum(t):
                ps = bank(pe, ("l2", t), ("l2_ln", t))
                pe.wait_ge(*at("l2_sq", t))
                mm(pe, ps[:, 0:NT], ones, SQ[:, t % 4, :], True, True).then_inc(*to("l2_summed", t))

            pe_norm(pe, gq)
            for c in range(24):
                w = W[:, weight(pe, ("gin", c)), :]
                for j in range(2):
                    t = 2 * c + j
                    ps = bank(pe, ("gin", t), ("gxp", t) if t < 32 else ("z_out", t))
                    for k in range(MT):
                        if t == 0:
                            pe.wait_ge(*at("h", (gq, k)))
                        ins = mm(pe, ps[:, 0:NT], w[:, k * 256 + j * P:k * 256 + j * P + P], H[:, k, :], k == 0, k == 7)
                    ins.then_inc(*to("gin_done", t))
                    if t > 32:
                        l2_sum(t - 33)
                weight_used[("gin", c)] = ("gin_done", t)
            l2_sum(15)
            w = W[:, weight(pe, ("gin", 24)), :]
            for x, name in enumerate(("beta", "dt")):
                ps = bank(pe, ("gin", name), ("g_e1", 0) if name == "beta" else ("g_t", 0))
                for k in range(MT):
                    ins = mm(pe, ps[0:16, 0:NT], w[:, k * 32 + 16 * x:k * 32 + 16 * x + 16], H[:, k, :], k == 0, k == 7)
                ins.then_inc(*to("gin_done", name))
            weight_used[("gin", 24)] = ("gin_done", "dt")
            for g, (first, n) in enumerate([(0, 4), (4, 3)]):
                ps = bank(pe, ("gtail", g), ("gtail_rows", g))
                for i in range(first, first + n):
                    a, b = (0, 96) if i == 0 else (96 + (i - 1) * P, 96 + i * P)
                    if i == 0:
                        pe.wait_ge(*at("gtail", 31))
                    ins = pe.transpose(ps[0:b - a, (i - first) * P:(i - first + 1) * P], TAILG[:, a:b], ident)
                ins.then_inc(*to("gtail_turned", g))
            ps = bank(pe, ("tok", 0), ("tok", 0))
            pe.wait_ge(*at("g_rows", 0))
            for c in range(3):
                n = P if c < 2 else 64
                for x, row in enumerate((0, 3, 4)):
                    ins = pe.transpose(ps[0:n, (c * 3 + x) * 16:(c * 3 + x) * 16 + 16], ROWS[:, row, c * P:c * P + n],
                                       ident[0:16, 0:16])
            ins.then_inc(*to("tok_turned", 0))
            for r, members in enumerate(g_in_round):
                kind = members[0][3]
                size = P if kind == "p" else 64
                t0 = 0 if kind == "p" else SEQ
                for n, _, u, _, i in members:
                    un = GUNIT[u]
                    for x in range(2 if kind == "p" else 4):
                        h = g_head(kind, i, 2 * x if kind == "p" else x)
                        sel = ident[0:16, h:h + 1].broadcast_to([16, P])
                        for what, row in (("gc", 3), ("bb", 0)):
                            ps = bank(pe, (what, n, x), (what, (n, x)))
                            cols = slice(0, SEQ) if kind == "p" else slice(SEQ, NT)
                            mm(pe, ps[:, cols], sel, ROWS[:, row, cols], True, True).then_inc(*to(what + "_done", (n, x)))
                    if r == 0 and u == 0:
                        pe.wait_ge(*at("qk_normed", 15))
                    ps = bank(pe, ("kq", n), ("kq_read", n))
                    if kind == "p":
                        for c in range(2):
                            cs = slice(c * P, c * P + P)
                            mm(pe, ps[:, c * P:c * P + P], QKV[:, 8 + i, cs], QKV[:, 8 + i, cs], True, True)
                            ins = mm(pe, ps[:, 256 + c * P:384 + c * P], QKV[:, 8 + i, cs], QKV[:, i, cs], True, True)
                    else:
                        for x in range(2):
                            hq = 2 * i + x
                            mm(pe, ps[0:64, x * 64:x * 64 + 64], QKV[:, 8 + hq, SEQ:NT], QKV[:, 8 + hq, SEQ:NT], True, True)
                            ins = mm(pe, ps[0:64, 256 + x * 64:320 + x * 64], QKV[:, 8 + hq, SEQ:NT], QKV[:, hq, SEQ:NT],
                                     True, True)
                    ins.then_inc(*to("kq_done", n))
                    ps = bank(pe, ("vt", n), ("vt", n))
                    for el in range(4):
                        c = slice((el % 2) * P, (el % 2) * P + P) if kind == "p" else slice(SEQ, NT)
                        ins = pe.transpose(ps[0:size, el * P:el * P + P], QKV[:, 16 + g_head(kind, i, el), c], ident)
                    ins.then_inc(*to("vt_done", n))
                    ps = bank(pe, ("kt", n), ("kt", n))
                    for x in range(2):
                        src = QKV[:, 8 + i, x * P:x * P + P] if kind == "p" else QKV[:, 8 + 2 * i + x, SEQ:NT]
                        ins = pe.transpose(ps[0:size, x * P:x * P + P], src, ident)
                    ins.then_inc(*to("kt_done", n))
                if kind == "s":
                    pe_states_read(pe, 4 * members[0][4])
                for lev in g_levels(kind):
                    for n, _, u, _, _ in members:
                        un = GUNIT[u]
                        pe.wait_ge(*at("goff", (n, lev)))
                        if lev:
                            pe.wait_ge(*at("ginv", (n, lev - 1)))
                        ps = bank(pe, ("gp", n, lev), ("gp", (n, lev)) if lev else ("ginv", (n, 0)))
                        for el in range(4):
                            ins = mm(pe, ps[0:size, el * P:el * P + size], un["off"][0:size, el, 0:size],
                                     un["inv"][0:size, el, 0:size] if lev else ident[0:size, 0:size], True, True)
                        ins.then_inc(*to("gpmm", (n, lev)))
                    if lev:
                        for n, _, u, _, _ in members:
                            un = GUNIT[u]
                            pe.wait_ge(*at("gp", (n, lev)))
                            for g in range(2):
                                ps = bank(pe, ("gimm", n, lev, g), ("ginv", (n, lev)))
                                for el in (2 * g, 2 * g + 1):
                                    o = (el % 2) * 256
                                    it = un["inv"][0:size, el, P:P + size]
                                    if lev < g_levels(kind)[-1]:
                                        mm(pe, ps[0:size, o:o + size], it, un["p"][0:size, el, 0:size], True, True)
                                    ins = mm(pe, ps[0:size, o + P:o + P + size], un["p"][0:size, el, 0:size], it, True, True)
                                ins.then_inc(*to("gimm", (n, lev, g)))
                if kind == "p":
                    for c in range(2):
                        for step in range(3):
                            for n, _, u, _, i in members:
                                un = GUNIT[u]
                                for x in range(2):
                                    h, el, s = 2 * i + x, 2 * x + c, 2 * u + x
                                    cs = slice(c * P, c * P + P)
                                    if step == 0 and c:
                                        pe.wait_ge(*at("g_state", (h, 0)))
                                        ps = bank(pe, ("ks", h), ("g_rhs", h))
                                        mm(pe, ps[:, 0:P], QKV[:, 8 + i, cs], GS[:, s, :], True, True)\
                                            .then_inc(*to("ks_done", h))
                                    if step == 1:
                                        if c == 0:
                                            pe.wait_ge(*at("ginv", (n, 6)))
                                            pe.wait_ge(*at("vt", n))
                                        else:
                                            pe.wait_ge(*at("g_rhs", h))
                                        ps = bank(pe, ("vn", h, c), ("vn", (h, c)))
                                        mm(pe, ps[:, 0:P], un["inv"][:, el, P:256], un["vb"][:, el, :] if c == 0 else GR[:, s, :],
                                           True, True).then_inc(*to("vn_done", (h, c)))
                                    if step == 2:
                                        pe.wait_ge(*at("vn", (h, c)))
                                        ps = bank(pe, ("go", h, c), ("go", (h, c)))
                                        if c:
                                            pe.wait_ge(*at("qg", (n, x)))
                                            mm(pe, ps[:, 0:P], GS[:, s, :], QG[:, s, cs], True, False)
                                        mm(pe, ps[:, 0:P], GV[:, s, :], un["aq"][:, el, :], not c, True)\
                                            .then_inc(*to("go_done", (h, c)))
                                        if c == 0:
                                            pe.wait_ge(*at("kt", n))
                                        ps = bank(pe, ("gmu", h, c), ("g_state", (h, c)))
                                        mm(pe, ps[:, 0:P], un["kg"][:, el, :], GV[:, s, :], True, True)\
                                            .then_inc(*to("g_mu", (h, c)))
                else:
                    n, _, _, _, i = members[0]
                    un = GUNIT[0]
                    for el in range(4):
                        h = 4 * i + el
                        if el < 3:
                            pe_states_read(pe, h + 1)
                        pe.wait_ge(*at("gs_rhs", h))
                        if el == 0:
                            pe.wait_ge(*at("ginv", (n, 2)))
                        ps = bank(pe, ("gvn", h), ("gs_vn", h))
                        mm(pe, ps[0:64, 0:P], un["inv"][0:64, el, P:P + 64], GR[0:64, h % 2, :], True, True)\
                            .then_inc(*to("gvn_done", h))
                        ps = bank(pe, ("gso", h), ("gs_o", h))
                        pe.wait_ge(*at("gs_z", h))
                        mm(pe, ps[:, 0:64], ZC[:, h % 2, :], ident[:, 64:128], True, False)
                        pe.wait_ge(*at("gs_vn", h))
                        mm(pe, ps[:, 0:64], GV[0:64, h % 2, :], un["aq"][0:64, el, 0:64], False, True)\
                            .then_inc(*to("gso_done", h))
                        pe.wait_ge(*at("kgm", h))
                        for g in range(2):
                            ps = bank(pe, ("gsm", h, g), ("gs_new", (h, g)))
                            for b in range(4):
                                ins = mm(pe, ps[:, b * P:b * P + P], KGM[h % 2][0:64, 4 * g + b, :], GV[0:64, h % 2, :],
                                         True, True)
                            ins.then_inc(*to("gs_mm", (h, g)))
            for h in range(16):
                ps = bank(pe, ("gn", h), ("gn_ln", h))
                pe.wait_ge(*at("go_sq", h))
                mm(pe, ps[:, 0:NT], ones, SQ[:, h % 4, :], True, True).then_inc(*to("go_summed", h))
            pe_out(pe, gq + 1, [[("gwo", c)] for c in range(8)], 16, lambda n: [("g_gated", n)], lambda n: Z[:, n, :])
            pe_norm(pe, gq + 1)

        def act_gdn(act, l):
            act_pre_norm(act, gq)
            act.wait_ge(*at("heads_in", 0))
            act.activation(AH[:, 2:3], AH[:, 0:1], ACT.Exp).then_inc(*to("exp_alog", 0))

            def e_minus(t):
                act.wait_ge(*at("gconv", t))
                if t >= 2:
                    act.wait_ge(*at("g_sig", t - 2))
                act.activation(EXG[:, t % 2, :], CVG[:, t % 2, :], ACT.Exp, scale=-1.0).then_inc(*to("g_e", t))
                act.wait_ge(*at("g_e", t))
                act.activation(EXG[:, t % 2, :], EXG[:, t % 2, :], ACT.Copy, bias=1.0).then_inc(*to("g_1e", t))

            for t in range(32):
                if t >= 4:
                    act.wait_ge(*at("gconv", t - 4))
                    act.wait_ge(*at("gtail", t - 4))
                act.wait_ge(*at("gin_done", t))
                ps = of(("gin", t))
                act.activation(XG[:, t % 4, 3:259], ps[:, 0:SEQ], ACT.Copy)
                act.activation(g_window(t % 4)[:, :, 3:11], sample(ps[:, SEQ:NT]), ACT.Copy).then_inc(*to("gxp", t))
                act.wait_ge(*at("gxp", t))
                act.wait_ge(*at("gxp_state", t))
                if t >= 2:
                    act.wait_ge(*at("gtap2", t - 2))
                act.activation(TAP3[:, t % 2, :], XG[:, t % 4, 3:347], ACT.Copy, scale=par("gdn_conv_w", 96 + t))\
                   .then_inc(*to("gtap3", t))
                if t:
                    e_minus(t - 1)
            e_minus(31)
            for t in range(32, 48):
                act.wait_ge(*at("gin_done", t))
                if t >= 34:
                    act.wait_ge(*at("z_1e", t - 2))
                act.activation(ZE[:, t % 2, :], of(("gin", t))[:, 0:NT], ACT.Exp, scale=-1.0)
                act.activation(Z[:, t - 32, :], of(("gin", t))[:, 0:NT], ACT.Copy).then_inc(*to("z_out", t))
                act.wait_ge(*at("g_silu", t - 32))
                act_square(act, t - 32, QKV[:, t - 32, :], ("l2_sq", t - 32), lambda n: ("l2_summed", n), 16)
                if t > 32:
                    l2_rstd(act, t - 33)
            l2_rstd(act, 15)
            act.wait_ge(*at("gin_done", "beta"))
            act.activation(ROWS[:, 0, :], of(("gin", "beta"))[0:16, 0:NT], ACT.Exp, scale=-1.0).then_inc(*to("g_e1", 0))
            act.wait_ge(*at("g_abs", 0))
            act.activation(ROWS[:, 2, :], ROWS[:, 2, :], ACT.Exp, scale=-1.0).then_inc(*to("g_sp", 0))
            act.wait_ge(*at("g_sp", 0))
            act.activation(ROWS[:, 2, :], ROWS[:, 2, :], ACT.Ln, bias=1.0).then_inc(*to("g_sp", 1))
            for g, n in ((0, 4), (1, 3)):
                act.wait_ge(*at("gtail_turned", g))
                act.activation(TOUTG[:, 4 * g:4 * g + n, :], of(("gtail", g))[:, 0:n * P], ACT.Copy)\
                   .then_inc(*to("gtail_rows", g))
            act.wait_ge(*at("gtail_rows", 1))
            act.dma_start(io["p_gdn_conv"][0, 0].rearrange("j (m p) -> (j m) p", p=P), TOUTG[0:96, 0, :])\
               .then_inc(*to("gtail_stored", 0, 16))
            rows = io["s_gdn_conv"][0].rearrange("b j (m p) -> (b j m) p", p=P)
            act.dma_start(rows.rearrange("(i r) p -> r i p", r=P), TOUTG[:, 1:7, :]).then_inc(*to("gtail_stored", 0, 16))
            act.wait_ge(*at("tok_turned", 0))
            ps = of(("tok", 0))
            for c in range(3):
                m = P if c < 2 else 64
                view = ps[0:m, c * 48:c * 48 + 48].rearrange("p (k h) -> p k h", k=3)
                act.activation(tokens3[0:m, c, 0:2, :], view[:, 0:2, :], ACT.Copy)
                act.activation(tokens3[0:m, c, T_EG, :], view[:, 1, :], ACT.Exp)
                ins = act.activation(tokens3[0:m, c, T_EGL, :], view[:, 2, :], ACT.Exp)
            ins.then_inc(*to("tok", 0))
            act.wait_ge(*at("gtail_stored", 0))
            for r, members in enumerate(g_in_round):
                kind = members[0][3]
                size = P if kind == "p" else 64
                for n, _, u, _, i in members:
                    un = GUNIT[u]
                    if r == 0 and u == 0:
                        act.wait_ge(*at("z_silu", 47))
                    if g_last(r, u):
                        act.wait_ge(*at(*g_last(r, u)))
                    if kind == "s" and r == 4:
                        act.wait_ge(*at("g_state", (15, 1)))
                    cols = slice(0, SEQ) if kind == "p" else slice(SEQ, NT)
                    for x in range(2 if kind == "p" else 4):
                        s = 2 * u + x
                        if r:
                            for step in g_rows_read(r, u, x):
                                act.wait_ge(*at(*step))
                        act.wait_ge(*at("gc_done", (n, x)))
                        act.activation(EG[:, s, cols], of(("gc", n, x))[:, cols], ACT.Exp)
                        act.activation(GCS[:, s, cols], of(("gc", n, x))[:, cols], ACT.Copy).then_inc(*to("gc", (n, x)))
                        act.wait_ge(*at("bb_done", (n, x)))
                        act.activation(BS[:, s, cols], of(("bb", n, x))[:, cols], ACT.Copy).then_inc(*to("bb", (n, x)))
                for n, _, u, _, i in members:
                    un = GUNIT[u]
                    act.wait_ge(*at("g_diff", n))
                    act.activation(un["p"][0:size, :, 0:size], un["p"][0:size, :, 0:size], ACT.Exp).then_inc(*to("g_decay", n))
                    act.wait_ge(*at("vt_done", n))
                    act.wait_ge(*at("tok", 0))
                    for el in range(4):
                        c, h = (el % 2, 2 * i + el // 2) if kind == "p" else (2, 4 * i + el)
                        ins = act.activation(un["vb"][0:size, el, :], of(("vt", n))[0:size, el * P:el * P + P], ACT.Copy,
                                             scale=tokens3[0:size, c, T_BETA, h:h + 1])
                    ins.then_inc(*to("vt", n))
                    act.wait_ge(*at("kt_done", n))
                    for el in range(4):
                        c, h = (el % 2, 2 * i + el // 2) if kind == "p" else (2, 4 * i + el)
                        x = el % 2 if kind == "p" else el // 2
                        ins = act.activation(un["kg"][0:size, el, :], of(("kt", n))[0:size, x * P:x * P + P], ACT.Copy,
                                             scale=tokens3[0:size, c, T_EGL, h:h + 1])
                    ins.then_inc(*to("kt", n))
                for lev in g_levels(kind):
                    if lev:
                        for n, _, u, _, _ in members:
                            act.wait_ge(*at("gpmm", (n, lev)))
                            if lev == 1:
                                act.wait_ge(*at("g_aq", n))
                            else:
                                act.wait_ge(*at("gimm", (n, lev - 1, 1)))
                            act.activation(GUNIT[u]["p"][0:size, :, 0:size],
                                           of(("gp", n, lev))[0:size, :].rearrange("p (a b) -> p a b", a=4)[:, :, 0:size],
                                           ACT.Copy).then_inc(*to("gp", (n, lev)))
                if kind == "p":
                    for c in range(2):
                        for n, _, u, _, i in members:
                            for x in range(2):
                                h, s = 2 * i + x, 2 * u + x
                                act.wait_ge(*at("vn_done", (h, c)))
                                if c == 0 and r:
                                    act.wait_ge(*at("g_mu", (h - 4, 1)))
                                if c == 1:
                                    act.wait_ge(*at("g_mu", (h, 0)))
                                act.activation(GV[:, s, :], of(("vn", h, c))[:, 0:P], ACT.Copy).then_inc(*to("vn", (h, c)))
                        for n, _, u, _, i in members:
                            for x in range(2):
                                h = 2 * i + x
                                act.wait_ge(*at("go_done", (h, c)))
                                act.activation(QKV[:, 16 + h, c * P:c * P + P], of(("go", h, c))[:, 0:P], ACT.Copy)\
                                   .then_inc(*to("go", (h, c)))
                    for n, _, u, _, i in members:
                        for x in range(2):
                            h, s = 2 * i + x, 2 * u + x
                            act.wait_ge(*at("g_state", (h, 1)))
                            act.dma_start(io["p_gdn_S"][0, 0, h], GS[:, s, :]).then_inc(*to(f"gps_stored{s}", h, 16))
                else:
                    i = members[0][4]
                    for el in range(4):
                        h = 4 * i + el
                        act.wait_ge(*at("gvn_done", h))
                        if h >= 2:
                            act.wait_ge(*at("gs_mm", (h - 2, 1)))
                        act.activation(GV[0:64, h % 2, :], of(("gvn", h))[0:64, 0:P], ACT.Copy).then_inc(*to("gs_vn", h))
                        act.wait_ge(*at("gso_done", h))
                        act.activation(QKV[:, 16 + h, SEQ:NT], of(("gso", h))[:, 0:64], ACT.Copy).then_inc(*to("gs_o", h))
            act.wait_ge(*at("gs_o", 15))
            act.wait_ge(*at("gs_mm", (15, 1)))
            for h in range(16):
                act_square(act, h, QKV[:, 16 + h, :], ("go_sq", h), lambda n: ("go_summed", n), 16)
                if h:
                    gn_rstd(act, h - 1)
            gn_rstd(act, 15)
            for h in (12, 13, 14, 15):
                act.wait_ge(*at(f"gs_out{h % 4}", h))
            for s in range(4):
                act.wait_ge(*at(f"gps_stored{s}", 12 + s))
            act_outputs(act, gq + 1)

        def g_rows_read(r, u, x):
            if r <= 3:
                n, _, _, kind, i = g_in_round[r - 1][u]
                h = 2 * i + x
                return [("g_am", n), ("g_state", (h, 1))]
            if r == 4:
                return [("g_state", (15, 1)), ("g_am", 7)]
            n, _, _, kind, i = g_in_round[r - 1][0]
            return [("g_am", n), ("gs_new", (4 * i + 3, 1)), ("km", 4 * i + 3)]

        def l2_rstd(act, t):
            act.wait_ge(*at("l2_summed", t))
            if t:
                act.wait_ge(*at("l2_rstd", t - 1))
            act.activation(halves[0][:, 0:NT], of(("l2", t))[:, 0:NT], ACT.Ln, bias=EB[:, 0:1]).then_inc(*to("l2_ln", t))
            act.wait_ge(*at("l2_ln", t))
            if t:
                act.wait_ge(*at("qk_normed", t - 1))
            act.activation(halves[0][:, NT:2 * NT], halves[0][:, 0:NT], ACT.Exp, scale=-0.5).then_inc(*to("l2_rstd", t))

        def gn_rstd(act, h):
            act.wait_ge(*at("go_summed", h))
            if h:
                act.wait_ge(*at("gn_rstd", h - 1))
                act.wait_ge(*at("g_n1", h - 1))
            act.activation(RS[:, 0, :], of(("gn", h))[:, 0:NT], ACT.Ln, bias=EB[:, 0:1], scale=1.0 / P).then_inc(*to("gn_ln", h))
            act.wait_ge(*at("gn_ln", h))
            act.activation(RS[:, 1, :], RS[:, 0, :], ACT.Exp, scale=-0.5).then_inc(*to("gn_rstd", h))

        def dve_states_read(dve, n, el, h):
            dve.wait_ge(*at("gks_done", h))
            dve.wait_ge(*at("vt", n))
            if h >= 2:
                dve.wait_ge(*at("gvn_done", h - 2))
            ps = of(("gks", h))[:, 0:P]
            dve.tensor_tensor(GR[0:64, h % 2, :], GUNIT[0]["vb"][0:64, el, :], ps[0:64], ALU.subtract)\
               .then_inc(*to("gs_rhs", h))
            if h >= 2:
                dve.wait_ge(*at("gso_done", h - 2))
            dve.tensor_copy(ZC[:, h % 2, :], ps).then_inc(*to("gs_z", h))
            for g in range(2):
                part = SGS[h % 4][g]
                gl = EG[:, el, SEQ + 7 + 32 * g:SEQ + 32 * g + 32:8].unsqueeze(2).broadcast_to([P, 4, P])
                dve.tensor_tensor(part, part, gl, ALU.mult).then_inc(*to("gs_scaled", (h, g)))

        def dve_gdn(dve, l):
            dve_pre_norm(dve, gq)

            def silu(t):
                p = t % 2
                dve.wait_ge(*at("g_1e", t))
                if t:
                    dve.wait_ge(*at("g_silu", t - 1))
                dve.reciprocal(GDG[:, 1, :], EXG[:, p, :]).then_inc(*to("g_sig", t))
                dve.wait_ge(*at("g_sig", t))
                dve.tensor_tensor(QKV[:, t, 0:SEQ], CVG[:, p, 0:SEQ], GDG[:, 1, 0:SEQ], ALU.mult)
                win = [v.rearrange("p (b w) -> p b w", b=DEC)[:, :, 3:11] for v in (CVG[:, p, 256:344], GDG[:, 1, 256:344])]
                dve.tensor_tensor(sample(QKV[:, t, SEQ:NT]), win[0], win[1], ALU.mult).then_inc(*to("g_silu", t))

            def l2_scale(t):
                dve.wait_ge(*at("l2_rstd", t))
                dve.scalar_tensor_tensor(out=QKV[:, t, :], in0=QKV[:, t, :], scalar=float(P ** -0.5) if t < 8 else 1.0,
                                         in1=halves[0][:, NT:2 * NT], op0=ALU.mult, op1=ALU.mult)\
                   .then_inc(*to("qk_normed", t))

            for t in range(32):
                w = lambda tap: par("gdn_conv_w", tap * 32 + t)
                x = XG[:, t % 4, :]
                dve.wait_ge(*at("gxp", t))
                dve.wait_ge(*at("gxp_state", t))
                if t:
                    dve.wait_ge(*at("gconv", t - 1))
                dve.wait_ge(*at("gtap3", t))
                dve.scalar_tensor_tensor(out=CTG[:, 1, :], in0=x[:, 2:346], scalar=w(2), in1=TAP3[:, t % 2, :],
                                         op0=ALU.mult, op1=ALU.add).then_inc(*to("gtap2", t))
                dve.wait_ge(*at("gtap2", t))
                dve.scalar_tensor_tensor(out=CTG[:, 0, :], in0=x[:, 1:345], scalar=w(1), in1=CTG[:, 1, :],
                                         op0=ALU.mult, op1=ALU.add).then_inc(*to("gtap1", t))
                dve.wait_ge(*at("gtap1", t))
                if t >= 2:
                    dve.wait_ge(*at("g_silu", t - 2))
                dve.scalar_tensor_tensor(out=CVG[:, t % 2, :], in0=x[:, 0:344], scalar=w(0), in1=CTG[:, 0, :],
                                         op0=ALU.mult, op1=ALU.add).then_inc(*to("gconv", t))
                if t:
                    silu(t - 1)
            silu(31)
            for t in range(32, 48):
                dve.wait_ge(*at("z_out", t))
                dve.tensor_scalar(ZE[:, t % 2, :], ZE[:, t % 2, :], 1.0, None, ALU.add).then_inc(*to("z_add", t))
                dve.wait_ge(*at("z_add", t))
                dve.reciprocal(ZE[:, t % 2, :], ZE[:, t % 2, :]).then_inc(*to("z_rec", t))
                dve.wait_ge(*at("z_rec", t))
                dve.tensor_tensor(Z[:, t - 32, :], Z[:, t - 32, :], ZE[:, t % 2, :], ALU.mult).then_inc(*to("z_1e", t))
                if t > 32:
                    l2_scale(t - 33)
            l2_scale(15)
            dve.wait_ge(*at("z_1e", 47))
            R = lambda k: ROWS[:, k, :]
            dve.wait_ge(*at("gin_done", "dt"))
            dve.tensor_scalar(R(1), of(("gin", "dt"))[0:16, 0:NT], AH[:, 1:2], None, ALU.add).then_inc(*to("g_t", 0))
            dve.wait_ge(*at("g_t", 0))
            dve.scalar_tensor_tensor(out=R(2), in0=R(1), scalar=-1.0, in1=R(1), op0=ALU.mult, op1=ALU.max)\
               .then_inc(*to("g_abs", 0))
            dve.wait_ge(*at("g_e1", 0))
            dve.tensor_scalar(R(0), R(0), 1.0, None, ALU.add).then_inc(*to("g_r", 0))
            dve.wait_ge(*at("g_r", 0))
            dve.reciprocal(R(0), R(0)).then_inc(*to("g_r", 1))
            dve.wait_ge(*at("g_sp", 1))
            dve.scalar_tensor_tensor(out=R(1), in0=R(1), scalar=0.0, in1=R(2), op0=ALU.max, op1=ALU.add)\
               .then_inc(*to("g_r", 2))
            dve.wait_ge(*at("g_r", 2))
            dve.wait_ge(*at("exp_alog", 0))
            dve.tensor_scalar(R(1), R(1), AH[:, 2:3], -1.0, ALU.mult, ALU.mult).then_inc(*to("g_r", 3))
            dve.wait_ge(*at("g_r", 3))
            dve.tensor_tensor_scan(R(3), const("seg128")[0:16, :], R(1), 0.0, ALU.mult, ALU.add).then_inc(*to("g_r", 4))
            dve.wait_ge(*at("g_r", 4))
            pr = R(3)[:, 0:SEQ].rearrange("p (c t) -> p c t", c=2)
            dve.tensor_tensor(R(4)[:, 0:SEQ].rearrange("p (c t) -> p c t", c=2),
                              pr[:, :, P - 1:P].broadcast_to([16, 2, P]), pr, ALU.subtract)
            sm = sample(R(3)[:, SEQ:NT])
            dve.tensor_tensor(sample(R(4)[:, SEQ:NT]), sm[:, :, 7:8].broadcast_to([16, DEC, 8]), sm, ALU.subtract)\
               .then_inc(*to("g_rows", 0))
            dve.wait_ge(*at("tok", 0))
            for c in range(3):
                m = P if c < 2 else 64
                ins = dve.scalar_tensor_tensor(out=tokens3[0:m, c, T_NBE, :], in0=tokens3[0:m, c, T_BETA, :], scalar=-1.0,
                                               in1=tokens3[0:m, c, T_EG, :], op0=ALU.mult, op1=ALU.mult)
            ins.then_inc(*to("g_nbe", 0))
            dve.sem_inc(*to("z_silu", 47))
            for r, members in enumerate(g_in_round):
                kind = members[0][3]
                size = P if kind == "p" else 64
                for n, _, u, _, i in members:
                    un = GUNIT[u]
                    if n == 0:
                        dve.wait_ge(*at("gtail_stored", 0))
                    if g_last(r, u):
                        dve.wait_ge(*at(*g_last(r, u)))
                    if kind == "s" and r == 4:
                        dve.wait_ge(*at("g_mu", (15, 1)))
                    for el in range(4):
                        x = el // 2 if kind == "p" else el
                        c, h = (el % 2, 2 * i + el // 2) if kind == "p" else (2, 4 * i + el)
                        dve.wait_ge(*at("gc", (n, x)))
                        ins = dve.tensor_scalar(un["p"][0:size, el, 0:size], GCS[0:size, 2 * u + x, c * P:c * P + size],
                                                tokens3[0:size, c, T_GC, h:h + 1], 0.0, ALU.subtract, ALU.min)
                    ins.then_inc(*to("g_diff", n))
                for n, _, u, _, i in members:
                    un = GUNIT[u]
                    dve.wait_ge(*at("g_decay", n))
                    dve.wait_ge(*at("kq_done", n))
                    kq = of(("kq", n))
                    def both(o):
                        if kind == "p":
                            return kq[:, o:o + 256].rearrange("p (c t) -> p c t", c=2).unsqueeze(1).broadcast_to([P, 2, 2, P])
                        return kq[0:64, o:o + 128].rearrange("p (q t) -> p q t", q=2).unsqueeze(2).broadcast_to([64, 2, 2, 64])
                    four = lambda v: v[0:size, :, 0:size].rearrange("p (a b) t -> p a b t", a=2)
                    if kind == "s":
                        mask = const("gincl_s")[0:64]
                    else:
                        mask = const("gincl")
                    dve.tensor_tensor(four(un["am"]), both(0), four(un["p"]), ALU.mult).then_inc(*to("g_am1", n))
                    dve.tensor_tensor(four(un["aq"]), both(256), four(un["p"]), ALU.mult).then_inc(*to("kq_read", n))
                    for x in range(2 if kind == "p" else 4):
                        dve.wait_ge(*at("bb", (n, x)))
                    if kind == "p":
                        am, beta = un["am"].rearrange("p (x c) t -> p x (c t)", x=2), BS[:, 2 * u:2 * u + 2, 0:SEQ]
                    else:
                        am, beta = un["am"][0:64, :, 0:64], BS[0:64, :, SEQ:NT]
                    dve.wait_ge(*at("g_am1", n))
                    dve.scalar_tensor_tensor(out=am, in0=am, scalar=-1.0, in1=beta, op0=ALU.mult, op1=ALU.mult)\
                       .then_inc(*to("g_am", n))
                    dve.wait_ge(*at("kq_read", n))
                    dve.tensor_tensor(un["aq"][0:size, :, 0:size], un["aq"][0:size, :, 0:size],
                                      mask.unsqueeze(1).broadcast_to([size, 4, size]), ALU.mult).then_inc(*to("g_aq", n))
                    if kind == "p":
                        for x in range(2):
                            dve.tensor_tensor(QG[:, 2 * u + x, P:SEQ], QKV[:, i, P:SEQ], EG[:, 2 * u + x, P:SEQ], ALU.mult)\
                               .then_inc(*to("qg", (n, x)))
                if kind == "s":
                    dve_states_read(dve, members[0][0], 0, 4 * members[0][4])
                for lev in g_levels(kind):
                    for n, _, u, _, _ in members:
                        un = GUNIT[u]
                        inv = un["inv"][0:size].rearrange("p a (x t) -> p a x t", x=2)[:, :, :, 0:size]
                        if lev == 0:
                            idb = ident[0:size, 0:size].unsqueeze(1).broadcast_to([size, 4, size])
                            dve.wait_ge(*at("gpmm", (n, 0)))
                            dve.tensor_tensor(inv[:, :, 0], of(("gp", n, 0))[0:size, :].rearrange("p (a b) -> p a b", a=4)
                                              [:, :, 0:size], idb, ALU.add)
                            dve.tensor_tensor(inv[:, :, 1], un["off"][0:size, :, 0:size], idb, ALU.add)\
                               .then_inc(*to("ginv", (n, 0)))
                        else:
                            dve.wait_ge(*at("ginv", (n, lev - 1)))
                            for g in range(2):
                                dve.wait_ge(*at("gimm", (n, lev, g)))
                                src = of(("gimm", n, lev, g))[0:size, :].rearrange("p (a x t) -> p a x t", a=2, x=2)
                                first = 1 if lev == g_levels(kind)[-1] else 0
                                part = inv[:, 2 * g:2 * g + 2, first:2]
                                ins = dve.tensor_tensor(part, part, src[:, :, first:2, 0:size], ALU.add)
                            ins.then_inc(*to("ginv", (n, lev)))
                if kind == "p":
                    for c in range(2):
                        if c:
                            for n, _, u, _, i in members:
                                for x in range(2):
                                    h, s = 2 * i + x, 2 * u + x
                                    dve.wait_ge(*at("ks_done", h))
                                    dve.wait_ge(*at("g_nbe", 0))
                                    dve.scalar_tensor_tensor(out=GR[:, s, :], in0=of(("ks", h))[:, 0:P],
                                                             scalar=tokens3[:, 1, T_NBE, h:h + 1],
                                                             in1=GUNIT[u]["vb"][:, 2 * x + 1, :], op0=ALU.mult, op1=ALU.add)\
                                       .then_inc(*to("g_rhs", h))
                        for n, _, u, _, i in members:
                            for x in range(2):
                                h, s = 2 * i + x, 2 * u + x
                                dve.wait_ge(*at("g_mu", (h, c)))
                                if c == 0:
                                    if r:
                                        dve.wait_ge(*at(f"gps_stored{s}", h - 4))
                                    ins = dve.tensor_copy(GS[:, s, :], of(("gmu", h, c))[:, 0:P])
                                else:
                                    ins = dve.scalar_tensor_tensor(out=GS[:, s, :], in0=GS[:, s, :],
                                                                   scalar=EG[:, s, SEQ - 1:SEQ], in1=of(("gmu", h, c))[:, 0:P],
                                                                   op0=ALU.mult, op1=ALU.add)
                                ins.then_inc(*to("g_state", (h, c)))
                else:
                    i = members[0][4]
                    for el in range(4):
                        h = 4 * i + el
                        if el < 3:
                            dve_states_read(dve, members[0][0], el + 1, h + 1)
                        for g in range(2):
                            part = SGS[h % 4][g]
                            dve.wait_ge(*at("gs_scaled", (h, g)))
                            dve.wait_ge(*at("gs_mm", (h, g)))
                            dve.tensor_tensor(part, part, of(("gsm", h, g)).rearrange("p (b v) -> p b v", b=4), ALU.add)\
                               .then_inc(*to("gs_new", (h, g)))
            for h in range(16):
                t = PS[:, h % 2, :]
                dve.wait_ge(*at("gn_rstd", h))
                dve.scalar_tensor_tensor(out=t, in0=QKV[:, 16 + h, :], scalar=par("gdn_norm_w", 0), in1=RS[:, 1, :],
                                         op0=ALU.mult, op1=ALU.mult).then_inc(*to("g_n1", h))
                dve.wait_ge(*at("g_n1", h))
                dve.tensor_tensor(Z[:, h, :], t, Z[:, h, :], ALU.mult).then_inc(*to("g_gated", h))
            dve.wait_ge(*at("g_gated", 15))
            dve_post_norm(dve, gq + 1)

        def pool_factors(pool, n, el, h):
            if h >= 2:
                pool.wait_ge(*at("gks_done", h - 2))
            pool.wait_ge(*at("gc", (n, el)))
            kq = KQM[h % 2].rearrange("p (b w) -> p b w", w=136)
            eg = sample(EG[:, el, SEQ:NT])
            pool.tensor_tensor(kq[:, :, 0:8], sample(QKV[:, 8 + h // 2, SEQ:NT]), eg, ALU.mult).then_inc(*to("km1", h))
            pool.tensor_tensor(kq[:, :, 64:72], sample(QKV[:, h // 2, SEQ:NT]), eg, ALU.mult)
            pool.wait_ge(*at("km1", h))
            pool.wait_ge(*at("bb", (n, el)))
            pool.tensor_tensor(kq[:, :, 0:8], kq[:, :, 0:8], sample(BS[:, el, SEQ:NT]), ALU.mult).then_inc(*to("km", h))
            if h >= 2:
                pool.wait_ge(*at("gs_mm", (h - 2, 1)))
            pool.wait_ge(*at("kt", n))
            pool.tensor_tensor(KGM[h % 2][0:64], GUNIT[0]["kg"][0:64, el, :].unsqueeze(1).broadcast_to([64, DEC, P]),
                               const("batch8")[0:64].unsqueeze(2).broadcast_to([64, DEC, P]), ALU.mult)\
                .then_inc(*to("kgm", h))

        def pool_gdn(pool, l):
            pool.wait_ge(*at("rstd", gq))
            for i in range(2):
                pool.memset(KQM[i], 0.0)
            pool.memset(XG[:, :, 0:3], 0.0)
            for t in range(32):
                if t >= 4:
                    pool.wait_ge(*at("gconv", t - 4))
                st = gdn_state[:, :].rearrange("p (b j m) -> p b j m", b=DEC, j=3)[:, :, :, t]
                pool.tensor_copy(g_window(t % 4)[:, :, 0:3], st).then_inc(*to("gxp_state", t))
                pool.wait_ge(*at("gxp", t))
                pool.tensor_copy(tailg_p[:, :, t], XG[:, t % 4, 256:259])
                pool.tensor_copy(tailg_s[:, :, :, t], g_window(t % 4)[:, :, 8:11]).then_inc(*to("gtail", t))
            for r, members in enumerate(g_in_round):
                kind = members[0][3]
                size = P if kind == "p" else 64
                if kind == "s":
                    if r == 4:
                        pool.wait_ge(*at("g_mu", (15, 1)))
                    pool_factors(pool, members[0][0], 0, 4 * members[0][4])
                for lev in g_levels(kind):
                    for n, _, u, _, _ in members:
                        un = GUNIT[u]
                        pool.wait_ge(*at("g_am", n))
                        if lev:
                            pool.wait_ge(*at("gpmm", (n, lev - 1)))
                            if lev == 1:
                                pool.wait_ge(*at("ginv", (n, 0)))
                        pool.tensor_tensor(un["off"][0:size, :, 0:size], un["am"][0:size, :, 0:size],
                                           const(f"lev{lev}")[0:size, 0:size].unsqueeze(1).broadcast_to([size, 4, size]),
                                           ALU.mult).then_inc(*to("goff", (n, lev)))
                if kind == "s":
                    for el in range(1, 4):
                        pool_factors(pool, members[0][0], el, 4 * members[0][4] + el)

        ma = {"n": 0}

        def take(*dims):
            o = ma["n"]
            ma["n"] += int(np.prod(dims))
            return arena(o, *dims)

        CM = take(MLA_CONST.shape[1])

        def mla_const(name, a=0, b=None):
            off, n = MLA_CONST_AT[name]
            return CM[:, off + a:off + (n if b is None else b)]

        LT = take(2, NT)
        KR = take(NT)
        o_qn = ma["n"]
        QN = take(8, NT)
        OLS = arena(o_qn, 2, MH, 64)
        QR = take(4, NT)
        QLS = take(2, DEC, P)
        QRS = take(DEC, P)
        CTOK = take(3, LAT + ROPE)
        VT = take(8, NT)
        o_r1 = ma["n"]
        CQ = take(4, NT)
        UKT = take(8, LAT)
        PSB = arena(o_r1, PAGE * PAGES + 64)
        OL = arena(o_r1 + PAGE * PAGES + 64, LAT)
        o_r2 = ma["n"]
        VTOK = take(2, D)
        PPR = take(3, 384)
        PTP = take(2, 384)
        RT = arena(o_r2 + 2 * D, 2, NT)
        PTS = arena(o_r2, 17, P)
        PGS = take(2, PAGES, LAT)
        PGR = take(2, PAGES * ROPE)
        KN = H[:, :, :].rearrange("p m t -> p (m t)")[:, 0:8 * SEQ].rearrange("p (a t) -> p a t", a=8)
        CTB = [halves[1][:, 0:1024], SMALL[:, 0:1024]]
        RTB = [halves[0][:, 0:512], SMALL[:, 1024:1536]]
        MSUM = SMALL[:, 1536:1548].rearrange("p (s n) -> p s n", s=3)
        MMAX = SMALL[:, 1548:1560].rearrange("p (s n) -> p s n", s=3)
        SMX, SSM, SNM, SRC = SMALL[:, 1560:1565], SMALL[:, 1568:1573], SMALL[:, 1576:1578], SMALL[:, 1580:1582]
        mq = 4
        NPAST = PAGE * PAGES

        def mla_events():
            yield "turn", 0
            for n in range(4 * DEC):
                b, g = divmod(n, 4)
                if g or n == 0:
                    yield "turn", n + 1
                yield "score", n
                if g == 0:
                    if b:
                        yield "out", b - 1
                    yield "new", b
                if g == 3:
                    yield "weigh", b
                    yield "turn", n + 2
                    if b < DEC - 1:
                        yield "score", n + 1
                    yield "values", b
            yield "out", DEC - 1

        def mla_order():
            done = set()
            for kind, n in mla_events():
                if (kind, n) in done or kind == "turn" and n >= 4 * DEC:
                    continue
                done.add((kind, n))
                yield kind, n

        def sp_pages(sp, b):
            if b == 0:
                sp.wait_ge(*at("rstd", mq))
                sp.wait_ge(*at("pages_in", 0))
            pages = [sp.value_load(PG[0:1, i:i + 1], min_val=0, max_val=POOL - 1)
                     for i in range(b * PAGES, (b + 1) * PAGES)]
            if b >= 2:
                sp.wait_ge(*at("s_values", b - 2))
            for j, page in enumerate(pages):
                sp.dma_start(PGS[:, b % 2, j, :], io["cache_mla_latent"][0][bass.ds(page, 1), :, :]
                             .rearrange("a p c -> (a p) c")).then_inc(*to(f"page{b % 2}", b, 16))

        def pe_mla(pe, l):
            pe_norm(pe, mq)
            for m in range(7):
                key = ("min", m // 2)
                w = W[:, weight(pe, key), :]
                ps = bank(pe, ("min", m), ("min_raw", m))
                for k in range(MT):
                    if m == 0:
                        pe.wait_ge(*at("h", (mq, k)))
                    if m < 6:
                        lhsT = w[:, k * 256 + (m % 2) * P:k * 256 + (m % 2) * P + P]
                    else:
                        lhsT = w[:, k * P:k * P + P]
                    ins = mm(pe, ps[:, 0:NT], lhsT, H[:, k, :], k == 0, k == 7)
                ins.then_inc(*to("min_done", m))
                weight_used[key] = ("min_done", m)
            ps = bank(pe, ("ln", "q"), ("mla_ln", "q"))
            for m in range(4):
                pe.wait_ge(*at("mla_sq", m))
                mm(pe, ps[:, 0:NT], ones, SQ[:, m % 4, :], m == 0, m == 3).then_inc(*to("mla_summed", m))
            ps = bank(pe, ("ln", "c"), ("mla_ln", "c"))
            for m in range(4, 6):
                pe.wait_ge(*at("mla_sq", m))
                mm(pe, ps[:, 0:NT], ones, SQ[:, m % 4, :], m == 4, m == 5).then_inc(*to("mla_summed", m))
            ps = bank(pe, ("swap", "k"), ("rot_s", "k"))
            pe.wait_ge(*at("const_mla", 0))
            pe.wait_ge(*at("min_raw", 6))
            mm(pe, ps[:, 0:NT], mla_const("swap"), KR, True, True).then_inc(*to("swapped", "k"))
            for c in range(4):
                w = W[:, weight(pe, ("qb", c)), :]
                for j in range(3):
                    ps = bank(pe, ("q", c, j), ("q_raw", (c, j)))
                    for k in range(4):
                        if c == 0 and j == 0:
                            pe.wait_ge(*at("cq", k))
                        lhsT = w[:, k * 384 + j * P:k * 384 + j * P + P]
                        ins = mm(pe, ps[:, 0:NT], lhsT, CQ[:, k, :], k == 0, k == 3)
                    ins.then_inc(*to("q_done", (c, j)))
                weight_used[("qb", c)] = ("q_done", (c, 2))
            for c in range(4):
                ps = bank(pe, ("swap", c), ("rot_s", c))
                pe.wait_ge(*at("q_raw", (c, 2)))
                mm(pe, ps[:, 0:NT], mla_const("swap"), QR[:, c, :], True, True).then_inc(*to("swapped", c))
            w = W[:, weight(pe, ("uk",)), :]
            for g in range(4):
                ps = bank(pe, ("kn", g), ("kn", g))
                for j in range(2):
                    a = 2 * g + j
                    for ct in range(2):
                        if g == 0 and j == 0:
                            pe.wait_ge(*at("c", ct))
                        ins = mm(pe, ps[:, j * SEQ:(j + 1) * SEQ], w[:, ct * D + a * P:ct * D + a * P + P],
                                 LT[:, ct, 0:SEQ], ct == 0, ct == 1)
                ins.then_inc(*to("kn_done", g))
            for g in range(4):
                ps = bank(pe, ("ukt", g), ("ukt", g))
                for j in range(2):
                    for ct in range(2):
                        a = 2 * g + j
                        ins = pe.transpose(ps[:, j * 256 + ct * P:j * 256 + ct * P + P],
                                           w[:, ct * D + a * P:ct * D + a * P + P], ident)
                ins.then_inc(*to("ukt_done", g))
            weight_used[("uk",)] = ("ukt_done", 3)
            for t in range(3):
                n = P if t < 2 else 64
                ps = bank(pe, ("ctok", t), ("ctok", t))
                for ct in range(2):
                    pe.transpose(ps[0:n, ct * P:ct * P + P], LT[:, ct, t * P:t * P + n], ident)
                if t == 0:
                    pe.wait_ge(*at("rot", "k"))
                pe.transpose(ps[0:n, 256:288], KR[0:32, t * P:t * P + n], ident[0:32, 0:32]).then_inc(*to("ctok_done", t))
            w = W[:, weight(pe, ("uv",)), :]
            for t in range(2):
                for g in range(2):
                    ps = bank(pe, ("v", t, g), ("vtok", (t, g)))
                    for ct in range(2):
                        ins = mm(pe, ps[:, :], LT[:, ct, t * P:t * P + P], w[:, ct * D + g * 512:ct * D + g * 512 + 512],
                                 ct == 0, ct == 1)
                    ins.then_inc(*to("v_done", (t, g)))
            for g in range(4):
                ps = bank(pe, ("ql", g), ("ql", g))
                if g == 0:
                    pe.wait_ge(*at("ukt", 3))
                for j in range(4):
                    h = 8 * (g // 2) + 2 * j + g % 2
                    rows = slice(64 * (h % 2), 64 * (h % 2) + 64)
                    pe.wait_ge(*at("q_raw", (h // 4, (h // 2) % 2)))
                    for ct in range(2):
                        ins = mm(pe, ps[:, j * P + ct * 64:j * P + ct * 64 + 64], UKT[rows, h // 2, ct * P:ct * P + P],
                                 QN[rows, h // 2, SEQ:NT], True, True)
                ins.then_inc(*to("ql_done", g))
            for g in range(2):
                ps = bank(pe, ("qrs", g), ("qrs", g))
                for j in range(8):
                    h = 8 * g + j
                    if h % 4 == 0:
                        pe.wait_ge(*at("rot", h // 4))
                    sel = mla_const("spread", P * (h % 4), P * (h % 4) + P)
                    ins = mm(pe, ps[:, j * 64:j * 64 + 64], sel, QR[:, h // 4, SEQ:NT], True, True)
                ins.then_inc(*to("qrs_done", g))
            for i in range(MH + 3):
                if i < MH:
                    h = i
                    ps = bank(pe, ("ps", h), ("p_exp", h))
                    if h == 0:
                        pe.wait_ge(*at("kn", 3))
                    nope, rot = slice(64 * (h % 2), 64 * (h % 2) + 64), slice(32 * (h % 4), 32 * (h % 4) + 32)
                    for qb, cols in ((0, slice(0, P)), (1, slice(P, 384))):
                        qs = slice(qb * P, qb * P + P)
                        ks = slice(0, P * (qb + 1))
                        mm(pe, ps[:, cols], QN[nope, h // 2, qs], KN[nope, h // 2, ks], True, False)
                        ins = mm(pe, ps[:, cols], QR[rot, h // 4, qs], KR[rot, ks], False, True)
                    ins.then_inc(*to("ps_done", h))
                if 2 <= i < MH + 2:
                    h = i - 2
                    ps = bank(pe, ("pt", h), ("pt", h))
                    pe.wait_ge(*at("p_norm", h))
                    for j in range(3):
                        ins = pe.transpose(ps[:, j * P:j * P + P], PPR[:, h % 3, j * P:j * P + P], ident)
                    ins.then_inc(*to("pt_done", h))
                if i >= 3:
                    h = i - 3
                    if h % 2 == 0:
                        ps_v = bank(pe, ("po", h // 2), ("po", h // 2))
                    rows = slice(64 * (h % 2), 64 * (h % 2) + 64)
                    if h == 0:
                        pe.wait_ge(*at("vtok", (1, 1)))
                    pe.wait_ge(*at("pt", h))
                    mm(pe, ps_v[rows, 0:SEQ], VTOK[:, 0, h * 64:h * 64 + 64], PTP[:, h % 2, 0:SEQ], True, False)
                    mm(pe, ps_v[rows, P:SEQ], VTOK[:, 1, h * 64:h * 64 + 64], PTP[:, h % 2, SEQ:384], False, True)\
                        .then_inc(*to("po_done", h))
            moving = {"n": 0}

            def moving_bank(key, *read_by):
                moving["n"] += 1
                return bank(pe, key, *read_by, which=5 + moving["n"] % 3)

            pe.wait_ge(*at("ql", 3))
            pe.wait_ge(*at("qrs", 1))
            pe.wait_ge(*at("ctok", 2))
            for kind, n in mla_order():
                b, g = divmod(n, 4) if kind in ("turn", "score") else (n, 0)
                cT = CTB[n % 2]
                if kind == "turn":
                    if g == 0:
                        pe.wait_ge(*at(f"page{b % 2}", b))
                        pe.wait_ge(*at(f"rope{b % 2}", b))
                    for ct in range(2):
                        ps = moving_bank(("turn", n, ct), ("c_turned_a" if ct == 0 else "c_turned", (n, ct)))
                        for j in range(4):
                            ins = pe.transpose(ps[:, j * P:j * P + P], PGS[:, b % 2, 4 * g + j, ct * P:ct * P + P], ident)
                        ins.then_inc(*to("turn_done", (n, ct)))
                    ps = moving_bank(("turn", n, 2), ("c_turned", (n, 2)))
                    pe.transpose(ps[:, 0:P], PGR[:, b % 2, g * P:g * P + P], ident).then_inc(*to("turn_done", (n, 2)))
                elif kind == "score":
                    ps = bank(pe, ("score", b, g), ("s_exp", (b, g)), which=g)
                    for ct in range(2):
                        pe.wait_ge(*at("c_turned_a" if ct == 0 else "c_turned", (n, ct)))
                        mm(pe, ps, QLS[:, ct, b, :], cT[:, ct * 512:ct * 512 + 512], ct == 0, False)
                    pe.wait_ge(*at("c_turned", (n, 2)))
                    mm(pe, ps, QRS[:, b, :], RTB[n % 2], False, True).then_inc(*to("score_done", (b, g)))
                elif kind == "new":
                    ps = bank(pe, ("score", b, 4), ("s_exp", (b, 4)), which=4)
                    for ct in range(2):
                        mm(pe, ps[:, 0:64], QLS[:, ct, b, :], LT[:, ct, SEQ:NT], ct == 0, False)
                    mm(pe, ps[:, 0:64], QRS[0:32, b, :], KR[0:32, SEQ:NT], False, True).then_inc(*to("score_done", (b, 4)))
                elif kind == "values":
                    for g in range(5):
                        ps = moving_bank(("sp", b, g), (sp_name(g), (b, g)))
                        pe.wait_ge(*at("s_exp", (b, g)))
                        if g < 4:
                            for j in range(4):
                                k = 4 * g + j
                                ins = pe.transpose(ps[:, j * P:j * P + P], PSB[:, k * P:k * P + P], ident)
                        else:
                            ins = pe.transpose(ps[0:64, 0:P], PSB[:, NPAST:NPAST + 64], ident)
                        ins.then_inc(*to("sp_done", (b, g)))
                    ps = bank(pe, ("so", b), ("s_out", b), which=4)
                    for k in range(PAGES):
                        if k % 4 == 0:
                            pe.wait_ge(*at(sp_name(k // 4), (b, k // 4)))
                        mm(pe, ps[:, 0:LAT], PTS[:, k, :], PGS[:, b % 2, k, :], k == 0, False)
                    pe.wait_ge(*at(sp_name(4), (b, 4)))
                    mm(pe, ps[:, 0:LAT], PTS[0:64, 16, :], CTOK[0:64, 2, 0:LAT], False, True).then_inc(*to("s_values", b))
                elif kind == "out":
                    ps = moving_bank(("ol", b), ("ol_turned", b))
                    pe.wait_ge(*at("s_out", b))
                    for ct in range(2):
                        ins = pe.transpose(ps[:, ct * P:ct * P + P], OL[:, ct * P:ct * P + P], ident)
                    ins.then_inc(*to("ol_done", b))
            ps = bank(pe, ("vs", 0), ("vs", 0))
            pe.wait_ge(*at("ol_turned", 7))
            w = W[:, where[("uv",)] % NS, :]
            for h in range(MH):
                rows = slice(64 * (h % 2), 64 * (h % 2) + 64)
                for ct in range(2):
                    ins = mm(pe, ps[rows, (h // 2) * 64:(h // 2) * 64 + 64], w[:, ct * D + h * 64:ct * D + h * 64 + 64],
                             OLS[:, ct, h, :], ct == 0, ct == 1)
            ins.then_inc(*to("vs_done", 0))
            weight_used[("uv",)] = ("vs_done", 0)
            pe_out(pe, mq + 1, [[("wo", l, c)] for c in range(4)], 8, lambda n: [("po", n), ("vs", 0)], lambda n: VT[:, n, :])
            pe_norm(pe, mq + 1)

        def sp_name(g):
            return "sp_turned" if g % 2 == 0 else "sp_turned_d"

        def act_mla(act, l):
            act.dma_start(CM, io["const_mla"]).then_inc(*to("const_mla", 0, 16))
            act_pre_norm(act, mq)
            for m in range(7):
                act.wait_ge(*at("min_done", m))
                src = of(("min", m))[:, 0:NT]
                dst = CQ[:, m, :] if m < 4 else LT[:, m - 4, :] if m < 6 else KR
                if m < 6:
                    act_square(act, m, src, ("mla_sq", m), lambda n: ("mla_summed", n), count=6)
                act.activation(dst, src, ACT.Copy).then_inc(*to("min_raw", m))
                for name, last, count, r in (("q", 3, 512, RS), ("c", 5, 256, PS)):
                    if m == last:
                        act.wait_ge(*at("mla_summed", last))
                        act.activation(r[:, 0, :], of(("ln", name))[:, 0:NT], ACT.Ln, bias=EB[:, 0:1], scale=1.0 / count)\
                           .then_inc(*to("mla_ln", name))
                        act.wait_ge(*at("mla_ln", name))
                        act.activation(r[:, 1, :], r[:, 0, :], ACT.Exp, scale=-0.5).then_inc(*to("mla_rstd", name))
            for c in range(4):
                for j in range(3):
                    act.wait_ge(*at("q_done", (c, j)))
                    dst = QN[:, 2 * c + j, :] if j < 2 else QR[:, c, :]
                    act.activation(dst, of(("q", c, j))[:, 0:NT], ACT.Copy).then_inc(*to("q_raw", (c, j)))
            for g in range(4):
                act.wait_ge(*at("kn_done", g))
                act.activation(KN[:, 2 * g:2 * g + 2, :], of(("kn", g)).rearrange("p (a t) -> p a t", a=2), ACT.Copy)\
                   .then_inc(*to("kn", g))
            for g in range(4):
                act.wait_ge(*at("ukt_done", g))
                act.activation(UKT[:, 2 * g:2 * g + 2, :], of(("ukt", g)).rearrange("p (a t) -> p a t", a=2), ACT.Copy)\
                   .then_inc(*to("ukt", g))
            for t in range(3):
                n = P if t < 2 else 64
                act.wait_ge(*at("ctok_done", t))
                act.activation(CTOK[0:n, t, :], of(("ctok", t))[0:n, 0:288], ACT.Copy).then_inc(*to("ctok", t))
            act.wait_ge(*at("ctok", 2))
            for part, (a, b) in enumerate(((0, LAT), (LAT, LAT + ROPE))):
                name = ("mla_latent", "mla_krope")[part]
                act.dma_start(io["p_" + name][0, 0].rearrange("(c t) f -> t c f", c=2), CTOK[:, 0:2, a:b])\
                   .then_inc(*to("mla_stored", l, 16))
                act.dma_start(io["s_" + name][0].rearrange("b s f -> (b s) f"), CTOK[0:64, 2, a:b])\
                   .then_inc(*to("mla_stored", l, 16))
            for t in range(2):
                for g in range(2):
                    act.wait_ge(*at("v_done", (t, g)))
                    if (t, g) == (0, 0):
                        act.wait_ge(*at("rot", 3))
                    act.activation(VTOK[:, t, g * 512:(g + 1) * 512], of(("v", t, g)), ACT.Copy).then_inc(*to("vtok", (t, g)))
            for g in range(4):
                act.wait_ge(*at("ql_done", g))
                src = of(("ql", g)).rearrange("p (h c b s) -> p h c b s", h=4, c=2, b=DEC)
                for ct in range(2):
                    h0 = 8 * (g // 2) + g % 2
                    dst = QLS[:, ct].rearrange("p b (h s) -> p h b s", h=MH)[:, h0:min(h0 + 8, MH):2]
                    ins = act.activation(dst, src[:, :, ct], ACT.Copy)
                ins.then_inc(*to("ql", g))
            for g in range(2):
                act.wait_ge(*at("qrs_done", g))
                dst = QRS.rearrange("p b (h s) -> p h b s", h=MH)[:, 8 * g:8 * g + 8]
                act.activation(dst, of(("qrs", g)).rearrange("p (h b s) -> p h b s", h=8, b=DEC), ACT.Copy)\
                   .then_inc(*to("qrs", g))
            for i in range(MH + 3):
                if i < MH:
                    h = i
                    act.wait_ge(*at("p_max", h))
                    if h >= 3:
                        act.wait_ge(*at("pt_done", h - 3))
                        act.wait_ge(*at("p_norm", h - 3))
                    for qb, cols in ((0, slice(0, P)), (1, slice(P, 384))):
                        ins = act.activation(PPR[:, h % 3, cols], of(("ps", h))[:, cols], ACT.Exp, bias=MMAX[:, h % 3, 2 + qb:3 + qb],
                                             scale=SCALE, accum_out=MSUM[:, h % 3, qb:qb + 1])
                    ins.then_inc(*to("p_exp", h))
                if 2 <= i < MH + 2:
                    h = i - 2
                    act.wait_ge(*at("pt_done", h))
                    if h >= 2:
                        act.wait_ge(*at("po_done", h - 2))
                    ps = of(("pt", h))[:, 0:384]
                    act.activation(PTP[:, h % 2, :], ps, ACT.Copy).then_inc(*to("pt", h))
                if i >= 3 and i % 2 == 0:
                    a = (i - 3) // 2
                    act.wait_ge(*at("po_done", i - 3))
                    act.activation(VT[:, a, 0:SEQ], of(("po", a))[:, 0:SEQ], ACT.Copy).then_inc(*to("po", a))
            for kind, n in mla_order():
                if kind == "turn":
                    act.wait_ge(*at("turn_done", (n, 0)))
                    if n >= 2:
                        act.wait_ge(*at("score_done", divmod(n - 2, 4)))
                    act.activation(CTB[n % 2][:, 0:512], of(("turn", n, 0)), ACT.Copy).then_inc(*to("c_turned_a", (n, 0)))
                elif kind == "weigh":
                    b = n
                    act.wait_ge(*at("s_max", b))
                    for g in range(5):
                        if b:
                            act.wait_ge(*at("sp_done", (b - 1, g)))
                            act.wait_ge(*at("s_rec", b - 1))
                        w = 512 if g < 4 else 64
                        act.activation(PSB[:, g * 512:g * 512 + w], of(("score", b, g))[:, 0:w], ACT.Exp, bias=SNM[:, 1:2],
                                       scale=SCALE, accum_out=SSM[:, g:g + 1]).then_inc(*to("s_exp", (b, g)))
                elif kind == "values":
                    b = n
                    for g in (0, 2, 4):
                        act.wait_ge(*at("sp_done", (b, g)))
                        if b:
                            act.wait_ge(*at("s_values", b - 1))
                        if g < 4:
                            act.activation(PTS[:, 4 * g:4 * g + 4, :].rearrange("p a t -> p (a t)"), of(("sp", b, g)), ACT.Copy)\
                               .then_inc(*to("sp_turned", (b, g)))
                        else:
                            act.activation(PTS[0:64, 16, :], of(("sp", b, g))[0:64, 0:P], ACT.Copy).then_inc(*to("sp_turned", (b, g)))
                elif kind == "out":
                    b = n
                    act.wait_ge(*at("ol_done", b))
                    dst = OLS.rearrange("p c h (b s) -> p c h b s", b=DEC)[:, :, :, b, :]
                    act.activation(dst, of(("ol", b))[:, 0:LAT].rearrange("p (c h s) -> p c h s", c=2, h=MH), ACT.Copy)\
                       .then_inc(*to("ol_turned", b))
            act.wait_ge(*at("vs_done", 0))
            act.activation(VT[:, :, SEQ:NT], of(("vs", 0)).rearrange("p (a t) -> p a t", a=8), ACT.Copy).then_inc(*to("vs", 0))
            act_outputs(act, mq + 1, ("mla_stored", l))

        def dve_mla(dve, l):
            dve_pre_norm(dve, mq)
            for m in range(6):
                name, r = ("q", RS) if m < 4 else ("c", PS)
                x = CQ[:, m, :] if m < 4 else LT[:, m - 4, :]
                dve.wait_ge(*at("min_raw", m))
                dve.wait_ge(*at("mla_rstd", name))
                dve.scalar_tensor_tensor(out=x, in0=x, scalar=par("mla_q_norm", m) if m < 4 else par("mla_kv_norm", m - 4),
                                         in1=r[:, 1, :], op0=ALU.mult, op1=ALU.mult)\
                   .then_inc(*(to("cq", m) if m < 4 else to("c", m - 4)))
            for n, key in enumerate(("k", 0, 1, 2, 3)):
                x = KR if key == "k" else QR[:, key, :]
                if n == 0:
                    dve.wait_ge(*at("const_mla", 0))
                dve.wait_ge(*at("swapped", key))
                if n >= 2:
                    dve.wait_ge(*at("rot", (None, "k", 0, 1, 2)[n - 1]))
                dve.tensor_tensor(RT[:, n % 2, :], of(("swap", key))[:, 0:NT], mla_const("sin"), ALU.mult).then_inc(*to("rot_s", key))
                dve.tensor_tensor(x, x, mla_const("cos"), ALU.mult).then_inc(*to("rot_c", key))
                dve.wait_ge(*at("rot_c", key))
                dve.tensor_tensor(x, x, RT[:, n % 2, :], ALU.add).then_inc(*to("rot", key))
            causal = mla_const("causal")
            for i in range(MH + 1):
                if i < MH:
                    h = i
                    dve.wait_ge(*at("ps_done", h))
                    ps = of(("ps", h))
                    diag = ps[:, 0:512].rearrange("p (a t) -> p a t", a=4)[:, 0:3:2, :]
                    dve.tensor_tensor(diag, diag, causal.unsqueeze(1).broadcast_to([P, 2, P]), ALU.add).then_inc(*to("p_masked", h))
                    dve.wait_ge(*at("p_masked", h))
                    if h >= 3:
                        dve.wait_ge(*at("p_exp", h - 3))
                    s = h % 3
                    dve.tensor_reduce(MMAX[:, s, 0:1], ps[:, 0:P], AX.X, ALU.max)
                    dve.tensor_reduce(MMAX[:, s, 1:2], ps[:, P:384], AX.X, ALU.max).then_inc(*to("p_maxr", h))
                    dve.wait_ge(*at("p_maxr", h))
                    dve.tensor_scalar(MMAX[:, s, 2:4], MMAX[:, s, 0:2], -SCALE, None, ALU.mult).then_inc(*to("p_max", h))
                if i:
                    h = i - 1
                    s = h % 3
                    dve.wait_ge(*at("p_exp", h))
                    dve.reciprocal(MSUM[:, s, 2:4], MSUM[:, s, 0:2]).then_inc(*to("p_rec", h))
                    dve.wait_ge(*at("p_rec", h))
                    dve.tensor_scalar(PPR[:, s, 0:P], PPR[:, s, 0:P], MSUM[:, s, 2:3], None, ALU.mult)
                    dve.tensor_scalar(PPR[:, s, P:384], PPR[:, s, P:384], MSUM[:, s, 3:4], None, ALU.mult)\
                       .then_inc(*to("p_norm", h))
            causal8 = mla_const("causal8")
            for kind, n in mla_order():
                if kind == "turn":
                    if n >= 2:
                        dve.wait_ge(*at("score_done", divmod(n - 2, 4)))
                    dve.wait_ge(*at("turn_done", (n, 1)))
                    dve.tensor_copy(CTB[n % 2][:, 512:1024], of(("turn", n, 1))).then_inc(*to("c_turned", (n, 1)))
                    dve.wait_ge(*at("turn_done", (n, 2)))
                    dve.tensor_tensor(RTB[n % 2].rearrange("p (j t) -> p j t", j=4),
                                      of(("turn", n, 2))[:, 0:P].unsqueeze(1).broadcast_to([P, 4, P]),
                                      mla_const("group4").unsqueeze(2).broadcast_to([P, 4, P]), ALU.mult)\
                       .then_inc(*to("c_turned", (n, 2)))
                elif kind == "score":
                    b, g = divmod(n, 4)
                    dve.wait_ge(*at("score_done", (b, g)))
                    if b and g == 0:
                        dve.wait_ge(*at("s_maxr", b - 1))
                    dve.tensor_reduce(SMX[:, g:g + 1], of(("score", b, g)), AX.X, ALU.max).then_inc(*to("s_gmax", (b, g)))
                elif kind == "new":
                    b = n
                    ps = of(("score", b, 4))[:, 0:64]
                    dve.wait_ge(*at("score_done", (b, 4)))
                    dve.tensor_tensor(ps, ps, causal8[:, 56 - 8 * b:120 - 8 * b], ALU.add).then_inc(*to("s_masked", b))
                    dve.wait_ge(*at("s_masked", b))
                    dve.tensor_reduce(SMX[:, 4:5], ps, AX.X, ALU.max).then_inc(*to("s_gmax", (b, 4)))
                elif kind == "weigh":
                    b = n
                    dve.wait_ge(*at("s_gmax", (b, 3)))
                    if b:
                        dve.wait_ge(*at("s_exp", (b - 1, 4)))
                    dve.tensor_reduce(SNM[:, 0:1], SMX, AX.X, ALU.max).then_inc(*to("s_maxr", b))
                    dve.wait_ge(*at("s_maxr", b))
                    dve.tensor_scalar(SNM[:, 1:2], SNM[:, 0:1], -SCALE, None, ALU.mult).then_inc(*to("s_max", b))
                elif kind == "values":
                    b = n
                    for g in (1, 3):
                        dve.wait_ge(*at("sp_done", (b, g)))
                        if b:
                            dve.wait_ge(*at("s_values", b - 1))
                        dve.tensor_copy(PTS[:, 4 * g:4 * g + 4, :].rearrange("p a t -> p (a t)"), of(("sp", b, g)))\
                           .then_inc(*to("sp_turned_d", (b, g)))
                    dve.wait_ge(*at("s_exp", (b, 4)))
                    if b:
                        dve.wait_ge(*at("s_out", b - 1))
                    dve.tensor_reduce(SRC[:, 0:1], SSM, AX.X, ALU.add).then_inc(*to("s_sum", b))
                    dve.wait_ge(*at("s_sum", b))
                    dve.reciprocal(SRC[:, 1:2], SRC[:, 0:1]).then_inc(*to("s_rec", b))
                    dve.wait_ge(*at("s_rec", b))
                    dve.wait_ge(*at("s_values", b))
                    if b:
                        dve.wait_ge(*at("ol_done", b - 1))
                    dve.tensor_scalar(OL, of(("so", b))[:, 0:LAT], SRC[:, 1:2], None, ALU.mult).then_inc(*to("s_out", b))
            dve_post_norm(dve, mq + 1)

        def pool_mla(pool, l):
            pool.wait_ge(*at("rstd", mq))
            pool.wait_ge(*at("pages_in", 0))
            for b in range(DEC):
                if b >= 2:
                    pool.wait_ge(*at("turn_done", (4 * (b - 2) + 3, 2)))
                for j in range(PAGES):
                    i = b * PAGES + j
                    page = pool.value_load(PG[0:1, i:i + 1], min_val=0, max_val=POOL - 1)
                    pool.dma_start(PGR[:, b % 2, j * ROPE:(j + 1) * ROPE], io["cache_mla_krope"][0][bass.ds(page, 1), :, :]
                                   .rearrange("a p c -> (a p) c")).then_inc(*to(f"rope{b % 2}", b, 16))

        block_ = ctx.enter_context(nc.Block())
        mixer_of = lambda l: "rwkv" if l in rw_of else "mla" if l == 1 else "gdn"

        @block_.tensor
        def _(pe):
            pe_prologue(pe)
            for l in range(layers):
                (pe_rwkv if l in rw_of else pe_mla if l == 1 else pe_gdn)(pe, l)
                pe_ffn(pe, l)
            pe_final(pe)

        @block_.sync
        def _(sp):
            sp_prologue(sp)
            for i, (key, loads) in enumerate(plan):
                if i >= NS:
                    sp.wait_ge(*at(*weight_used[plan[i - NS][0]]))
                for dst, src in loads:
                    sp.dma_start(dst, src).then_inc(*to(f"slot{i % NS}", key, 16))
                if key[0] == "wo" and key[1] in rw_of and key[2] == 3:
                    sp_rwkv_states(sp, key[1])
                if key == ("gwo", 3):
                    sp_states(sp)
                if key in (("uv",), ("wo", 1, 0)):
                    for b in range(2) if key[0] == "uv" else range(2, DEC):
                        sp_pages(sp, b)

        @block_.scalar
        def _(act):
            act.preload_act_table_set("natural_log_exp_and_others")
            act_loads(act)
            for l in range(layers):
                (act_rwkv if l in rw_of else act_mla if l == 1 else act_gdn)(act, l)
                act_ffn(act, l)
            act_final(act)

        @block_.vector
        def _(dve):
            dve_prologue(dve)
            for l in range(layers):
                (dve_rwkv if l in rw_of else dve_mla if l == 1 else dve_gdn)(dve, l)
                dve_ffn(dve, l)

        @block_.gpsimd
        def _(pool):
            for l in range(layers):
                if mixer_of(l) == "rwkv":
                    pool_rwkv_chunks(pool, l)
                elif mixer_of(l) == "mla":
                    pool_mla(pool, l)
                else:
                    pool_gdn(pool, l)
                pool_squares(pool, 4 * l + 1)
                pool_ffn(pool, l)
                pool_squares(pool, 4 * l + 3)

    return sig.found


INPUTS = ["x_prompt", "x_sample", "state_rwkv_wkv", "state_rwkv_shift", "cache_mla_latent", "cache_mla_krope",
          "state_gdn_S", "state_gdn_conv", "state_ffn_conv", "page_table", "norm_w", "rw_mu", "rw_wrkv", "rw_w0",
          "rw_w1", "rw_w2", "rw_a0", "rw_a1", "rw_a2", "rw_v0", "rw_v1", "rw_v2", "rw_g1", "rw_g2", "rw_kk",
          "rw_ka", "rw_rk", "rw_lnx_w", "rw_lnx_b", "rw_wo", "mla_w_in", "mla_q_norm", "mla_kv_norm", "mla_w_qb",
          "mla_w_uk", "mla_w_uv", "mla_wo", "gdn_w_in", "gdn_conv_w", "gdn_a_log", "gdn_dt_bias", "gdn_norm_w",
          "gdn_wo", "ffn_w_up", "ffn_conv_w", "ffn_conv_b", "ffn_w_down"]
OUTPUTS = [("y_prompt", (1, SEQ, D)), ("y_sample", (DEC, STEPS, D)),
           ("p_rwkv_wkv", (2, 1, 16, 64, 64)), ("p_rwkv_shift", (2, 1, D)), ("p_mla_latent", (1, 1, SEQ, LAT)),
           ("p_mla_krope", (1, 1, SEQ, ROPE)), ("p_gdn_S", (1, 1, GH, P, P)), ("p_gdn_conv", (1, 1, 3, 4096)),
           ("p_ffn_conv", (DEPTH, 1, 2, 2 * DFF)),
           ("s_rwkv_wkv", (2, DEC, 16, 64, 64)), ("s_rwkv_shift", (2, DEC, D)), ("s_mla_latent", (1, DEC, STEPS, LAT)),
           ("s_mla_krope", (1, DEC, STEPS, ROPE)), ("s_gdn_S", (1, DEC, GH, P, P)), ("s_gdn_conv", (1, DEC, 3, 4096)),
           ("s_ffn_conv", (DEPTH, DEC, 2, 2 * DFF))]
LAYERS = DEPTH


def declare(nc, arrays):
    io = {name: nc.dram_tensor(name, a.shape, mybir.dt.from_np(a.dtype), kind="ExternalInput").ap()
          for name, a in arrays.items()}
    for name, shape in OUTPUTS:
        io[name] = nc.dram_tensor("out_" + name, shape, F32, kind="ExternalOutput").ap()
    io["ffn_state_t"] = nc.dram_tensor("ffn_state_t", (P, DEPTH * 704), F32, kind="Internal").ap()
    io["v_first"] = nc.dram_tensor("v_first", (P, BLK), F32, kind="Internal").ap()
    return io


def kernel(**inputs):
    import concourse.bacc as bacc
    from concourse.bass_utils import run_bass_kernel_spmd

    arrays = {name: np.ascontiguousarray(inputs[name]) for name in INPUTS}
    arrays["const"] = CONST
    arrays["const_mla"] = MLA_CONST
    counted = bacc.Bacc("TRN2", target_bir_lowering=False, num_devices=1)
    values = build(counted, declare(counted, arrays), None, LAYERS)
    nc = bacc.Bacc("TRN2", target_bir_lowering=False, num_devices=1)
    build(nc, declare(nc, arrays), values, LAYERS)
    result = run_bass_kernel_spmd(nc, [arrays], core_ids=[0]).results[0]
    return tuple(result["out_" + name] for name, _ in OUTPUTS)
```
